# Optimizing a Trainium2 kernel written in Bass

```python
import math
import jax, jax.numpy as jnp
from jax import lax
import numpy as np

D_MODEL = 2048
BATCH = 1
SEQ = 512
DEPTH = 2
DEC_BATCH = 8
DEC_SEQ = 4
PAST_LEN = 4096
PAGE_SIZE = 128

PLE_DIM = 256
CONV_W = 4
EPS = 1e-6
N_EVEN = (DEPTH + 1) // 2
N_ODD = DEPTH // 2
DN_HEADS = 8
DN_DK = 128
DN_DV = 128
DN_W = DN_HEADS * DN_DV
DN_QKV = 2 * DN_HEADS * DN_DK + DN_W
DN_CHUNK = 64
GLA_HEADS = 4
GLA_DK = 128
GLA_DV = 256
GLA_KW = GLA_HEADS * GLA_DK
GLA_W = GLA_HEADS * GLA_DV
GLA_RANK = 16
GLA_GATE_NORM = 16.0
GLA_CHUNK = 16
AB_SIZES = (DN_QKV, DN_HEADS, DN_HEADS, DN_W, GLA_KW, GLA_KW, GLA_W, GLA_RANK, GLA_W)
AB_IN = sum(AB_SIZES)
AB_OUT = DN_W + GLA_W
SSD_HEADS = 16
SSD_HEADDIM = 64
SSD_W = SSD_HEADS * SSD_HEADDIM
SSD_GROUPS = 4
SSD_STATE = 64
SSD_XBC = SSD_W + 2 * SSD_GROUPS * SSD_STATE
SSD_CHUNK = 64
LRU_W = 1024
LRU_BLOCKS = 16
LRU_BS = LRU_W // LRU_BLOCKS
LRU_C = 8.0
CD_SIZES = (SSD_W, SSD_XBC, SSD_HEADS, LRU_W, LRU_W)
CD_IN = sum(CD_SIZES)
CD_OUT = SSD_W + LRU_W

kernel_name = 'hybrid_deltanet_gla_ssd_rglru_step'

def _rmsnorm(x, g):
    xf = x.astype(jnp.float32)
    y = xf * lax.rsqrt(jnp.mean(xf * xf, axis=-1, keepdims=True) + EPS)
    return (y * g.astype(jnp.float32)).astype(x.dtype)

def _l2norm(x):
    xf = x.astype(jnp.float32)
    return (xf * lax.rsqrt(jnp.sum(xf * xf, axis=-1, keepdims=True) + EPS)).astype(x.dtype)

def _split(u, sizes):
    idx = np.cumsum(sizes)[:-1].tolist()
    return jnp.split(u, idx, axis=-1)

def _causal_conv(x, buf, w, b=None):
    L = x.shape[1]
    xx = jnp.concatenate([buf.astype(x.dtype), x], axis=1)
    out = xx[:, 0:L] * w[0]
    for tap in range(1, w.shape[0]):
        out = out + xx[:, tap:tap + L] * w[tap]
    if b is not None:
        out = out + b
    return out, xx[:, L:]

def _chunk_len(L, c):
    return c if L % c == 0 else L

def _to_chunks(t, C):
    B_, L = t.shape[:2]
    return jnp.moveaxis(t.reshape(B_, L // C, C, *t.shape[2:]), 2, 3)

def _from_chunks(o):
    B_, N, H, C = o.shape[:4]
    return jnp.moveaxis(o, 2, 3).reshape(B_, N * C, H, *o.shape[4:])

def _inter_chunk(s0, qg, kend, gend, A, v):
    def step(S, inp):
        qg_n, kend_n, gend_n, A_n, v_n = inp
        o = jnp.einsum('bhid,bhde->bhie', qg_n, S) + jnp.einsum('bhij,bhje->bhie', A_n, v_n)
        S = gend_n * S + jnp.einsum('bhid,bhie->bhde', kend_n, v_n)
        return S, o
    xs = tuple(jnp.moveaxis(t, 1, 0) for t in (qg, kend, gend, A, v))
    S, o = lax.scan(step, s0.astype(v.dtype), xs)
    return _from_chunks(jnp.moveaxis(o, 0, 1)), S

def _gated_delta(q, k, v, beta, g, s0):
    f32 = jnp.float32
    dt_ = v.dtype
    DV = v.shape[-1]
    C = _chunk_len(q.shape[1], DN_CHUNK)
    q, k, v, beta, g = (_to_chunks(t, C) for t in (q, k, v, beta, g))
    G = jnp.cumsum(g.astype(f32), axis=-1)
    causal = jnp.tril(jnp.ones((C, C), dtype=bool))
    strict = causal & ~jnp.eye(C, dtype=bool)
    decay = jnp.exp(jnp.where(causal, G[..., :, None] - G[..., None, :], -jnp.inf))
    bf = beta.astype(f32)
    kk = jnp.einsum('bnhid,bnhjd->bnhij', k, k).astype(f32)
    A = jnp.where(strict, bf[..., :, None] * kk * decay, 0.0)
    M = A + jnp.eye(C, dtype=f32)
    rhs = jnp.concatenate([bf[..., None] * v.astype(f32),
                           (bf * jnp.exp(G))[..., None] * k.astype(f32)], axis=-1)
    sol = lax.linalg.triangular_solve(M, rhs, left_side=True, lower=True)
    u0 = sol[..., :DV].astype(dt_)
    wk = sol[..., DV:].astype(dt_)
    qk = (jnp.einsum('bnhid,bnhjd->bnhij', q, k).astype(f32) * decay).astype(dt_)
    qg = q * jnp.exp(G)[..., None].astype(dt_)
    kend = k * jnp.exp(G[..., -1:] - G)[..., None].astype(dt_)
    gend = jnp.exp(G[..., -1]).astype(dt_)[..., None, None]

    def step(S, inp):
        u0_n, wk_n, qk_n, qg_n, kend_n, gend_n = inp
        u = u0_n - jnp.einsum('bhid,bhde->bhie', wk_n, S)
        o = jnp.einsum('bhid,bhde->bhie', qg_n, S) + jnp.einsum('bhij,bhje->bhie', qk_n, u)
        S = gend_n * S + jnp.einsum('bhid,bhie->bhde', kend_n, u)
        return S, o
    xs = tuple(jnp.moveaxis(t, 1, 0) for t in (u0, wk, qk, qg, kend, gend))
    S, o = lax.scan(step, s0.astype(dt_), xs)
    return _from_chunks(jnp.moveaxis(o, 0, 1)), S

def _gla(q, k, v, glog, s0):
    f32 = jnp.float32
    dt_ = v.dtype
    C = _chunk_len(q.shape[1], GLA_CHUNK)
    q, k, v, glog = (_to_chunks(t, C) for t in (q, k, v, glog))
    G = jnp.cumsum(glog.astype(f32), axis=3)
    causal = jnp.tril(jnp.ones((C, C), dtype=bool))
    decay = jnp.exp(jnp.where(causal[:, :, None], G[..., :, None, :] - G[..., None, :, :], -jnp.inf))
    A = jnp.einsum('bnhid,bnhjd,bnhijd->bnhij', q.astype(f32), k.astype(f32), decay).astype(dt_)
    qg = q * jnp.exp(G).astype(dt_)
    kend = k * jnp.exp(G[..., -1:, :] - G).astype(dt_)
    gend = jnp.exp(G[..., -1, :]).astype(dt_)[..., :, None]
    return _inter_chunk(s0, qg, kend, gend, A, v)

def _scalar_decay(q, k, v, g, s0):
    f32 = jnp.float32
    dt_ = v.dtype
    C = _chunk_len(q.shape[1], SSD_CHUNK)
    q, k, v, g = (_to_chunks(t, C) for t in (q, k, v, g))
    G = jnp.cumsum(g.astype(f32), axis=-1)
    causal = jnp.tril(jnp.ones((C, C), dtype=bool))
    decay = jnp.exp(jnp.where(causal, G[..., :, None] - G[..., None, :], -jnp.inf))
    A = (jnp.einsum('bnhid,bnhjd->bnhij', q, k).astype(f32) * decay).astype(dt_)
    qg = q * jnp.exp(G)[..., None].astype(dt_)
    kend = k * jnp.exp(G[..., -1:] - G)[..., None].astype(dt_)
    gend = jnp.exp(G[..., -1]).astype(dt_)[..., None, None]
    return _inter_chunk(s0, qg, kend, gend, A, v)

def _lin_combine(l, r):
    return (l[0] * r[0], r[0] * l[1] + r[1])

def _mixer_ab(xn, st_dn, st_conv, st_gla, w, j):
    B_, L, _ = xn.shape
    u = xn @ w['ab_w_in'][j]
    qkv, beta_in, a_in, z_dn, gq, gk, gv, g_lr, z_gla = _split(u, AB_SIZES)
    qkv, conv_new = _causal_conv(qkv, st_conv, w['dn_conv_w'][j])
    qkv = jax.nn.silu(qkv)
    q, k, v = _split(qkv, (DN_HEADS * DN_DK, DN_HEADS * DN_DK, DN_W))
    q = _l2norm(q.reshape(B_, L, DN_HEADS, DN_DK)) * (DN_DK ** -0.5)
    k = _l2norm(k.reshape(B_, L, DN_HEADS, DN_DK))
    v = v.reshape(B_, L, DN_HEADS, DN_DV)
    beta = jax.nn.sigmoid(beta_in)
    g = -jnp.exp(w['dn_a_log'][j]) * jax.nn.softplus(a_in + w['dn_dt_bias'][j])
    o_dn, dn_new = _gated_delta(q, k, v, beta, g, st_dn)
    o_dn = _rmsnorm(o_dn, w['dn_norm'][j]).reshape(B_, L, DN_W) * jax.nn.silu(z_dn)
    gq = gq.reshape(B_, L, GLA_HEADS, GLA_DK) * (GLA_DK ** -0.5)
    gk = gk.reshape(B_, L, GLA_HEADS, GLA_DK)
    gv = gv.reshape(B_, L, GLA_HEADS, GLA_DV)
    glog = jax.nn.log_sigmoid(g_lr @ w['gla_wa2'][j] + w['gla_ba'][j]) / GLA_GATE_NORM
    glog = glog.reshape(B_, L, GLA_HEADS, GLA_DK)
    o_gla, gla_new = _gla(gq, gk, gv, glog, st_gla)
    o_gla = _rmsnorm(o_gla, w['gla_norm'][j]).reshape(B_, L, GLA_W) * jax.nn.silu(z_gla)
    y = jnp.concatenate([o_dn, o_gla], axis=-1) @ w['ab_w_out'][j]
    return y, dn_new, conv_new, gla_new

def _mixer_cd(xn, st_ssd, st_sconv, st_lru, st_lconv, w, j):
    B_, L, _ = xn.shape
    u = xn @ w['cd_w_in'][j]
    z, xbc, dt_in, z_lru, x_lru = _split(u, CD_SIZES)
    xbc, sconv_new = _causal_conv(xbc, st_sconv, w['ssd_conv_w'][j], w['ssd_conv_b'][j])
    xbc = jax.nn.silu(xbc)
    xs, bm, cm = _split(xbc, (SSD_W, SSD_GROUPS * SSD_STATE, SSD_GROUPS * SSD_STATE))
    xs = xs.reshape(B_, L, SSD_HEADS, SSD_HEADDIM)
    rep = SSD_HEADS // SSD_GROUPS
    bm = jnp.repeat(bm.reshape(B_, L, SSD_GROUPS, SSD_STATE), rep, axis=2)
    cm = jnp.repeat(cm.reshape(B_, L, SSD_GROUPS, SSD_STATE), rep, axis=2)
    dt = jax.nn.softplus(dt_in + w['ssd_dt_bias'][j])
    g = -jnp.exp(w['ssd_a_log'][j]) * dt
    y, ssd_new = _scalar_decay(cm, bm, xs * dt[..., None], g, st_ssd)
    y = y + w['ssd_d'][j][:, None] * xs
    y = (y.reshape(B_, L, SSD_W) * jax.nn.silu(z)).reshape(B_, L, SSD_GROUPS, SSD_W // SSD_GROUPS)
    y_ssd = _rmsnorm(y, w['ssd_norm'][j].reshape(SSD_GROUPS, -1)).reshape(B_, L, SSD_W)
    xc, lconv_new = _causal_conv(x_lru, st_lconv, w['lru_conv_w'][j], w['lru_conv_b'][j])
    xb = xc.reshape(B_, L, LRU_BLOCKS, LRU_BS)
    r = jax.nn.sigmoid(jnp.einsum('blnc,ncd->blnd', xb, w['lru_wa'][j]).reshape(B_, L, LRU_W) + w['lru_ba'][j])
    i = jax.nn.sigmoid(jnp.einsum('blnc,ncd->blnd', xb, w['lru_wx'][j]).reshape(B_, L, LRU_W) + w['lru_bx'][j])
    log_a = -LRU_C * r * jax.nn.softplus(-w['lru_lambda'][j])
    a = jnp.exp(log_a)
    b = jnp.sqrt(-jnp.expm1(2.0 * log_a)) * (i * xc)
    b = b.at[:, 0].add(a[:, 0] * st_lru.astype(b.dtype))
    _, hs = lax.associative_scan(_lin_combine, (a, b), axis=1)
    y_lru = hs * jax.nn.silu(z_lru)
    y = jnp.concatenate([y_ssd, y_lru], axis=-1) @ w['cd_w_out'][j]
    return y, ssd_new, sconv_new, hs[:, -1], lconv_new

def _trunk(x, p, states, w):
    st_dn, st_dnc, st_gla, st_ssd, st_ssdc, st_lru, st_lruc = states
    outs = [[] for _ in range(7)]
    h = x
    for li in range(DEPTH):
        xn = _rmsnorm(h, w['norm_g'][li])
        j = li // 2
        if li % 2 == 0:
            y, *new = _mixer_ab(xn, st_dn[j], st_dnc[j], st_gla[j], w, j)
            slots = (0, 1, 2)
        else:
            y, *new = _mixer_cd(xn, st_ssd[j], st_ssdc[j], st_lru[j], st_lruc[j], w, j)
            slots = (3, 4, 5, 6)
        for s, n in zip(slots, new):
            outs[s].append(n)
        h = h + y
        gate = jax.nn.sigmoid(_rmsnorm(h, w['ple_norm'][li]) @ w['ple_w_gate'][li])
        h = h + gate * (p[li] @ w['ple_w_proj'][li])
    return _rmsnorm(h, w['final_norm']), [jnp.stack(o) for o in outs]

def setup_inputs(seed: int = 0) -> dict:
    key = jax.random.key(seed)
    ks = iter(jax.random.split(key, 64))

    def nrm(shape, scale):
        return scale * jax.random.normal(next(ks), shape, jnp.float32)

    def unif(shape, lo, hi):
        return jax.random.uniform(next(ks), shape, jnp.float32, lo, hi)

    def dt_bias(shape):
        dt = jnp.exp(unif(shape, math.log(1e-3), math.log(1e-1)))
        return dt + jnp.log(-jnp.expm1(-dt))

    s_lam = unif((N_ODD, LRU_W), 0.9, 0.999) ** (1.0 / LRU_C)
    return {
        'x_prompt': nrm((BATCH, SEQ, D_MODEL), 1.0),
        'x_sample': nrm((DEC_BATCH, DEC_SEQ, D_MODEL), 1.0),
        'state_dn': nrm((N_EVEN, DEC_BATCH, DN_HEADS, DN_DK, DN_DV), 0.1),
        'state_dn_conv': nrm((N_EVEN, DEC_BATCH, CONV_W - 1, DN_QKV), 1.0),
        'state_gla': nrm((N_EVEN, DEC_BATCH, GLA_HEADS, GLA_DK, GLA_DV), 0.3),
        'state_ssd': nrm((N_ODD, DEC_BATCH, SSD_HEADS, SSD_STATE, SSD_HEADDIM), 0.3),
        'state_ssd_conv': nrm((N_ODD, DEC_BATCH, CONV_W - 1, SSD_XBC), 1.0),
        'state_lru': nrm((N_ODD, DEC_BATCH, LRU_W), 0.5),
        'state_lru_conv': nrm((N_ODD, DEC_BATCH, CONV_W - 1, LRU_W), 1.0),
        'p_prompt': nrm((DEPTH, BATCH, SEQ, PLE_DIM), 1.0),
        'p_sample': nrm((DEPTH, DEC_BATCH, DEC_SEQ, PLE_DIM), 1.0),
        'norm_g': 1.0 + nrm((DEPTH, D_MODEL), 0.05),
        'final_norm': 1.0 + nrm((D_MODEL,), 0.05),
        'ab_w_in': nrm((N_EVEN, D_MODEL, AB_IN), D_MODEL ** -0.5),
        'dn_conv_w': nrm((N_EVEN, CONV_W, DN_QKV), 0.5),
        'dn_a_log': jnp.log(unif((N_EVEN, DN_HEADS), 1.0, 16.0)),
        'dn_dt_bias': dt_bias((N_EVEN, DN_HEADS)),
        'dn_norm': 1.0 + nrm((N_EVEN, DN_DV), 0.05),
        'gla_wa2': nrm((N_EVEN, GLA_RANK, GLA_KW), GLA_RANK ** -0.5),
        'gla_ba': nrm((N_EVEN, GLA_KW), 0.01),
        'gla_norm': 1.0 + nrm((N_EVEN, GLA_DV), 0.05),
        'ab_w_out': nrm((N_EVEN, AB_OUT, D_MODEL), AB_OUT ** -0.5),
        'cd_w_in': nrm((N_ODD, D_MODEL, CD_IN), D_MODEL ** -0.5),
        'ssd_conv_w': nrm((N_ODD, CONV_W, SSD_XBC), 0.5),
        'ssd_conv_b': nrm((N_ODD, SSD_XBC), 0.01),
        'ssd_a_log': jnp.log(unif((N_ODD, SSD_HEADS), 1.0, 16.0)),
        'ssd_dt_bias': dt_bias((N_ODD, SSD_HEADS)),
        'ssd_d': 1.0 + nrm((N_ODD, SSD_HEADS), 0.05),
        'ssd_norm': 1.0 + nrm((N_ODD, SSD_W), 0.05),
        'lru_conv_w': nrm((N_ODD, CONV_W, LRU_W), 0.5),
        'lru_conv_b': nrm((N_ODD, LRU_W), 0.01),
        'lru_wa': nrm((N_ODD, LRU_BLOCKS, LRU_BS, LRU_BS), LRU_BS ** -0.5),
        'lru_ba': nrm((N_ODD, LRU_W), 0.01),
        'lru_wx': nrm((N_ODD, LRU_BLOCKS, LRU_BS, LRU_BS), LRU_BS ** -0.5),
        'lru_bx': nrm((N_ODD, LRU_W), 0.01),
        'lru_lambda': jnp.log(s_lam) - jnp.log1p(-s_lam),
        'cd_w_out': nrm((N_ODD, CD_OUT, D_MODEL), CD_OUT ** -0.5),
        'ple_w_proj': nrm((DEPTH, PLE_DIM, D_MODEL), 0.5 * PLE_DIM ** -0.5),
        'ple_norm': 1.0 + nrm((DEPTH, D_MODEL), 0.05),
        'ple_w_gate': nrm((DEPTH, D_MODEL, D_MODEL), D_MODEL ** -0.5),
    }

def reference(x_prompt, x_sample, state_dn, state_dn_conv, state_gla, state_ssd, state_ssd_conv,
              state_lru, state_lru_conv, p_prompt, p_sample, norm_g, final_norm, ab_w_in, dn_conv_w,
              dn_a_log, dn_dt_bias, dn_norm, gla_wa2, gla_ba, gla_norm, ab_w_out, cd_w_in, ssd_conv_w,
              ssd_conv_b, ssd_a_log, ssd_dt_bias, ssd_d, ssd_norm, lru_conv_w, lru_conv_b, lru_wa, lru_ba,
              lru_wx, lru_bx, lru_lambda, cd_w_out, ple_w_proj, ple_norm, ple_w_gate):
    w = {
        'norm_g': norm_g, 'final_norm': final_norm,
        'ab_w_in': ab_w_in, 'dn_conv_w': dn_conv_w, 'dn_a_log': dn_a_log, 'dn_dt_bias': dn_dt_bias,
        'dn_norm': dn_norm, 'gla_wa2': gla_wa2, 'gla_ba': gla_ba, 'gla_norm': gla_norm, 'ab_w_out': ab_w_out,
        'cd_w_in': cd_w_in, 'ssd_conv_w': ssd_conv_w, 'ssd_conv_b': ssd_conv_b, 'ssd_a_log': ssd_a_log,
        'ssd_dt_bias': ssd_dt_bias, 'ssd_d': ssd_d, 'ssd_norm': ssd_norm,
        'lru_conv_w': lru_conv_w, 'lru_conv_b': lru_conv_b, 'lru_wa': lru_wa, 'lru_ba': lru_ba,
        'lru_wx': lru_wx, 'lru_bx': lru_bx, 'lru_lambda': lru_lambda, 'cd_w_out': cd_w_out,
        'ple_w_proj': ple_w_proj, 'ple_norm': ple_norm, 'ple_w_gate': ple_w_gate,
    }
    B_ = x_prompt.shape[0]
    dt_ = x_prompt.dtype
    zero_states = (
        jnp.zeros((N_EVEN, B_, DN_HEADS, DN_DK, DN_DV), dt_),
        jnp.zeros((N_EVEN, B_, CONV_W - 1, DN_QKV), dt_),
        jnp.zeros((N_EVEN, B_, GLA_HEADS, GLA_DK, GLA_DV), dt_),
        jnp.zeros((N_ODD, B_, SSD_HEADS, SSD_STATE, SSD_HEADDIM), dt_),
        jnp.zeros((N_ODD, B_, CONV_W - 1, SSD_XBC), dt_),
        jnp.zeros((N_ODD, B_, LRU_W), dt_),
        jnp.zeros((N_ODD, B_, CONV_W - 1, LRU_W), dt_),
    )
    y_prompt, (dn_p, dnc_p, gla_p, ssd_p, ssdc_p, lru_p, lruc_p) = _trunk(x_prompt, p_prompt, zero_states, w)
    sample_states = (state_dn, state_dn_conv, state_gla, state_ssd, state_ssd_conv, state_lru, state_lru_conv)
    y_sample, (dn_s, dnc_s, gla_s, ssd_s, ssdc_s, lru_s, lruc_s) = _trunk(x_sample, p_sample, sample_states, w)
    return (y_prompt, y_sample, dn_p, dnc_p, gla_p, ssd_p, ssdc_p, lru_p, lruc_p,
            dn_s, dnc_s, gla_s, ssd_s, ssdc_s, lru_s, lruc_s)


_drawn_inputs = setup_inputs


def setup_inputs(seed=0):
    import zlib

    import numpy as np

    out = dict(_drawn_inputs(seed))
    spreads = {}
    factors = {'gla_ba': 8.0,
     'ssd_conv_b': 3.291,
     'ssd_d': 13.804,
     'lru_ba': 24.338,
     'lru_bx': 8.0,
     'ple_norm': 5.944}
    for name, (base, spread) in spreads.items():
        noise = np.random.default_rng([zlib.crc32(name.encode()), seed]).standard_normal(out[name].shape)
        drawn = base * np.exp(spread * noise) if base else spread * noise
        out[name] = __import__('jax').numpy.asarray(drawn.astype(out[name].dtype))
    for name, factor in factors.items():
        out[name] = (out[name] * factor).astype(out[name].dtype)
    return out
```

```python
from contextlib import ExitStack

import concourse.bass as bass
from concourse import mybir

F32, F32R, BF16, U16 = mybir.dt.float32, mybir.dt.float32r, mybir.dt.bfloat16, mybir.dt.uint16
ALU = mybir.AluOpType
ACT = mybir.ActivationFunctionType

P = 128
D_MODEL, SEQ, NB, LS = 2048, 512, 8, 4
NS = NB * LS
T = SEQ + NS
NT = SEQ // P
KT = D_MODEL // P
PLE = 256
EPS = 1e-6
DN_H, DN_QKV, DN_W = 8, 3072, 1024
GLA_H, GLA_KW, GLA_W, GLA_R = 4, 512, 1024, 16
SSD_H, SSD_W, SSD_G, SSD_N = 16, 1024, 4, 64
SSD_XBC = SSD_W + 2 * SSD_G * SSD_N
LRU_W = 1024
TAPS = 4
HALF = T // 2
D0 = SEQ - HALF

AB_BETA, AB_A, AB_Z = DN_QKV, DN_QKV + DN_H, DN_QKV + 2 * DN_H
AB_GQ = AB_Z + DN_W
AB_GK = AB_GQ + GLA_KW
AB_GV = AB_GK + GLA_KW
AB_LR = AB_GV + GLA_W
AB_GZ = AB_LR + GLA_R
CD_XBC = SSD_W
CD_DT = CD_XBC + SSD_XBC
CD_ZL = CD_DT + SSD_H
CD_XL = CD_ZL + LRU_W


def column_tiles():
    tiles = [("ab", 0, (AB_BETA, AB_A, AB_LR, AB_LR), "ab")]
    for h in range(DN_H):
        tiles += [("ab", 0, (c + P * h,), "ab") for c in (0, DN_W, 2 * DN_W, AB_Z)]
    for h in range(GLA_H):
        tiles += [("ab", 0, (c,), "ab") for c in (AB_GQ + P * h, AB_GK + P * h, AB_GV + 2 * P * h,
                                                   AB_GV + 2 * P * h + P, AB_GZ + 2 * P * h, AB_GZ + 2 * P * h + P)]
    tiles += [("abo", 0, (P * c,), "out0") for c in range(KT)]
    tiles += [("gate", 0, (P * c,), "gate0") for c in range(KT)]
    tiles += [("cd", 0, (CD_DT,), "cd")]
    tiles += [("cd", 0, (CD_XBC + SSD_W + P * c,), "cd") for c in range(4)]
    for p in range(SSD_H // 2):
        tiles += [("cd", 0, (c + P * p,), "cd") for c in (CD_XBC, 0)]
    for j in range(LRU_W // P):
        tiles += [("cd", 0, (c + P * j,), "cd") for c in (CD_XL, CD_ZL)]
    tiles += [("cdo", 0, (P * c,), "out1") for c in range(KT)]
    tiles += [("gate", 1, (P * c,), "gate1") for c in range(KT)]
    return tiles


def dn_groups():
    g = [("ssq", "dn_ln", 1), ("ssk", "dn_ln", 2), ("gbc", "dn_eg", 1), ("bbc", "dn_kb", 1), ("dm", "dn_D", 1),
         ("kk", "dn_at", 1), ("qk", "dn_qkt", 1), ("t1", "dn_t1", 1), ("kt", "dn_kend", 1), ("vt", "dn_bv", 1)]
    for l in range(1, 7):
        g.append((f"x{l}", "dn_x", l))
        if l < 6:
            g.append((f"y{l}", "dn_t", l))
        g.append((f"yt{l}", "dn_tt", l))
    return g + [("wk", "dn_nwk", 1), ("u0", "dn_u", 1), ("us", "dn_u", 2), ("s0", "dn_s", 1), ("ss", "dn_snew", 1),
                ("u1", "dn_u", 3), ("s1", "dn_s", 2), ("u2", "dn_u", 4), ("s2", "dn_s", 3), ("u3", "dn_u", 5),
                ("s3", "dn_s", 4), ("o", "dn_o1", 1), ("n", "dn_ln", 3)]


def gla_groups():
    return [("lg", "gl_m", 1), ("qk", "gl_at", 1)] + [(f"l{l}", "gl_at", l + 2) for l in range(7)] + \
           [("kt", "gl_kend", 1), ("v0", "gl_v", 1), ("v1", "gl_v", 2), ("sA", "gl_s", 1), ("o0", "gl_o1", 1),
            ("o1", "gl_o1", 2), ("sb0", "gl_snew", 1), ("sb1", "gl_snew", 2), ("n", "gl_ln", 1)]


def ssd_groups(p):
    return [("dmA", "sp_D", 1), ("dmB", "sp_D", 2), ("ebc", "sp_ebc", 1), ("xt", "sp_v", 1), ("sP", "sp_s", 1),
            ("ss", "sp_snew", 1), ("i", "sp_i", 1), ("o", "sp_o", 1)] + ([("n", "sp_ln", 1)] if p % 2 else [])


FILL = {("dn", "ssq"): 3.0}
LEAD = 18

PER_UNIT = {"dn_ln": 3, "dn_x": 6, "dn_t": 5, "dn_tt": 6, "dn_u": 5, "dn_s": 4, "gl_at": 8, "gl_v": 2, "gl_o1": 2,
            "gl_snew": 2, "gl_um": 2, "gl_ed": 7, "gl_E": 7, "gl_qkt": 7, "gl_osq": 2, "sp_D": 2, "bc_b": 2,
            "bc_cb": 4, "tail_copied": 1, "nrm_ln": 1}

UNITS = [("ab_rows", 0)] + [("dn", h) for h in range(DN_H)] + [("gla", h) for h in range(GLA_H)] + [("ab_tail", 0)]
UNITS_CD = [("cd_rows", 0), ("bc", 0)] + [("ssd", p) for p in range(SSD_H // 2)] + \
           [("lru", j) for j in range(LRU_W // P)] + [("cd_tail", 0)]


def group_table():
    order, count = [], {}

    def add(unit, name, reader, value):
        order.append((unit, name, reader, value))

    def once(unit, name, reader):
        count[reader] = count.get(reader, 0) + 1
        add(unit, name, reader, count[reader])

    once(("setup", 0), "pv", "in_copied")
    once(("setup", 0), "h0", "in_copied")
    once(("setup", 0), "h1", "in_copied")
    for t in range(NT + 1):
        for i in range(2):
            once(("setup", 0), f"x{t}{i}", "in_copied")
    once(("norm", 0), "n", "nrm_ln")
    for unit in UNITS:
        kind, h = unit
        if kind == "ab_rows":
            once(unit, "c0", "rows_copied")
        if kind == "dn":
            for n, r, i in dn_groups():
                add(unit, n, r, PER_UNIT.get(r, 1) * h + i)
        if kind == "gla":
            for n, r, i in gla_groups():
                add(unit, n, r, PER_UNIT.get(r, 1) * h + i)
        if kind == "ab_tail":
            for i in range(3):
                once(unit, f"t{i}", "tail_copied")
    for layer in range(2):
        if layer:
            for unit in UNITS_CD:
                kind, h = unit
                if kind == "cd_rows":
                    once(unit, "eg", "rows_copied")
                    once(unit, "c0", "rows_copied")
                if kind == "bc":
                    add(unit, "bt", "bc_b", 1)
                    add(unit, "bts", "bc_b", 2)
                    for g in range(4):
                        add(unit, f"cb{g}", "bc_cb", g + 1)
                if kind == "ssd":
                    for n, r, i in ssd_groups(h):
                        add(unit, n, r, h // 2 + 1 if r == "sp_ln" else PER_UNIT.get(r, 1) * h + i)
                if kind == "lru":
                    add(unit, "r", "lr_r", h + 1)
                    add(unit, "i", "lr_i", h + 1)
                if kind == "cd_tail":
                    for i in range(3):
                        once(unit, f"t{i}", "tail_copied")
        once(("norm", 1 + 2 * layer), "n", "nrm_ln")
        for i in range(2):
            once(("gate", layer), f"p{i}", "in_copied")
        for c in range(KT):
            once(("gate", layer), f"g{c}", "gate_read")
        once(("norm", 2 + 2 * layer), "n", "nrm_ln")
    for t in range(NT + 1):
        for i in range(2):
            once(("final", 0), f"y{t}{i}", "out_copied")
    return order


SEMS = """w_landed0 w_landed1 w_landed2 hi_ready lo_ready slice_done dense_read0 dense_read1 stage_stored0 stage_stored1
act_chain dve_chain pool_chain act_evac work_ready in_copied nrm_sq nrm_ln nrm_rstd nrm_tmp nrm_hi x_ready0 x_ready1 z_loaded dn_z sp_z sq_added sq_summed
consts_loaded params_loaded rows_loaded x_loaded0 x_loaded1 h_stored y_loaded h_loaded
rows_copied rows_act rows_dve rows_ready pool_rows eg_rows u_loaded s_loaded out_stored
dn_smp dn_conv dn_silu dn_sq dn_ln dn_rs dn_eg dn_kb dn_D dn_at dn_tt1 dn_qkt dn_t1 dn_kend dn_bv dn_x dn_t dn_tt
dn_nwk dn_mwk dn_u dn_um dn_s dn_gs dn_snew dn_osq dn_o1 dn_rstd dn_y
gl_q gl_abs gl_m gl_l gl_G gl_eg gl_kd gl_kf gl_qg gl_ed gl_E gl_qkt gl_at gl_kend gl_v gl_s gl_um gl_gs gl_snew gl_osq
gl_o1 gl_ln gl_rstd gl_y
bc_smp bc_conv bc_silu bc_b bc_cb
sp_smp sp_conv sp_silu sp_D sp_ebc sp_A sp_v sp_um sp_s sp_gs sp_snew sp_i sp_o sp_y sp_sq sp_ln sp_rstd sp_out
lr_smp lr_conv lr_r lr_i lr_a lr_z lr_t lr_sq lr_hs lr_y lr_w
tail_copied tail_made nrm_y sp_sel ssd_stored y_stored0 y_stored1 p_loaded wp_loaded0 wp_loaded1 gate_sig gate_read gate_done out_copied zeroed consts_set masks_loaded""".split()


PARAM_ROWS = {
    "norm_g": (0, 0, 32), "final_norm": (0, 32, 16), "ple_norm": (0, 48, 32), "ssd_norm": (0, 80, 8),
    "dn_conv_w": (1, 0, 96), "gla_ba": (1, 96, 4), "dn_norm": (1, 100, 1), "gla_norm": (1, 101, 2),
    "ssd_conv_w": (2, 0, 48), "ssd_conv_b": (2, 48, 12), "lru_conv_w": (2, 60, 32), "lru_conv_b": (2, 92, 8),
    "lru_ba": (2, 100, 8), "lru_bx": (2, 108, 8), "lru_lambda": (2, 116, 8)}
PARAM_DMAS = len(PARAM_ROWS) + 4
ROW_DMAS = 7


def as_rows(ap):
    if len(ap.shape) == 1:
        return ap.rearrange("(c x) -> c x", x=P)
    if len(ap.shape) == 2:
        return ap.rearrange("l (c x) -> (l c) x", x=P)
    return ap.rearrange("l t (c x) -> (l t c) x", x=P)


def trunk(nc, I, O):
    with ExitStack() as ctx:
        def sb(name, shape, dt=F32):
            return ctx.enter_context(nc.sbuf_tensor(name, shape, dt))

        S = {n: ctx.enter_context(nc.semaphore("s_" + n)) for n in SEMS}

        psd = [ctx.enter_context(nc.psum_tensor(f"psd{i}", [P, 1024], F32)) for i in range(2)]
        psw = [ctx.enter_context(nc.psum_tensor(f"psw{i}", [P, 1024], F32)) for i in range(2)]
        xh, xl = sb("xh", [P, KT, T], F32R), sb("xl", [P, KT, T], F32R)
        arena = sb("arena", [P, KT * T])
        KH = KT // 2
        NW = 3
        w_raw = sb("w_raw", [P, NW, KH, P])
        w_hi, w_lo = sb("w_hi", [P, NW, KH, P], F32R), sb("w_lo", [P, NW, KH, P], F32R)
        raws = sb("raws", [P, 6 * T])
        stage = sb("stage", [P, 2, T])
        extra = sb("extra", [P, 4 * T])
        sbuf = sb("states", [P, 2048])
        hist = sb("hist", [P, 44, 36])
        smp = sb("smp", [P, 4, NB, TAPS - 1 + LS])
        pv = sb("pv", [P, 3 * P])
        cols = sb("cols", [P, NT + 1, P])
        rowG, rowB, rowlr = sb("rowG", [P, T]), sb("rowB", [P, T]), sb("rowlr", [P, T])
        ident, ones = sb("ident", [P, P]), sb("ones", [P, P])
        cb16 = sb("cb16", [P, 14 * P + P + P + 32 + T + 8 * 32 + 8], BF16)
        cst = sb("cst", [P, 8])
        egt = sb("egt", [P, SSD_H * 12 + 8])
        small = sb("small", [P, 64])
        selp = sb("selp", [P, P])
        wa2 = sb("wa2", [P, GLA_KW])

        MX = cb16[:, 0:7 * P].rearrange("p (l j) -> p l j", l=7)
        MT = cb16[:, 7 * P:14 * P].rearrange("p (l j) -> p l j", l=7)
        o16 = 14 * P
        ib16, negm, negs = cb16[:, o16:o16 + P], cb16[:, o16 + P:o16 + 2 * P], cb16[0:NS, o16 + 2 * P:o16 + 2 * P + NS]
        o16 += 2 * P + NS
        rmask = cb16[:, o16:o16 + T]
        bmask = cb16[:, o16 + T:o16 + T + NB * NS].rearrange("p (b i) -> p b i", b=NB)
        rowm = cb16[0:NS, o16 + T + NB * NS:o16 + T + NB * NS + NB]

        uT = nc.dram_tensor("uT_scratch", [60, P, T], F32, kind="Internal").ap()
        yT = nc.dram_tensor("yT_scratch", [KT, P, T], F32, kind="Internal").ap()
        hD = nc.dram_tensor("hT_scratch", [KT, P, T], F32, kind="Internal").ap()

        def pvc(name, i, n=1):
            col, row, _ = PARAM_ROWS[name]
            return pv[:, P * col + row + i:P * col + row + i + n]

        def slot(i, n=1, w=T):
            return arena[:, T * i:T * i + n * w]

        def ssd_x(p):
            return rowlr[:, :] if p % 2 else arena[:, 5632:5632 + T]

        def lru_slot(j, i):
            return slot(7 * (j % 2) + i)

        zloads, n = {}, 0
        for u in UNITS + UNITS_CD:
            if u[0] in ("dn", "ssd", "lru"):
                n += 16
                zloads[u] = n

        def hT(c):
            return arena[:, T * c:T * (c + 1)]

        def tiles4(ap):
            return ap.rearrange("p (t i) -> p t i", t=NT)

        def bc4(ap):
            return ap.unsqueeze(1).broadcast_to([ap.shape[0], NT, ap.shape[1]])

        def tok(t):
            return (P * t, P) if t < NT else (SEQ, NS)

        TILES = column_tiles()
        GROUPS = group_table()
        NO = {(u, n): i for i, (u, n, _, _) in enumerate(GROUPS)}
        assert len(NO) == len(GROUPS)
        first = {}
        for d, t in enumerate(TILES):
            first.setdefault(t[3], d)
        staged = {}
        count = [0, 0]
        for ph in ("ab", "cd"):
            for d in [d for d, t in enumerate(TILES) if t[3] == ph][1:]:
                e = sum(count) % 2
                count[e] += 1
                staged[d] = (d - first[ph] - 1, e, 16 * count[e])
        SL = KT
        NSL = SL * len(TILES)
        XPH = (0, 2, 3, 5)
        phases = ["ab", "out0", "gate0", "cd", "out1", "gate1"]

        def first_slice(ph):
            return SL * first[ph]

        def end_slice(ph):
            i = phases.index(ph) + 1
            return SL * first[phases[i]] if i < len(phases) else NSL

        RAW = {}
        d = first["ab"] + 1
        for h in range(DN_H):
            RAW["dn", h] = (d, 4)
            d += 4
        for h in range(GLA_H):
            RAW["gla", h] = (d, 6)
            d += 6
        d = first["cd"] + 1
        RAW["bc", 0] = (d, 4)
        d += 4
        for p in range(SSD_H // 2):
            RAW["ssd", p] = (d, 2)
            d += 2
        for j in range(LRU_W // P):
            RAW["lru", j] = (d, 2)
            d += 2

        target = {}
        for ph, units in (("ab", UNITS), ("cd", UNITS_CD)):
            last = SL * (first[ph] + 1)
            for i, u in enumerate(units):
                nxt = [SL * (RAW[v][0] + RAW[v][1]) for v in units[i + 1:] if v in RAW]
                lead = LEAD if i + 1 < len(units) and units[i + 1] in zloads else 2
                end = min(nxt[0] + lead, end_slice(ph)) if nxt else end_slice(ph)
                mine = [n for (v, n, _, _) in GROUPS if v == u]
                weight = [FILL.get((u[0], n), FILL.get(u[0], 1.0)) for n in mine]
                for j, n in enumerate(mine):
                    target[u, n] = last + int((end - last) * sum(weight[:j + 1]) / sum(weight) + 1e-6)
                target[u, "start"] = last
                if mine or u[0] in RAW:
                    last = max(last, end)
                target[u, "end"] = last

        STORES = {"dn": 3, "gla": 3, "ab_tail": 6, "ssd": 2, "lru": 1, "cd_tail": 6}
        stored, total = {}, 0
        for u in UNITS + UNITS_CD:
            stored[u] = total
            n = STORES.get(u[0], 0)
            if u[0] == "ssd" and u[1] % 2 == 0:
                n -= 1
            total += 16 * n
        stored["end"] = total
        loads = {}
        n = 0
        for u in UNITS + UNITS_CD:
            if u in RAW:
                n += 16
                loads[u] = n
        sloads, n = {}, 0
        for u in UNITS + UNITS_CD:
            if u[0] in ("dn", "gla"):
                n += 16
            if u[0] == "ssd":
                n += 32
            if u[0] == "lru":
                n += 64
            sloads[u] = n

        block = ctx.enter_context(nc.Block())

        W_DRAM = {"ab": I["ab_w_in"], "abo": I["ab_w_out"], "gate": I["ple_w_gate"], "cd": I["cd_w_in"],
                  "cdo": I["cd_w_out"]}

        @block.sync
        def _(sp):
            for q in range(2 * len(TILES)):
                name, layer, starts, _ = TILES[q // 2]
                if q >= NW:
                    sp.wait_ge(S["lo_ready"], q - NW + 1)
                width = P // len(starts)
                for i, c in enumerate(starts):
                    src = W_DRAM[name][layer, 1024 * (q % 2):1024 * (q % 2) + 1024, c:c + width]
                    sp.dma_start(w_raw[:, q % NW, :, width * i:width * (i + 1)],
                                 src.rearrange("(k p) n -> p k n", p=P)).then_inc(S[f"w_landed{q % NW}"], 16)

        landed, c3 = [], [0, 0, 0]
        for q in range(2 * len(TILES)):
            c3[q % NW] += 16 * len(TILES[q // 2][2])
            landed.append(c3[q % NW])

        @block.tensor
        def _(pe):
            at = [0]

            def dense_slice(n):
                d, k = n // SL, n % SL
                q, r = n // KH, (n // KH) % NW
                ph = phases.index(TILES[d][3])
                if k == 0 and d >= 2:
                    pe.wait_ge(S[f"dense_read{d % 2}"], d // 2)
                if d == first[TILES[d][3]]:
                    pe.wait_ge(S[f"x_ready{k % 2}"], KH * ph + k // 2 + 1)
                if k % KH == 0:
                    pe.wait_ge(S["lo_ready"], q + 1)
                out = psd[d % 2]
                for i, (w, x) in enumerate(((w_hi, xh), (w_hi, xl), (w_lo, xh))):
                    for half in range(2):
                        mm = pe.matmul(out[:, D0 + HALF * half:D0 + HALF * (half + 1)], w[:, r, k % KH, :],
                                       x[:, k, HALF * half:HALF * (half + 1)],
                                       start=(k == 0 and i == 0), stop=(k == KT - 1 and i == 2))
                mm.then_inc(S["slice_done"], 1)

            def fill(to):
                while at[0] < to:
                    dense_slice(at[0])
                    at[0] += 1

            def group(u, name):
                if (u, name) in target:
                    fill(target[u, name])
                g = NO[u, name]
                if g >= 2:
                    _, _, reader, value = GROUPS[g - 2]
                    pe.wait_ge(S[reader], value)
                return psw[g % 2]

            def prompt_and_samples(W, lhsT, rhs, rows=P, **kw):
                pe.matmul(W[0:rows, 0:SEQ], lhsT, rhs[:, 0:SEQ], **kw)
                return pe.matmul(W[0:rows, SEQ:T], lhsT, rhs[:, SEQ:T], **kw)

            def blocks(W, lhsT, rhs, samples=True):
                for t in range(NT):
                    mm = pe.matmul(W[:, P * t:P * t + P], lhsT[:, P * t:P * t + P], rhs[:, P * t:P * t + P],
                                   start=True, stop=True)
                if samples:
                    mm = pe.matmul(W[0:NS, SEQ:T], lhsT[0:samples, SEQ:T], rhs[0:samples, SEQ:T], start=True, stop=True)
                return mm

            def to_token_major(W, src):
                for t in range(NT):
                    pe.transpose(W[:, P * t:P * t + P], src[:, P * t:P * t + P], ident[:, :])
                return pe.transpose(W[0:NS, SEQ:SEQ + P], src[:, SEQ:T], ident[:, :])

            def norm(i):
                W = group(("norm", i), "n")
                pe.wait_ge(S["sq_added"], i + 1)
                prompt_and_samples(W, ones[:, :], sbuf[:, T:2 * T], start=True, stop=True).then_inc(S["work_ready"], 1)

            def columns_of_rows(u):
                W = group(u, "c0")
                pe.wait_ge(S["rows_ready"], 1 if u[0] == "ab_rows" else 2)
                st = slot(0)
                for t in range(NT):
                    pe.transpose(W[:, P * t:P * t + P], st[:, P * t:P * t + P], ident[:, :])
                pe.transpose(W[0:NS, SEQ:SEQ + P], st[:, SEQ:T], ident[:, :]).then_inc(S["work_ready"], 1)

            def decay_exponents(u, name, h, nh):
                W = group(u, name)
                sel = ident[0:nh, h:h + 1].broadcast_to([nh, P])
                pe.matmul(W[:, 0:SEQ], sel, rowG[0:nh, 0:SEQ], start=True, stop=False)
                pe.matmul(W[:, 0:SEQ], ib16, bc4(negm), start=False, stop=True)
                pe.matmul(W[0:NS, SEQ:T], sel[:, 0:NS], rowG[0:nh, SEQ:T], start=True, stop=False)
                pe.matmul(W[0:NS, SEQ:T], ib16[0:NS, 0:NS], negs, start=False, stop=True).then_inc(S["work_ready"], 1)

            def dn(h):
                u = ("dn", h)
                q, k, v = slot(0), slot(1), slot(2)
                Tm, X, kb, qg, AT, QKT, TT = slot(3), slot(4), slot(7), slot(8), slot(9), slot(10), slot(11)
                bgk, kend, bv = (arena[:, 12 * T + 640 * i:12 * T + 640 * (i + 1)] for i in range(3))
                nwk, osq = slot(3), slot(4)
                mwk = arena[:, 12 * T + 1920:12 * T + 1920 + 256].rearrange("p (b i) -> p b i", b=NB)
                uu, SS, um = extra[:, 0:640], extra[:, 640:640 + 512], extra[0:NS, 1152:2176]
                Sin = sbuf[:, 0:1024].rearrange("p (b e) -> p b e", b=NB)
                W = group(u, "ssq")
                pe.wait_ge(S["dn_sq"], h + 1)
                prompt_and_samples(W, ones[:, :], slot(6), start=True, stop=True).then_inc(S["work_ready"], 1)
                W = group(u, "ssk")
                prompt_and_samples(W, ones[:, :], slot(7), start=True, stop=True).then_inc(S["work_ready"], 1)
                sel = ident[0:DN_H, h:h + 1].broadcast_to([DN_H, P])
                W = group(u, "gbc")
                prompt_and_samples(W, sel, rowG[0:DN_H, :], start=True, stop=True).then_inc(S["work_ready"], 1)
                W = group(u, "bbc")
                prompt_and_samples(W, sel, rowB[0:DN_H, :], start=True, stop=True).then_inc(S["work_ready"], 1)
                decay_exponents(u, "dm", h, DN_H)
                W = group(u, "kk")
                pe.wait_ge(S["dn_kb"], h + 1)
                blocks(W, k, kb, samples=P).then_inc(S["work_ready"], 1)
                W = group(u, "qk")
                blocks(W, k, q, samples=P).then_inc(S["work_ready"], 1)
                W = group(u, "t1")
                pe.wait_ge(S["dn_tt1"], h + 1)
                for t in range(NT):
                    pe.transpose(W[:, P * t:P * t + P], TT[:, P * t:P * t + P], ident[:, :])
                pe.transpose(W[0:NS, SEQ:T], TT[0:NS, SEQ:T], ident[0:NS, 0:NS]).then_inc(S["work_ready"], 1)
                W = group(u, "kt")
                to_token_major(W, k).then_inc(S["work_ready"], 1)
                W = group(u, "vt")
                to_token_major(W, v).then_inc(S["work_ready"], 1)
                for l in range(1, 7):
                    ns = NS if l == 1 else 0
                    W = group(u, f"x{l}")
                    if l == 1:
                        pe.wait_ge(S["dn_t1"], h + 1)
                    else:
                        pe.wait_ge(S["dn_tt"], 6 * h + l - 1)
                    blocks(W, AT, Tm, samples=ns).then_inc(S["work_ready"], 1)
                    if l < 6:
                        W = group(u, f"y{l}")
                        pe.wait_ge(S["dn_x"], 6 * h + l)
                        blocks(W, TT, X, samples=ns).then_inc(S["work_ready"], 1)
                    W = group(u, f"yt{l}")
                    pe.wait_ge(S["dn_x"], 6 * h + l)
                    blocks(W, X, TT, samples=ns).then_inc(S["work_ready"], 1)
                W = group(u, "wk")
                pe.wait_ge(S["dn_tt"], 6 * h + 6)
                for t in range(NT):
                    pe.matmul(W[:, P * t:P * t + P], bgk[:, P * t:P * t + P], TT[:, P * t:P * t + P], start=True, stop=True)
                pe.matmul(W[:, SEQ:T], bgk[0:NS, SEQ:SEQ + P], TT[0:NS, SEQ:T], start=True, stop=True).then_inc(S["work_ready"], 1)

                def u_step(t):
                    W = group(u, f"u{t}")
                    mm = pe.matmul(W[:, 0:P], TT[:, P * t:P * t + P], bv[:, P * t:P * t + P], start=True, stop=t == 0)
                    if t:
                        pe.wait_ge(S["dn_nwk"], h + 1)
                        pe.wait_ge(S["dn_s"], 4 * h + t)
                        mm = pe.matmul(W[:, 0:P], nwk[:, P * t:P * t + P], SS[:, P * (t - 1):P * t], start=False, stop=True)
                    mm.then_inc(S["work_ready"], 1)

                def s_step(t):
                    W = group(u, f"s{t}")
                    pe.wait_ge(S["dn_u"], 5 * h + (1, 3, 4, 5)[t])
                    pe.matmul(W[:, 0:P], kend[:, P * t:P * t + P], uu[:, P * t:P * t + P], start=True,
                              stop=True).then_inc(S["work_ready"], 1)

                u_step(0)
                W = group(u, "us")
                pe.wait_ge(S["dn_mwk"], h + 1)
                pe.wait_ge(S["s_loaded"], sloads[u])
                pe.matmul(W[0:NS, 0:P], TT[0:NS, SEQ:T], bv[0:NS, SEQ:SEQ + P], start=True, stop=False)
                for b in range(NB):
                    mm = pe.matmul(W[0:NS, 0:P], mwk[:, b, :], Sin[:, b, :], start=False, stop=b == NB - 1)
                mm.then_inc(S["work_ready"], 1)
                s_step(0)
                W = group(u, "ss")
                pe.wait_ge(S["dn_um"], h + 1)
                for i in range(2):
                    mm = pe.matmul(W[:, 512 * i:512 * i + 512], kend[0:NS, SEQ:SEQ + P], um[:, 512 * i:512 * i + 512],
                                   start=True, stop=True)
                mm.then_inc(S["work_ready"], 1)
                for t in range(1, NT):
                    u_step(t)
                    s_step(t)
                W = group(u, "o")
                for t in range(NT):
                    if t:
                        pe.matmul(W[:, P * t:P * t + P], SS[:, P * (t - 1):P * t], qg[:, P * t:P * t + P], start=True, stop=False)
                    pe.matmul(W[:, P * t:P * t + P], uu[:, P * t:P * t + P], QKT[:, P * t:P * t + P], start=t == 0, stop=True)
                mm = pe.matmul(W[:, SEQ:T], uu[0:NS, SEQ:SEQ + P], QKT[0:NS, SEQ:T], start=True, stop=True,
                               skip_group_check=True)
                for b in range(NB):
                    cc = slice(SEQ + LS * b, SEQ + LS * b + LS)
                    mm = pe.matmul(W[:, cc], Sin[:, b, :], qg[:, cc], start=False, stop=True, skip_group_check=True)
                mm.then_inc(S["work_ready"], 1)
                W = group(u, "n")
                pe.wait_ge(S["dn_osq"], h + 1)
                prompt_and_samples(W, ones[:, :], osq, start=True, stop=True).then_inc(S["work_ready"], 1)

            def gla(h):
                u = ("gla", h)
                q, k = raws[:, 0:T], raws[:, T:2 * T]
                qg, kendT, qt, kt, AT = slot(6), slot(7), slot(9), slot(10), slot(11)
                kend = arena[:, 12 * T:12 * T + 640]
                vt = arena[:, 12 * T + 640:12 * T + 1920].rearrange("p (t e) -> p t e", t=NT + 1)
                SS = extra[:, 0:1024].rearrange("p (t e) -> p t e", t=NT)
                um = extra[0:NS, 1024:2048]
                Sin = sbuf[:, :].rearrange("p (b e) -> p b e", b=NB)
                W = group(u, "lg")
                prompt_and_samples(W, wa2[64:64 + GLA_R, P * h:P * h + P], rowlr[64:64 + GLA_R, :],
                                   start=True, stop=True).then_inc(S["work_ready"], 1)
                W = group(u, "qk")
                pe.wait_ge(S["gl_q"], h + 1)
                blocks(W, k, q, samples=P).then_inc(S["work_ready"], 1)
                for l in range(7):
                    W = group(u, f"l{l}")
                    pe.wait_ge(S["gl_qkt"], 7 * h + l + 1)
                    blocks(W, kt, qt, samples=P if l < 2 else 0).then_inc(S["work_ready"], 1)
                W = group(u, "kt")
                to_token_major(W, kendT).then_inc(S["work_ready"], 1)
                for e in range(2):
                    W = group(u, f"v{e}")
                    to_token_major(W, raws[:, T * (2 + e):T * (3 + e)]).then_inc(S["work_ready"], 1)
                W = group(u, "sA")
                pe.wait_ge(S["gl_v"], 2 * h + 2)
                for t in range(NT):
                    mm = pe.matmul(W[:, 256 * t:256 * t + 256], kend[:, P * t:P * t + P], vt[:, t, :], start=True, stop=True)
                mm.then_inc(S["work_ready"], 1)
                for e in range(2):
                    W = group(u, f"o{e}")
                    if e == 0:
                        pe.wait_ge(S["gl_s"], h + 1)
                        pe.wait_ge(S["s_loaded"], sloads[u])
                    ec = slice(P * e, P * e + P)
                    for t in range(NT):
                        pe.matmul(W[:, P * t:P * t + P], vt[:, t, ec], AT[:, P * t:P * t + P], start=True, stop=t == 0)
                        if t:
                            pe.matmul(W[:, P * t:P * t + P], SS[:, t - 1, ec], qg[:, P * t:P * t + P], start=False, stop=True)
                    mm = pe.matmul(W[:, SEQ:T], vt[0:NS, NT, ec], AT[0:NS, SEQ:T], start=True, stop=True, skip_group_check=True)
                    for b in range(NB):
                        cc = slice(SEQ + LS * b, SEQ + LS * b + LS)
                        mm = pe.matmul(W[:, cc], Sin[:, b, ec], qg[:, cc], start=False, stop=True, skip_group_check=True)
                    mm.then_inc(S["work_ready"], 1)
                for i in range(2):
                    W = group(u, f"sb{i}")
                    pe.wait_ge(S["gl_um"], 2 * h + i + 1)
                    for j in range(2):
                        mm = pe.matmul(W[:, 512 * j:512 * j + 512], kend[0:NS, SEQ:SEQ + P], um[:, 512 * j:512 * j + 512],
                                       start=True, stop=True)
                    mm.then_inc(S["work_ready"], 1)
                W = group(u, "n")
                pe.wait_ge(S["gl_osq"], 2 * h + 2)
                for e in range(2):
                    pe.matmul(W[:, 0:SEQ], ones[:, :], slot(9 + e)[:, 0:SEQ], start=e == 0, stop=e == 1)
                    mm = pe.matmul(W[:, SEQ:T], ones[:, :], slot(9 + e)[:, SEQ:T], start=e == 0, stop=e == 1)
                mm.then_inc(S["work_ready"], 1)

            def bc():
                u = ("bc", 0)
                Bt = arena[:, 8 * T:8 * T + 1280].rearrange("p (t n) -> p t n", t=NT + 1)
                W = group(u, "bt")
                pe.wait_ge(S["bc_silu"], 1)
                for t in range(NT):
                    for i in range(2):
                        mm = pe.transpose(W[:, 256 * t + P * i:256 * t + P * i + P], slot(i)[:, P * t:P * t + P], ident[:, :])
                mm.then_inc(S["work_ready"], 1)
                W = group(u, "bts")
                for i in range(2):
                    mm = pe.transpose(W[0:NS, P * i:P * i + P], slot(i)[:, SEQ:T], ident[:, :])
                mm.then_inc(S["work_ready"], 1)
                for g in range(SSD_G):
                    W = group(u, f"cb{g}")
                    pb = SSD_N * (g % 2)
                    B, C = slot(g // 2)[pb:pb + SSD_N, :], slot(2 + g // 2)[pb:pb + SSD_N, :]
                    blocks(W, B, C, samples=SSD_N).then_inc(S["work_ready"], 1)

            def ssd(p):
                u = ("ssd", p)
                g = p // 2
                pb = SSD_N * (g % 2)
                hp = slice(pb, pb + SSD_N)
                C = slot(2 + g // 2)[hp, :]
                Bt = arena[:, 8 * T:8 * T + 1280].rearrange("p (t n) -> p t n", t=NT + 1)
                A = [slot(0), slot(1)]
                xs = ssd_x(p)
                v, v2, SS = arena[:, 6720:7360], arena[:, 7360:8000], arena[:, 8000:8640]
                um = extra[0:NS, 0:1024]
                Sin = sbuf[:, 0:1024].rearrange("p (b e) -> p b e", b=NB)
                decay_exponents(u, "dmA", 2 * p, SSD_H)
                decay_exponents(u, "dmB", 2 * p + 1, SSD_H)
                W = group(u, "ebc")
                pe.wait_ge(S["sp_sel"], p + 1)
                prompt_and_samples(W, selp[0:SSD_H, :], rowG[0:SSD_H, :], start=True, stop=True).then_inc(S["work_ready"], 1)
                W = group(u, "xt")
                pe.wait_ge(S["sp_silu"], p + 1)
                to_token_major(W, xs).then_inc(S["work_ready"], 1)
                W = group(u, "sP")
                pe.wait_ge(S["sp_v"], p + 1)
                for t in range(NT):
                    mm = pe.matmul(W[hp, P * t:P * t + P], Bt[:, t, SSD_N * g:SSD_N * (g + 1)], v2[:, P * t:P * t + P],
                                   start=True, stop=True)
                mm.then_inc(S["work_ready"], 1)
                W = group(u, "ss")
                pe.wait_ge(S["sp_um"], p + 1)
                for i in range(2):
                    mm = pe.matmul(W[hp, 512 * i:512 * i + 512], Bt[0:NS, NT, SSD_N * g:SSD_N * (g + 1)],
                                   um[:, 512 * i:512 * i + 512], start=True, stop=True)
                mm.then_inc(S["work_ready"], 1)
                W = group(u, "i")
                pe.wait_ge(S["sp_s"], p + 1)
                pe.wait_ge(S["s_loaded"], sloads[u])
                for t in range(NT):
                    pe.matmul(W[:, P * t:P * t + P], SS[hp, P * t:P * t + P], C[:, P * t:P * t + P], start=True, stop=True)
                for b in range(NB):
                    cc = slice(SEQ + LS * b, SEQ + LS * b + LS)
                    mm = pe.matmul(W[:, cc], Sin[hp, b, :], C[:, cc], start=True, stop=True)
                mm.then_inc(S["work_ready"], 1)
                W = group(u, "o")
                pe.wait_ge(S["sp_A"], p + 1)
                for e in range(2):
                    he = slice(SSD_N * e, SSD_N * (e + 1))
                    for t in range(NT):
                        pe.matmul(W[he, P * t:P * t + P], v[:, P * t + SSD_N * e:P * t + SSD_N * (e + 1)],
                                  A[e][:, P * t:P * t + P], start=True, stop=True)
                    mm = pe.matmul(W[he, SEQ:T], v[0:NS, SEQ + SSD_N * e:SEQ + SSD_N * (e + 1)], A[e][0:NS, SEQ:T],
                                   start=True, stop=True)
                mm.then_inc(S["work_ready"], 1)
                if p % 2:
                    W = group(u, "n")
                    pe.wait_ge(S["sp_sq"], p + 1)
                    for e in range(2):
                        sq = raws[:, T * (2 + e):T * (3 + e)]
                        pe.matmul(W[:, 0:SEQ], ones[:, :], sq[:, 0:SEQ], start=e == 0, stop=e == 1)
                        mm = pe.matmul(W[:, SEQ:T], ones[:, :], sq[:, SEQ:T], start=e == 0, stop=e == 1)
                    mm.then_inc(S["work_ready"], 1)

            def lru(j):
                u = ("lru", j)
                bd = sbuf[:, 256 * (j % 2):256 * (j % 2) + 256].rearrange("p (i n) -> p i n", i=2)
                for i, name in enumerate("ri"):
                    W = group(u, name)
                    if i == 0:
                        pe.wait_ge(S["lr_conv"], j + 1)
                        pe.wait_ge(S["s_loaded"], sloads[u])
                    prompt_and_samples(W, bd[:, i, :], lru_slot(j, 0), start=True, stop=True).then_inc(S["work_ready"], 1)

            def tail(u, ntiles, base, rows):
                pe.wait_ge(S["tail_made"], 1 if u[0] == "ab_tail" else 2)
                i = 0
                for n, (b0, nt) in enumerate(zip(base, ntiles)):
                    W = group(u, f"t{n}")
                    for j in range(nt):
                        mm = pe.transpose(W[0:rows[n], P * j:P * j + P], hist[:, b0 + j, 0:rows[n]], ident[:, :])
                    mm.then_inc(S["work_ready"], 1)

            def gate(layer):
                u = ("gate", layer)
                ptok = raws[:, 0:1280].rearrange("p (t c) -> p t c", t=NT + 1)
                pT = raws[:, 1280:1280 + 2 * T].rearrange("p (k t) -> p k t", k=2)
                wp = raws[:, 2368:2880].rearrange("p (s k n) -> p s k n", s=2, k=2)
                for i in range(2):
                    W = group(u, f"p{i}")
                    if i == 0:
                        pe.wait_ge(S["p_loaded"], 32 * (layer + 1))
                    for t in range(NT + 1):
                        c, n = tok(t)
                        mm = pe.transpose(W[:, c:c + n], ptok[0:n, t, P * i:P * i + P], ident[0:n, 0:n])
                    mm.then_inc(S["work_ready"], 1)
                _, _, reader, value = GROUPS[NO[u, "p1"]]
                pe.wait_ge(S[reader], value)
                for c in range(KT):
                    fill(first_slice(f"gate{layer}") + SL * (c + 1))
                    W = group(u, f"g{c}")
                    pe.wait_ge(S[f"wp_loaded{c % 2}"], 16 * (8 * layer + c // 2 + 1))
                    for k in range(2):
                        pe.matmul(W[:, 0:SEQ], wp[:, c % 2, k, :], pT[:, k, 0:SEQ], start=k == 0, stop=k == 1)
                        mm = pe.matmul(W[:, SEQ:T], wp[:, c % 2, k, :], pT[:, k, SEQ:T], start=k == 0, stop=k == 1)
                    mm.then_inc(S["work_ready"], 1)

            u = ("setup", 0)
            pe.wait_ge(S["consts_loaded"], 16)
            pe.wait_ge(S["masks_loaded"], 16)
            pe.wait_ge(S["consts_set"], 1)
            W = group(u, "pv")
            pe.wait_ge(S["params_loaded"], PARAM_DMAS * 16)
            for i, n in enumerate((88, 103, 124)):
                mm = pe.transpose(W[:, P * i:P * i + n], slot(0)[0:n, P * i:P * i + P], ident[0:n, 0:n])
            mm.then_inc(S["work_ready"], 1)
            W = group(u, "h0")
            hrow = arena[:, T:]
            for i in range(24):
                mm = pe.transpose(W[:, 32 * i:32 * i + 24], hrow[0:24, P * i:P * i + P], ident[0:24, 0:24])
            mm.then_inc(S["work_ready"], 1)
            W = group(u, "h1")
            for i in range(12):
                pe.transpose(W[:, 24 * i:24 * i + 24], hrow[0:24, 3072 + P * i:3072 + P * i + P], ident[0:24, 0:24])
            for i in range(8):
                mm = pe.transpose(W[:, 512 + 32 * i:512 + 32 * i + 32], hrow[0:32, 4608 + P * i:4608 + P * i + P],
                                  ident[0:32, 0:32])
            mm.then_inc(S["work_ready"], 1)
            for t in range(NT + 1):
                _, n = tok(t)
                src = raws if t % 2 == 0 else sbuf
                for i in range(2):
                    W = group(u, f"x{t}{i}")
                    if i == 0:
                        pe.wait_ge(S[f"x_loaded{t % 2}"], 16 * (t // 2 + 1))
                    for c in range(8):
                        mm = pe.transpose(W[:, P * c:P * c + n], src[0:n, P * (8 * i + c):P * (8 * i + c) + P],
                                          ident[0:n, 0:n])
                    mm.then_inc(S["work_ready"], 1)
            norm(0)
            fill(SL)
            for u in UNITS:
                if u[0] == "ab_rows":
                    columns_of_rows(u)
                elif u[0] == "dn":
                    dn(u[1])
                elif u[0] == "gla":
                    gla(u[1])
                else:
                    tail(u, (8, 8, 8), (0, 8, 16), (27, 27, 27))
            fill(end_slice("out0"))
            norm(1)
            gate(0)
            norm(2)
            fill(first_slice("cd") + SL)
            for u in UNITS_CD:
                if u[0] == "cd_rows":
                    W = group(u, "eg")
                    pe.wait_ge(S["eg_rows"], 1)
                    for h in range(SSD_H):
                        mm = pe.matmul(W[:, 12 * h:12 * h + 12], ident[0:SSD_H, h:h + 1].broadcast_to([SSD_H, P]),
                                  small[0:SSD_H, 16:28], start=True, stop=True)
                    mm.then_inc(S["work_ready"], 1)
                    columns_of_rows(u)
                elif u[0] == "bc":
                    bc()
                elif u[0] == "ssd":
                    ssd(u[1])
                elif u[0] == "lru":
                    lru(u[1])
                else:
                    tail(u, (8, 4, 8), (24, 32, 36), (27, 27, 36))
            fill(end_slice("out1"))
            norm(3)
            gate(1)
            norm(4)
            pe.wait_ge(S["nrm_hi"], 4 * KT + KT)
            for t in range(NT + 1):
                c0, n = tok(t)
                for i in range(2):
                    W = group(("final", 0), f"y{t}{i}")
                    for c in range(8):
                        mm = pe.transpose(W[0:n, P * c:P * c + P], hT(8 * i + c)[:, c0:c0 + n], ident[:, :])
                    mm.then_inc(S["work_ready"], 1)

        @block.scalar
        def _(act):
            at, chained, evac = [0], [0], [0]

            def link(ins):
                chained[0] += 1
                ins.then_inc(S["act_chain"], 1)
                act.wait_ge(S["act_chain"], chained[0])

            def split_hi(q):
                act.wait_ge(S[f"w_landed{q % NW}"], landed[q])
                if q >= NW:
                    act.wait_ge(S["slice_done"], KH * (q - NW + 1))
                act.copy(w_hi[:, q % NW], w_raw[:, q % NW]).then_inc(S["hi_ready"], 1)

            def evacuate(d):
                evac[0] = d + 1
                if TILES[d][3] not in ("ab", "cd"):
                    return
                act.wait_ge(S["slice_done"], SL * (d + 1))
                src = psd[d % 2][:, D0:D0 + T]
                if d in staged:
                    i, e, n = staged[d]
                    if n > 16:
                        act.wait_ge(S[f"stage_stored{e}"], n - 16)
                    act.copy(stage[:, e, :], src).then_inc(S[f"dense_read{d % 2}"], 1)
                    act.wait_ge(S[f"dense_read{d % 2}"], d // 2 + 1)
                    act.dma_start(uT[i], stage[:, e, :]).then_inc(S[f"stage_stored{e}"], 16)
                else:
                    act.copy(rowlr[:, :], src).then_inc(S[f"dense_read{d % 2}"], 1)

            def fill(to):
                while at[0] < to:
                    n = at[0]
                    if n % KH == 0 and n // KH + 2 < NSL // KH:
                        split_hi(n // KH + 2)
                    if n % SL == 1 and evac[0] < n // SL:
                        evacuate(n // SL - 1)
                    at[0] += 1
                if to in (end_slice("ab"), end_slice("cd")) and evac[0] < to // SL:
                    evacuate(to // SL - 1)

            def group(u, name):
                if (u, name) in target:
                    fill(target[u, name])
                g = NO[u, name]
                act.wait_ge(S["work_ready"], g + 1)
                return psw[g % 2]

            def skip(u, name):
                fill(target[u, name])

            def free(u):
                act.wait_ge(S["out_stored"], stored[u])

            def rstd_of(W, out, ready, value, done, ln):
                act.activation(out, W[:, 0:T], ACT.Ln, bias=cst[:, 0:1], scale=ready).then_inc(ln, 1)
                act.wait_ge(ln, value)
                act.activation(out, out, ACT.Exp, scale=-0.5).then_inc(done, 1)

            def square(i, c):
                if c >= 3:
                    act.wait_ge(S["sq_summed"], (KT - 2) * i + c - 2)
                if i % 2:
                    d = first[f"out{i // 2}"] + c
                    act.wait_ge(S[f"dense_read{d % 2}"], d // 2 + 1)
                elif i:
                    act.wait_ge(S["gate_done"], KT * (i // 2 - 1) + c + 1)
                dst = sbuf[:, T:2 * T] if c == 0 else extra[:, T * (2 + c % 2):T * (3 + c % 2)]
                act.activation(dst, hT(c), ACT.Square).then_inc(S["nrm_sq"], 1)

            def norm(i, final=False):
                if i == 0:
                    act.wait_ge(S["in_copied"], 10)
                    for c in range(KT):
                        square(i, c)
                W = group(("norm", i), "n")
                rstd_of(W, sbuf[:, 0:T], 1.0 / D_MODEL, i + 1, S["nrm_rstd"], S["nrm_ln"])
                if final:
                    return
                for c in range(KT):
                    act.wait_ge(S["nrm_tmp"], KT * i + c + 1)
                    act.copy(xh[:, c, :], extra[:, T * (2 + c % 2):T * (3 + c % 2)]).then_inc(S["nrm_hi"], 1)

            def rows_ab():
                fill(SL + 2)
                act.wait_ge(S["rows_loaded"], 16 * ROW_DMAS)
                act.wait_ge(S["h_stored"], 16)
                act.wait_ge(S["dense_read0"], 1)
                H = slice(0, DN_H)
                act.activation(rowB[H, :], rowlr[0:DN_H, :], ACT.Sigmoid).then_inc(S["rows_act"], 1)
                link(act.activation(slot(1)[H, :], rowlr[32:32 + DN_H, :], ACT.Identity))
                rows_tail(DN_H, 1, small[H, 0:1], small[H, 1:2], slot(1))

            def rows_tail(nh, n, bias, alog, a):
                H = slice(0, nh)
                link(act.activation(slot(2)[H, :], a[H, :], ACT.Abs, bias=bias))
                link(act.activation(slot(2)[H, :], slot(2)[H, :], ACT.Exp, scale=-1.0))
                act.activation(slot(2)[H, :], slot(2)[H, :], ACT.Ln, bias=cst[H, 1:2]).then_inc(S["rows_act"], 1)
                act.activation(small[H, 40:41], alog, ACT.Exp).then_inc(S["rows_act"], 1)
                act.wait_ge(S["rows_dve"], n)
                act.activation(slot(5)[H, :], rowG[H, :], ACT.Exp)
                act.activation(slot(6)[H, :], slot(6)[H, :], ACT.Exp).then_inc(S["rows_act"], 1)

            def columns_of_rows(u):
                W = group(u, "c0")
                act.copy(cols[:, 0:NT, :], tiles4(W[:, 0:SEQ]))
                act.copy(cols[0:NS, NT, :], W[0:NS, SEQ:SEQ + P]).then_inc(S["rows_copied"], 1)

            def decays(W, dst, col, done):
                for t in range(NT):
                    act.activation(dst[:, P * t:P * t + P], W[:, P * t:P * t + P], ACT.Exp, bias=cols[:, t, col:col + 1])
                act.activation(dst[0:NS, SEQ:T], W[0:NS, SEQ:T], ACT.Exp, bias=cols[0:NS, NT, col:col + 1]).then_inc(done, 1)

            def silu_squares(h):
                act.wait_ge(S["dn_conv"], h + 1)
                act.activation(slot(0, 3), slot(0, 3), ACT.Silu).then_inc(S["dn_silu"], 1)
                act.wait_ge(S["dn_silu"], h + 1)
                act.activation(slot(6, 2), slot(0, 2), ACT.Square).then_inc(S["dn_sq"], 1)

            def dn(h):
                u = ("dn", h)
                if h == 0:
                    fill(target[u, "start"])
                    act.wait_ge(S["rows_copied"], 1)
                    silu_squares(0)
                uu = extra[:, 0:640]
                W = group(u, "ssq")
                if h:
                    act.wait_ge(S["dn_y"], h)
                act.activation(slot(3), W[:, 0:T], ACT.Ln, bias=cst[:, 0:1]).then_inc(S["dn_ln"], 1)
                W = group(u, "ssk")
                act.activation(slot(4), W[:, 0:T], ACT.Ln, bias=cst[:, 0:1]).then_inc(S["dn_ln"], 1)
                act.wait_ge(S["dn_ln"], 3 * h + 2)
                act.activation(slot(3, 2), slot(3, 2), ACT.Exp, scale=-0.5).then_inc(S["dn_rs"], 1)
                W = group(u, "gbc")
                if h:
                    act.wait_ge(S["dn_s"], 4 * h)
                    act.wait_ge(S["dn_gs"], h)
                act.activation(slot(5), W[:, 0:T], ACT.Exp).then_inc(S["dn_eg"], 1)
                skip(u, "bbc")
                W = group(u, "dm")
                decays(W, slot(6), h, S["dn_D"])
                skip(u, "kk")
                skip(u, "qk")
                W = group(u, "t1")
                act.wait_ge(S["dn_kb"], h + 1)
                act.copy(slot(3)[:, 0:SEQ], W[:, 0:SEQ])
                act.copy(slot(3)[0:NS, SEQ:T], W[0:NS, SEQ:T]).then_inc(S["dn_t1"], 1)
                for n, _, _ in dn_groups()[8:27]:
                    if n != "wk":
                        skip(u, n)
                W = group(u, "wk")
                act.mul(slot(3), W[:, 0:T], -1.0).then_inc(S["dn_nwk"], 1)

                def u_copy(t):
                    W = group(u, f"u{t}")
                    act.copy(uu[:, P * t:P * t + P], W[:, 0:P]).then_inc(S["dn_u"], 1)

                u_copy(0)
                W = group(u, "us")
                act.copy(uu[0:NS, SEQ:SEQ + P], W[0:NS, 0:P]).then_inc(S["dn_u"], 1)
                skip(u, "s0")
                skip(u, "ss")
                for t in range(1, NT):
                    u_copy(t)
                    skip(u, f"s{t}")
                z = raws[:, 3 * T:4 * T]
                act.wait_ge(S["z_loaded"], zloads[u])
                act.activation(z, z, ACT.Silu).then_inc(S["dn_z"], 1)
                W = group(u, "o")
                act.activation(slot(4), W[:, 0:T], ACT.Square).then_inc(S["dn_osq"], 1)
                W = group(u, "n")
                rstd_of(W, slot(3), 1.0 / P, 3 * h + 3, S["dn_rstd"], S["dn_ln"])
                if h + 1 < DN_H:
                    silu_squares(h + 1)

            def gla(h):
                u = ("gla", h)
                fill(target[u, "start"])
                free(u)
                kend = arena[:, 12 * T:12 * T + 640]
                vt = arena[:, 12 * T + 640:12 * T + 1920].rearrange("p (t e) -> p t e", t=NT + 1)
                act.wait_ge(S["u_loaded"], loads[u])
                act.mul(raws[:, 0:T], raws[:, 0:T], float(P) ** -0.5).then_inc(S["gl_q"], 1)
                link(act.activation(raws[:, 4 * T:6 * T], raws[:, 4 * T:6 * T], ACT.Silu))
                W = group(u, "lg")
                act.activation(slot(0), W[:, 0:T], ACT.Abs, bias=pvc("gla_ba", h)).then_inc(S["gl_abs"], 1)
                act.wait_ge(S["gl_abs"], h + 1)
                link(act.activation(slot(1), slot(0), ACT.Exp, scale=-1.0))
                act.activation(slot(1), slot(1), ACT.Ln, bias=cst[:, 1:2]).then_inc(S["gl_l"], 1)
                act.wait_ge(S["gl_G"], h + 1)
                act.activation(slot(4), slot(3), ACT.Exp, scale=1.0 / 16).then_inc(S["gl_eg"], 1)
                act.wait_ge(S["gl_kd"], h + 1)
                act.activation(slot(5), slot(5), ACT.Exp, scale=1.0 / 16).then_inc(S["gl_kf"], 1)
                skip(u, "qk")
                for l in range(7):
                    E = slot((8, 2)[l % 2])
                    act.wait_ge(S["gl_ed"], 7 * h + l + 1)
                    act.activation(E, E, ACT.Exp, scale=1.0 / 16).then_inc(S["gl_E"], 1)
                    skip(u, f"l{l}")
                W = group(u, "kt")
                act.copy(kend[:, 0:SEQ], W[:, 0:SEQ])
                act.copy(kend[0:NS, SEQ:SEQ + P], W[0:NS, SEQ:SEQ + P]).then_inc(S["gl_kend"], 1)
                for e in range(2):
                    W = group(u, f"v{e}")
                    ec = slice(P * e, P * e + P)
                    act.copy(vt[:, 0:NT, ec], tiles4(W[:, 0:SEQ]))
                    act.copy(vt[0:NS, NT, ec], W[0:NS, SEQ:SEQ + P]).then_inc(S["gl_v"], 1)
                skip(u, "sA")
                for e in range(2):
                    W = group(u, f"o{e}")
                    act.activation(slot(9 + e), W[:, 0:T], ACT.Square).then_inc(S["gl_osq"], 1)
                skip(u, "sb0")
                skip(u, "sb1")
                W = group(u, "n")
                rstd_of(W, slot(2), 1.0 / 256, h + 1, S["gl_rstd"], S["gl_ln"])

            def bc():
                u = ("bc", 0)
                fill(target[u, "start"])
                Bt = arena[:, 8 * T:8 * T + 1280].rearrange("p (t n) -> p t n", t=NT + 1)
                act.wait_ge(S["bc_conv"], 1)
                act.activation(slot(0, 4), slot(0, 4), ACT.Silu).then_inc(S["bc_silu"], 1)
                W = group(u, "bt")
                act.copy(Bt[:, 0:NT, :], W[:, :].rearrange("p (t n) -> p t n", t=NT)).then_inc(S["bc_b"], 1)
                W = group(u, "bts")
                act.copy(Bt[0:NS, NT, :], W[0:NS, 0:256]).then_inc(S["bc_b"], 1)
                for g in range(SSD_G):
                    W = group(u, f"cb{g}")
                    act.copy(slot(4 + g)[:, 0:SEQ], W[:, 0:SEQ])
                    act.copy(slot(4 + g)[0:NS, SEQ:T], W[0:NS, SEQ:T]).then_inc(S["bc_cb"], 1)

            def ssd(p):
                u = ("ssd", p)
                if p == 0:
                    fill(target[u, "start"])
                    free(u)
                    act.wait_ge(S["sp_conv"], 1)
                    act.activation(ssd_x(0), ssd_x(0), ACT.Silu).then_inc(S["sp_silu"], 1)
                    act.wait_ge(S["rows_copied"], 3)
                    act.wait_ge(S["bc_cb"], 4)
                for i, n in enumerate(("dmA", "dmB")):
                    W = group(u, n)
                    decays(W, slot(i), 2 * p + i, S["sp_D"])
                W = group(u, "ebc")
                act.activation(arena[:, 6176:6176 + T], W[:, 0:T], ACT.Exp).then_inc(S["sp_ebc"], 1)
                act.wait_ge(S["z_loaded"], zloads[u])
                act.activation(raws[:, T:2 * T], raws[:, T:2 * T], ACT.Silu).then_inc(S["sp_z"], 1)
                if p + 1 < SSD_H // 2:
                    act.wait_ge(S["sp_conv"], p + 2)
                    act.activation(ssd_x(p + 1), ssd_x(p + 1), ACT.Silu).then_inc(S["sp_silu"], 1)
                for n in ("xt", "sP", "ss", "i", "o"):
                    skip(u, n)
                act.wait_ge(S["sp_y"], p + 1)
                e = p % 2
                act.activation(raws[:, T * (2 + e):T * (3 + e)], extra[:, 1024 + T * e:1024 + T * (e + 1)],
                               ACT.Square).then_inc(S["sp_sq"], 1)
                if e:
                    W = group(u, "n")
                    rstd_of(W, raws[:, 5 * T:6 * T], 1.0 / 256, p // 2 + 1, S["sp_rstd"], S["sp_ln"])

            def lru(j):
                u = ("lru", j)
                if j == 0:
                    fill(target[u, "start"])
                free(("lru", max(j - 1, 0)))
                W = group(u, "r")
                act.activation(lru_slot(j, 1), W[:, 0:T], ACT.Sigmoid, bias=pvc("lru_ba", j)).then_inc(S["lr_r"], 1)
                W = group(u, "i")
                act.activation(lru_slot(j, 2), W[:, 0:T], ACT.Sigmoid, bias=pvc("lru_bx", j)).then_inc(S["lr_i"], 1)
                act.wait_ge(S["lr_r"], j + 1)
                act.activation(lru_slot(j, 3), lru_slot(j, 1), ACT.Exp, scale=small[:, 48 + j:49 + j])
                act.activation(lru_slot(j, 4), lru_slot(j, 1), ACT.Tanh, scale=small[:, 56 + j:57 + j]).then_inc(S["lr_a"], 1)
                act.wait_ge(S["z_loaded"], zloads[u])
                act.activation(raws[:, T:2 * T], raws[:, T:2 * T], ACT.Silu).then_inc(S["lr_z"], 1)
                act.wait_ge(S["lr_t"], j + 1)
                act.activation(lru_slot(j, 5), lru_slot(j, 5), ACT.Sqrt).then_inc(S["lr_sq"], 1)

            def tail(u, first_group):
                for n in range(3):
                    rows = 36 if (u[0], n) == ("cd_tail", 2) else 27
                    W = group(u, f"t{n}")
                    if n == 0:
                        free(u)
                    act.copy(raws[0:rows, 1024 * n:1024 * n + 1024] if (u[0], n) != ("cd_tail", 1) else
                             raws[0:rows, 1024:1536], W[0:rows, 0:1024] if (u[0], n) != ("cd_tail", 1) else
                             W[0:rows, 0:512]).then_inc(S["tail_copied"], 1)

            def y_split(layer):
                act.wait_ge(S["y_loaded"], 16 * (layer + 1))
                act.wait_ge(S["slice_done"], end_slice(("ab", "cd")[layer]))
                for c in range(KT):
                    act.copy(xh[:, c, :], hT(c)).then_inc(S["nrm_y"], 1)

            def out_proj(layer):
                for c in range(KT):
                    fill(SL * (first[f"out{layer}"] + c + 1))
                    if c:
                        square(2 * layer + 1, c - 1)
                square(2 * layer + 1, KT - 1)

            def gate(layer):
                u = ("gate", layer)
                pT = raws[:, 1280:1280 + 2 * T].rearrange("p (k t) -> p k t", k=2)
                for i in range(2):
                    W = group(u, f"p{i}")
                    act.copy(pT[:, i, :], W[:, 0:T]).then_inc(S["in_copied"], 1)
                for c in range(KT):
                    d = first[f"gate{layer}"] + c
                    fill(SL * (d + 1))
                    act.wait_ge(S["slice_done"], SL * (d + 1))
                    if c >= 2:
                        act.wait_ge(S["gate_done"], KT * layer + c - 1)
                    act.activation(extra[:, T * (c % 2):T * (c % 2) + T], psd[d % 2][:, D0:D0 + T],
                                   ACT.Sigmoid).then_inc(S[f"dense_read{d % 2}"], 1)
                    if c:
                        square(2 * layer + 2, c - 1)
                square(2 * layer + 2, KT - 1)

            act.dma_start(ident[:, :], I["cf"]).then_inc(S["consts_loaded"], 16)
            act.wait_ge(S["consts_set"], 1)
            act.wait_ge(S["zeroed"], 1)
            split_hi(0)
            split_hi(1)
            u = ("setup", 0)
            W = group(u, "pv")
            act.copy(pv[:, 0:88], W[:, 0:88])
            act.copy(pv[:, P:P + 103], W[:, P:P + 103])
            act.copy(pv[:, 2 * P:2 * P + 124], W[:, 2 * P:2 * P + 124]).then_inc(S["in_copied"], 1)
            W = group(u, "h0")
            act.copy(hist[:, 0:24, 0:24], W[:, 0:768].rearrange("p (i r) -> p i r", i=24)[:, :, 0:24]).then_inc(S["in_copied"], 1)
            W = group(u, "h1")
            act.copy(hist[:, 24:36, 0:24], W[:, 0:288].rearrange("p (i r) -> p i r", i=12))
            act.copy(hist[:, 36:44, 0:32], W[:, 512:768].rearrange("p (i r) -> p i r", i=8)).then_inc(S["in_copied"], 1)
            for t in range(NT + 1):
                c0, n = tok(t)
                for i in range(2):
                    W = group(u, f"x{t}{i}")
                    dst = arena[:, :].rearrange("p (c t) -> p c t", c=KT)[:, 8 * i:8 * i + 8, c0:c0 + n]
                    act.copy(dst, W[:, :].rearrange("p (c t) -> p c t", c=8)[:, :, 0:n]).then_inc(S["in_copied"], 1)
            act.wait_ge(S["in_copied"], 1)
            lam = pvc("lru_lambda", 0, 8)
            link(act.activation(small[:, 48:56], lam, ACT.Abs))
            link(act.activation(small[:, 48:56], small[:, 48:56], ACT.Exp, scale=-1.0))
            act.activation(small[:, 48:56], small[:, 48:56], ACT.Ln, bias=cst[:, 1:2]).then_inc(S["rows_act"], 1)
            norm(0)
            for u in UNITS:
                if u[0] == "ab_rows":
                    rows_ab()
                    columns_of_rows(u)
                elif u[0] == "dn":
                    dn(u[1])
                elif u[0] == "gla":
                    gla(u[1])
                else:
                    fill(target[u, "start"])
                    fill(end_slice("ab"))
                    tail(u, 0)
            y_split(0)
            out_proj(0)
            norm(1)
            gate(0)
            norm(2)
            for u in UNITS_CD:
                if u[0] == "cd_rows":
                    fill(first_slice("cd") + SL + 2)
                    act.wait_ge(S["h_stored"], 32)
                    act.wait_ge(S[f"dense_read{first['cd'] % 2}"], first["cd"] // 2 + 1)
                    H = slice(0, SSD_H)
                    rows_tail(SSD_H, 2, small[H, 10:11], small[H, 11:12], rowlr)
                    act.activation(small[H, 16:20], rowG[H, 0:SEQ].rearrange("p (t i) -> p t i", t=NT)[:, :, P - 1], ACT.Exp)
                    act.activation(small[H, 20:28], rowG[H, SEQ:T].rearrange("p (b i) -> p b i", b=NB)[:, :, LS - 1],
                                   ACT.Exp).then_inc(S["eg_rows"], 1)
                    W = group(u, "eg")
                    act.copy(egt[:, 0:SSD_H * 12], W[:, 0:SSD_H * 12]).then_inc(S["rows_copied"], 1)
                    columns_of_rows(u)
                elif u[0] == "bc":
                    bc()
                elif u[0] == "ssd":
                    ssd(u[1])
                elif u[0] == "lru":
                    lru(u[1])
                else:
                    fill(end_slice("cd"))
                    tail(u, 3)
            y_split(1)
            out_proj(1)
            norm(3)
            gate(1)
            norm(4, final=True)
            for t in range(NT + 1):
                _, n = tok(t)
                dst = raws if t % 2 == 0 else sbuf
                for i in range(2):
                    W = group(("final", 0), f"y{t}{i}")
                    if t >= 2 and i == 0:
                        act.wait_ge(S[f"y_stored{t % 2}"], 16 * (t // 2))
                    act.copy(dst[0:n, 1024 * i:1024 * i + 1024], W[0:n, :]).then_inc(S["out_copied"], 1)

        @block.vector
        def _(dve):
            at, chained = [0], [0]

            def go(ins):
                chained[0] += 1
                ins.then_inc(S["dve_chain"], 1)

            def wait_chain():
                dve.wait_ge(S["dve_chain"], chained[0])

            def link(ins):
                go(ins)
                wait_chain()

            def split_lo(q):
                dve.wait_ge(S["hi_ready"], q + 1)
                dve.tensor_tensor(w_lo[:, q % NW], w_raw[:, q % NW], w_hi[:, q % NW].bitcast(F32),
                                  ALU.subtract).then_inc(S["lo_ready"], 1)

            def fill(to):
                while at[0] < to:
                    n = at[0]
                    if n % KH == 0 and n // KH + 2 < NSL // KH:
                        split_lo(n // KH + 2)
                    at[0] += 1

            def group(u, name):
                if (u, name) in target:
                    fill(target[u, name])
                g = NO[u, name]
                dve.wait_ge(S["work_ready"], g + 1)
                return psw[g % 2]

            def skip(u, name):
                fill(target[u, name])

            def free(u):
                dve.wait_ge(S["out_stored"], stored[u])

            def norm(i, final=False):
                g = pvc(("norm_g", "ple_norm", "norm_g", "ple_norm", "final_norm")[i], (0, 0, 16, 16, 0)[i], 16)
                dve.wait_ge(S["nrm_rstd"], i + 1)
                if 0 < i < 4:
                    dve.wait_ge(S["slice_done"], (0, end_slice("out0"), end_slice("gate0"), end_slice("out1"))[i])
                for c in range(KT):
                    if final:
                        dve.scalar_tensor_tensor(hT(c), hT(c), g[:, c:c + 1], sbuf[:, 0:T], ALU.mult,
                                                 ALU.mult).then_inc(S["nrm_hi"], 1)
                        continue
                    tmp = extra[:, T * (2 + c % 2):T * (3 + c % 2)]
                    if c >= 2:
                        dve.wait_ge(S[f"x_ready{c % 2}"], KH * XPH[i] + c // 2)
                    dve.scalar_tensor_tensor(tmp, hT(c), g[:, c:c + 1], sbuf[:, 0:T], ALU.mult,
                                             ALU.mult).then_inc(S["nrm_tmp"], 1)
                    if c % 2 == 0:
                        dve.wait_ge(S["nrm_hi"], KT * i + c + 1)
                        dve.tensor_tensor(xl[:, c, :], tmp, xh[:, c, :].bitcast(F32), ALU.subtract)\
                           .then_inc(S["x_ready0"], 1)

            def conv_tap(n, tap, samples, wcol, bcol, dst, done, src=0):
                if tap:
                    wait_chain()
                for i in range(n):
                    w = wcol(i, TAPS - 1 - tap)
                    if samples:
                        y = dst(i)[:, SEQ:T].rearrange("p (b s) -> p b s", b=NB)
                        x = smp[:, i, :, TAPS - 1 - tap:TAPS - 1 - tap + LS]
                    else:
                        y = dst(i)[:, tap:SEQ]
                        x = raws[:, T * (src + i):T * (src + i) + SEQ - tap]
                    if tap == 0:
                        go(dve.tensor_scalar(y, x, w, bcol(i) if bcol else None, ALU.mult, *([ALU.add] if bcol else [])))
                    elif samples and tap == TAPS - 1 and i == n - 1:
                        dve.scalar_tensor_tensor(y, x, w, y, ALU.mult, ALU.add).then_inc(done, 1)
                    else:
                        go(dve.scalar_tensor_tensor(y, x, w, y, ALU.mult, ALU.add))

            def conv(n, wcol, bcol, dst, smp_ready, value, done, src=0):
                for tap in range(TAPS):
                    conv_tap(n, tap, False, wcol, bcol, dst, done, src)
                dve.wait_ge(smp_ready, value)
                for tap in range(TAPS):
                    conv_tap(n, tap, True, wcol, bcol, dst, done, src)
                wait_chain()

            def by_token(dst, W, col, width=P, nh=1, done=None):
                w = width // nh

                def view(ap, t):
                    return ap.rearrange("p (t h e) -> p t h e", t=t, h=nh)
                a = dve.tensor_tensor(view(dst[:, 0:SEQ], NT), view(W[:, 0:SEQ], NT),
                                      cols[:, 0:NT, col:col + nh].unsqueeze(3).broadcast_to([P, NT, nh, w]), ALU.mult)
                go(a)
                b = dve.tensor_tensor(view(dst[0:NS, SEQ:SEQ + P], 1), view(W[0:NS, SEQ:SEQ + P], 1),
                                      cols[0:NS, NT:NT + 1, col:col + nh].unsqueeze(3).broadcast_to([NS, 1, nh, w]), ALU.mult)
                if done is None:
                    go(b)
                else:
                    b.then_inc(done, 1)

            def masked(dst, W, mask, done, samples=True):
                a = dve.tensor_tensor(tiles4(dst[:, 0:SEQ]), tiles4(W[:, 0:SEQ]), bc4(mask), ALU.mult)
                if samples:
                    go(a)
                    a = dve.tensor_tensor(dst[0:NS, SEQ:T], W[0:NS, SEQ:T], mask[0:NS, 0:NS], ALU.mult)
                if done is None:
                    go(a)
                else:
                    a.then_inc(done, 1)

            def minus(dst, W, samples, done):
                a = dve.tensor_tensor(dst[:, 0:SEQ], dst[:, 0:SEQ], W[:, 0:SEQ], ALU.subtract)
                if samples:
                    go(a)
                    a = dve.tensor_tensor(dst[0:NS, SEQ:T], dst[0:NS, SEQ:T], W[0:NS, SEQ:T], ALU.subtract)
                a.then_inc(done, 1)

            def cumsum(rows, src, dst, done):
                return dve.tensor_tensor_scan(dst, rmask[0:rows, :], src, 0.0, ALU.mult, ALU.add)

            def to_chunk_end(rows, dst, G, done):
                for a, b, n, m in ((0, SEQ, NT, P), (SEQ, T, NB, LS)):
                    g = G[0:rows, a:b].rearrange("p (t i) -> p t i", t=n)
                    ins = dve.tensor_tensor(dst[0:rows, a:b].rearrange("p (t i) -> p t i", t=n),
                                            g[:, :, m - 1:m].broadcast_to([rows, n, m]), g, ALU.subtract)
                    if b == T:
                        ins.then_inc(done, 1)
                    else:
                        go(ins)

            def rows_g(nh, n, bias, a):
                H = slice(0, nh)
                dve.wait_ge(S["rows_act"], 4 if n == 1 else 7)
                link(dve.tensor_scalar(slot(3)[H, :], a[H, :], bias, 0.0, ALU.add, ALU.max))
                link(dve.tensor_tensor(slot(3)[H, :], slot(3)[H, :], slot(2)[H, :], ALU.add))
                link(dve.tensor_scalar(slot(4)[H, :], slot(3)[H, :], small[H, 40:41], -1.0, ALU.mult, ALU.mult))
                link(cumsum(nh, slot(4)[H, :], rowG[H, :], None))
                to_chunk_end(nh, slot(6), rowG, S["rows_dve"])

            def rows_ab():
                dve.wait_ge(S["h_stored"], 16)
                dve.memset(slot(0), 0.0).then_inc(S["dve_chain"], 1)
                chained[0] += 1
                fill(SL)
                H = slice(0, DN_H)
                dve.wait_ge(S["rows_act"], 4)
                wait_chain()
                rows_g(DN_H, 1, small[H, 0:1], slot(1))
                go(dve.tensor_scalar(slot(0)[0:DN_H, :], rowG[H, :], -1.0, None, ALU.mult))
                go(dve.tensor_copy(slot(0)[32:32 + DN_H, :], rowB[H, :]))
                dve.wait_ge(S["rows_act"], 5)
                go(dve.tensor_tensor(slot(0)[64:64 + DN_H, :], rowB[H, :], slot(5)[H, :], ALU.mult))
                go(dve.tensor_copy(slot(0)[96:96 + DN_H, :], slot(6)[H, :]))
                wait_chain()
                dve.tensor_scalar(small[:, 41:42], cst[:, 1:2], 1.0, None, ALU.mult).then_inc(S["rows_ready"], 1)

            def rows_cd():
                dve.wait_ge(S["h_stored"], 32)
                link(dve.memset(slot(0), 0.0))
                fill(first_slice("cd") + SL)
                H = slice(0, SSD_H)
                dve.wait_ge(S["rows_act"], 7)
                rows_g(SSD_H, 2, small[H, 10:11], rowlr)
                go(dve.tensor_scalar(slot(0)[0:SSD_H, :], rowG[H, :], -1.0, None, ALU.mult))
                go(dve.tensor_copy(slot(0)[32:32 + SSD_H, :], slot(3)[H, :]))
                dve.wait_ge(S["rows_act"], 8)
                go(dve.tensor_tensor(slot(0)[64:64 + SSD_H, :], slot(3)[H, :], slot(6)[H, :], ALU.mult))
                wait_chain()
                dve.tensor_scalar(small[:, 41:42], cst[:, 1:2], 1.0, None, ALU.mult).then_inc(S["rows_ready"], 1)

            def dn_conv(h, tap, samples=False):
                steps = range(tap, TAPS) if h == 0 else (tap,)
                for tap in steps:
                    conv_tap(3, tap, samples, lambda i, w: pvc("dn_conv_w", 24 * w + 8 * i + h), None, slot, S["dn_conv"])

            def dn(h):
                u = ("dn", h)
                if h == 0:
                    fill(target[u, "start"])
                q, k = slot(0), slot(1)
                Tm, X, eG, Dm, kb, qg, AT, QKT, TT = (slot(i) for i in range(3, 12))
                bgk, kend, bv = (arena[:, 12 * T + 640 * i:12 * T + 640 * (i + 1)] for i in range(3))
                nwk = slot(3)
                mwk = arena[:, 12 * T + 1920:12 * T + 1920 + 256].rearrange("p (b i) -> p b i", b=NB)
                uu, SS = extra[:, 0:640], extra[:, 640:640 + 512]
                um = extra[0:NS, 1152:2176].rearrange("p (b e) -> p b e", b=NB)
                Snew = sbuf[:, 1024:2048]
                if h == 0:
                    dve.wait_ge(S["u_loaded"], loads[u])
                    dve.wait_ge(S["rows_copied"], 1)
                    dn_conv(0, 0)
                    dve.wait_ge(S["dn_smp"], 1)
                    dn_conv(0, 0, samples=True)
                for n in ("ssq", "ssk", "gbc"):
                    skip(u, n)
                dve.wait_ge(S["dn_rs"], h + 1)
                go(dve.scalar_tensor_tensor(q, q, float(P) ** -0.5, slot(3), ALU.mult, ALU.mult))
                link(dve.tensor_tensor(k, k, slot(4), ALU.mult))
                dve.wait_ge(S["dn_eg"], h + 1)
                go(dve.tensor_tensor(qg, q, eG, ALU.mult))
                W = group(u, "bbc")
                dve.tensor_tensor(kb, k, W[:, 0:T], ALU.mult).then_inc(S["dn_kb"], 1)
                skip(u, "dm")
                W = group(u, "kk")
                dve.wait_ge(S["dn_D"], h + 1)
                free(u)
                go(dve.tensor_tensor(AT[:, 0:SEQ], W[:, 0:SEQ], Dm[:, 0:SEQ], ALU.mult))
                dve.tensor_tensor(AT[0:NS, SEQ:T], W[0:NS, SEQ:T], Dm[0:NS, SEQ:T], ALU.mult).then_inc(S["dn_at"], 1)
                dve.wait_ge(S["dn_at"], h + 1)
                masked(X, AT, MT[:, 0, :], None)
                wait_chain()
                go(dve.tensor_tensor(tiles4(TT[:, 0:SEQ]), bc4(ident[:, :]), tiles4(X[:, 0:SEQ]), ALU.subtract))
                dve.tensor_tensor(TT[0:NS, SEQ:T], ident[0:NS, 0:NS], X[0:NS, SEQ:T], ALU.subtract).then_inc(S["dn_tt1"], 1)
                W = group(u, "qk")
                go(dve.tensor_tensor(QKT[:, 0:SEQ], W[:, 0:SEQ], Dm[:, 0:SEQ], ALU.mult))
                dve.tensor_tensor(QKT[0:NS, SEQ:T], W[0:NS, SEQ:T], Dm[0:NS, SEQ:T], ALU.mult).then_inc(S["dn_qkt"], 1)
                skip(u, "t1")
                W = group(u, "kt")
                by_token(bgk, W, 64 + h)
                by_token(kend, W, 96 + h, done=S["dn_kend"])
                W = group(u, "vt")
                by_token(bv, W, 32 + h, done=S["dn_bv"])
                for l in range(1, 7):
                    W = group(u, f"x{l}")
                    masked(X, W, MX[:, l, :], S["dn_x"], samples=l == 1)
                    if l < 6:
                        W = group(u, f"y{l}")
                        if l == 1:
                            dve.wait_ge(S["dn_t1"], h + 1)
                        minus(Tm, W, l == 1, S["dn_t"])
                    W = group(u, f"yt{l}")
                    minus(TT, W, l == 1, S["dn_tt"])
                skip(u, "wk")
                dve.wait_ge(S["dn_nwk"], h + 1)
                dve.tensor_tensor(mwk, nwk[:, SEQ:T].unsqueeze(1).broadcast_to([P, NB, NS]), bmask, ALU.mult)\
                   .then_inc(S["dn_mwk"], 1)
                skip(u, "u0")
                skip(u, "us")
                dve.wait_ge(S["dn_u"], 5 * h + 2)
                dve.tensor_tensor(um, uu[0:NS, SEQ:SEQ + P].unsqueeze(1).broadcast_to([NS, NB, P]),
                                  rowm.unsqueeze(2).broadcast_to([NS, NB, P]), ALU.mult).then_inc(S["dn_um"], 1)

                def s_step(t):
                    W = group(u, f"s{t}")
                    if t == 0:
                        dve.tensor_copy(SS[:, 0:P], W[:, 0:P]).then_inc(S["dn_s"], 1)
                    else:
                        dve.wait_ge(S["dn_s"], 4 * h + t)
                        dve.scalar_tensor_tensor(SS[:, P * t:P * t + P], SS[:, P * (t - 1):P * t],
                                                 eG[:, P * t + P - 1:P * t + P], W[:, 0:P], ALU.mult,
                                                 ALU.add).then_inc(S["dn_s"], 1)

                s_step(0)
                W = group(u, "ss")
                dve.wait_ge(S["dn_gs"], h + 1)
                dve.tensor_tensor(Snew, Snew, W[:, 0:1024], ALU.add).then_inc(S["dn_snew"], 1)
                ahead = h + 1 < DN_H
                if ahead:
                    dve.wait_ge(S["u_loaded"], loads["dn", h + 1])
                    dn_conv(h + 1, 0)
                for t in range(1, NT):
                    skip(u, f"u{t}")
                    s_step(t)
                    if ahead:
                        dn_conv(h + 1, t)
                if ahead:
                    dve.wait_ge(S["dn_smp"], h + 2)
                    for tap in range(TAPS):
                        dn_conv(h + 1, tap, samples=True)
                W = group(u, "o")
                dve.wait_ge(S["dn_osq"], h + 1)
                dve.wait_ge(S["dn_z"], h + 1)
                dve.scalar_tensor_tensor(slot(9), W[:, 0:T], pvc("dn_norm", 0), raws[:, 3 * T:4 * T], ALU.mult,
                                         ALU.mult).then_inc(S["dn_o1"], 1)
                skip(u, "n")
                dve.wait_ge(S["dn_rstd"], h + 1)
                dve.wait_ge(S["dn_o1"], h + 1)
                dve.tensor_tensor(slot(9), slot(9), slot(3), ALU.mult).then_inc(S["dn_y"], 1)

            def gla(h):
                u = ("gla", h)
                fill(target[u, "start"])
                free(u)
                q, k = raws[:, 0:T], raws[:, T:2 * T]
                G, eG, kf, qg, kendT, qt, kt, AT = slot(3), slot(4), slot(5), slot(6), slot(7), slot(9), slot(10), slot(11)
                vt = arena[:, 12 * T + 640:12 * T + 1920].rearrange("p (t e) -> p t e", t=NT + 1)
                SS = extra[:, 0:1024].rearrange("p (t e) -> p t e", t=NT)
                um = extra[0:NS, 1024:2048].rearrange("p (b e) -> p b e", b=4)
                W = group(u, "lg")
                dve.wait_ge(S["gl_abs"], h + 1)
                dve.tensor_scalar(slot(2), W[:, 0:T], pvc("gla_ba", h), 0.0, ALU.add, ALU.min).then_inc(S["gl_m"], 1)
                dve.wait_ge(S["gl_m"], h + 1)
                dve.wait_ge(S["gl_l"], h + 1)
                link(dve.tensor_tensor(slot(2), slot(2), slot(1), ALU.subtract))
                cumsum(P, slot(2), G, None).then_inc(S["gl_G"], 1)
                dve.wait_ge(S["gl_G"], h + 1)
                to_chunk_end(P, kf, G, S["gl_kd"])

                def exponents(l):
                    s = 1 << l
                    E = slot((8, 2)[l % 2])
                    w = T if l < 2 else SEQ
                    g = G[:, 0:w].rearrange("p (n i) -> p n i", i=2 * s)
                    e = E[:, 0:w].rearrange("p (n i) -> p n i", i=2 * s)
                    ref = g[:, :, s - 1:s].broadcast_to([P, w // (2 * s), s])
                    go(dve.tensor_tensor(e[:, :, 0:s], ref, g[:, :, 0:s], ALU.subtract))
                    if l >= 2:
                        dve.tensor_tensor(e[:, :, s:], g[:, :, s:], ref, ALU.subtract).then_inc(S["gl_ed"], 1)
                    else:
                        dve.tensor_tensor(e[:, :, s:], g[:, :, s:], ref, ALU.subtract).then_inc(S["gl_ed"], 1)

                exponents(0)
                dve.wait_ge(S["gl_q"], h + 1)
                dve.wait_ge(S["gl_eg"], h + 1)
                go(dve.tensor_tensor(qg, q, eG, ALU.mult))
                dve.wait_ge(S["gl_kf"], h + 1)
                dve.tensor_tensor(kendT, k, kf, ALU.mult).then_inc(S["gl_qg"], 1)
                W = group(u, "qk")
                masked(AT, W, ident[:, :], S["gl_at"])
                for l in range(7):
                    if l < 6:
                        exponents(l + 1)
                    s = 1 << l
                    w = T if l < 2 else SEQ
                    E = slot((8, 2)[l % 2])
                    dve.wait_ge(S["gl_E"], 7 * h + l + 1)

                    def part(ap, lo):
                        return ap[:, 0:w].rearrange("p (n i) -> p n i", i=2 * s)[:, :, lo:lo + s]
                    go(dve.tensor_tensor(part(qt, s), part(q, s), part(E, s), ALU.mult))
                    dve.tensor_tensor(part(kt, 0), part(k, 0), part(E, 0), ALU.mult).then_inc(S["gl_qkt"], 1)
                    W = group(u, f"l{l}")
                    dve.wait_ge(S["gl_at"], 8 * h + l + 1)
                    if l < 2:
                        go(dve.copy_predicated(AT[0:NS, SEQ:T], MT[0:NS, l, 0:NS].bitcast(U16), W[0:NS, SEQ:T]))
                    dve.copy_predicated(tiles4(AT[:, 0:SEQ]), bc4(MT[:, l, :].bitcast(U16)), tiles4(W[:, 0:SEQ]))\
                       .then_inc(S["gl_at"], 1)
                for n in ("kt", "v0", "v1"):
                    skip(u, n)
                W = group(u, "sA")
                link(dve.tensor_copy(SS[:, 0, :], W[:, 0:256]))
                for t in range(1, NT):
                    ins = dve.scalar_tensor_tensor(SS[:, t, :], SS[:, t - 1, :], eG[:, P * t + P - 1:P * t + P],
                                                   W[:, 256 * t:256 * t + 256], ALU.mult, ALU.add)
                    if t < NT - 1:
                        link(ins)
                    else:
                        ins.then_inc(S["gl_s"], 1)

                def mask_v(i):
                    dve.wait_ge(S["gl_v"], 2 * h + 2)
                    dve.tensor_tensor(um, vt[0:NS, NT, :].unsqueeze(1).broadcast_to([NS, 4, 256]),
                                      rowm[:, 4 * i:4 * i + 4].unsqueeze(2).broadcast_to([NS, 4, 256]),
                                      ALU.mult).then_inc(S["gl_um"], 1)

                mask_v(0)
                for e in range(2):
                    W = group(u, f"o{e}")
                    dve.wait_ge(S["gl_osq"], 2 * h + e + 1)
                    dve.scalar_tensor_tensor(slot(e), W[:, 0:T], pvc("gla_norm", e), raws[:, T * (4 + e):T * (5 + e)],
                                             ALU.mult, ALU.mult).then_inc(S["gl_o1"], 1)
                for i in range(2):
                    W = group(u, f"sb{i}")
                    if i == 0:
                        dve.wait_ge(S["gl_gs"], h + 1)
                    if i == 0:
                        mask_v(1)
                    half = sbuf[:, 1024 * i:1024 * i + 1024]
                    dve.tensor_tensor(half, half, W[:, 0:1024], ALU.add).then_inc(S["gl_snew"], 1)
                skip(u, "n")
                dve.wait_ge(S["gl_rstd"], h + 1)
                dve.wait_ge(S["gl_o1"], 2 * h + 2)
                dve.tensor_tensor(slot(9, 2).rearrange("p (e t) -> p e t", e=2), slot(0, 2).rearrange("p (e t) -> p e t", e=2),
                                  slot(2).unsqueeze(1).broadcast_to([P, 2, T]), ALU.mult).then_inc(S["gl_y"], 1)

            def bc():
                u = ("bc", 0)
                fill(target[u, "start"])
                dve.wait_ge(S["u_loaded"], loads[u])
                dve.wait_ge(S["rows_copied"], 3)
                conv(4, lambda i, w: pvc("ssd_conv_w", 12 * w + 8 + i), lambda i: pvc("ssd_conv_b", 8 + i), slot,
                     S["bc_smp"], 1, S["bc_conv"])
                for n in ("bt", "bts", "cb0", "cb1", "cb2", "cb3"):
                    skip(u, n)
                link(dve.memset(arena[:, 8000:8000 + P], 0.0))

            def ssd(p):
                u = ("ssd", p)
                if p == 0:
                    fill(target[u, "start"])
                    free(u)
                g, e2 = p // 2, p % 2
                pb = SSD_N * (g % 2)
                hp = slice(pb, pb + SSD_N)
                xs, ebc = ssd_x(p), arena[:, 6176:6176 + T]
                v, v2, SS = arena[:, 6720:7360], arena[:, 7360:8000], arena[:, 8000:8640]
                um = extra[0:NS, 0:1024].rearrange("p (b e) -> p b e", b=NB)
                y = extra[:, 1024 + T * e2:1024 + T * (e2 + 1)]
                t1 = raws[:, 4 * T:5 * T]
                for n in ((0, 1) if p == 0 else (p + 1,)):
                    if n < SSD_H // 2:
                        dve.wait_ge(S["u_loaded"], loads["ssd", n])
                        if n > 1:
                            dve.wait_ge(S["sp_y"], n - 1)
                        conv(1, lambda i, w: pvc("ssd_conv_w", 12 * w + n), lambda i: pvc("ssd_conv_b", n),
                             lambda i: ssd_x(n), S["sp_smp"], n + 1, S["sp_conv"])
                for n in ("dmA", "dmB", "ebc"):
                    skip(u, n)
                dve.wait_ge(S["bc_cb"], 4)
                dve.wait_ge(S["sp_D"], 2 * p + 2)
                for e in range(2):
                    go(dve.tensor_tensor(slot(e)[:, 0:SEQ], slot(e)[:, 0:SEQ], slot(4 + g)[:, 0:SEQ], ALU.mult))
                    ins = dve.tensor_tensor(slot(e)[0:NS, SEQ:T], slot(e)[0:NS, SEQ:T], slot(4 + g)[0:NS, SEQ:T], ALU.mult)
                    if e:
                        ins.then_inc(S["sp_A"], 1)
                    else:
                        go(ins)
                W = group(u, "xt")
                free(u)
                by_token(v, W, 32 + 2 * p, nh=2)
                by_token(v2, W, 64 + 2 * p, nh=2, done=S["sp_v"])
                dve.wait_ge(S["sp_v"], p + 1)
                dve.tensor_tensor(um, v2[0:NS, SEQ:SEQ + P].unsqueeze(1).broadcast_to([NS, NB, P]),
                                  rowm.unsqueeze(2).broadcast_to([NS, NB, P]), ALU.mult).then_inc(S["sp_um"], 1)
                W = group(u, "sP")
                eg = egt[hp, 24 * p:24 * p + 24].rearrange("p (h c) -> p h c", h=2)
                for t in range(NT):
                    a = SS[hp, P * t:P * t + P].rearrange("p (h e) -> p h e", h=2)
                    b = SS[hp, P * t + P:P * t + 2 * P].rearrange("p (h e) -> p h e", h=2)
                    link(dve.tensor_tensor(b, a, eg[:, :, t:t + 1].broadcast_to([SSD_N, 2, SSD_N]), ALU.mult))
                    ins = dve.tensor_tensor(SS[hp, P * t + P:P * t + 2 * P], SS[hp, P * t + P:P * t + 2 * P],
                                            W[hp, P * t:P * t + P], ALU.add)
                    if t < NT - 1:
                        link(ins)
                    else:
                        ins.then_inc(S["sp_s"], 1)
                W = group(u, "ss")
                dve.wait_ge(S["sp_gs"], p + 1)
                dve.tensor_tensor(sbuf[hp, 1024:2048], sbuf[hp, 1024:2048], W[hp, 0:1024], ALU.add).then_inc(S["sp_snew"], 1)
                W = group(u, "i")
                dve.wait_ge(S["sp_ebc"], p + 1)
                dve.tensor_tensor(t1, W[:, 0:T], ebc, ALU.mult).then_inc(S["sp_i"], 1)
                dve.wait_ge(S["sp_i"], p + 1)
                W = group(u, "o")
                dve.tensor_tensor(t1, W[:, 0:T], t1, ALU.add).then_inc(S["sp_o"], 1)
                dve.wait_ge(S["sp_o"], p + 1)
                link(dve.scalar_tensor_tensor(t1, xs, egt[:, SSD_H * 12 + p:SSD_H * 12 + p + 1], t1, ALU.mult, ALU.add))
                dve.wait_ge(S["sp_z"], p + 1)
                dve.tensor_tensor(y, t1, raws[:, T:2 * T], ALU.mult).then_inc(S["sp_y"], 1)
                if e2:
                    skip(u, "n")
                    dve.wait_ge(S["sp_rstd"], p // 2 + 1)
                    dve.wait_ge(S["sp_y"], p + 1)
                    for e in range(2):
                        ye = extra[:, 1024 + T * e:1024 + T * (e + 1)]
                        ins = dve.scalar_tensor_tensor(ye, ye, pvc("ssd_norm", p - 1 + e), raws[:, 5 * T:6 * T], ALU.mult,
                                                       ALU.mult)
                        if e:
                            ins.then_inc(S["sp_out"], 1)
                        else:
                            go(ins)

            def lru(j):
                u = ("lru", j)
                if j == 0:
                    fill(target[u, "start"])
                    free(u)
                for n in ((0, 1) if j == 0 else (j + 1,)):
                    if n < LRU_W // P:
                        dve.wait_ge(S["u_loaded"], loads["lru", n])
                        conv(1, lambda i, w: pvc("lru_conv_w", 8 * w + n), lambda i: pvc("lru_conv_b", n),
                             lambda i: lru_slot(n, 0), S["lr_smp"], n + 1, S["lr_conv"], src=2 * (n % 2))
                skip(u, "r")
                skip(u, "i")
                if j:
                    free(("lru", j - 1))
                xc, y, ig, a, th, b, hs = (lru_slot(j, i) for i in range(7))
                dve.wait_ge(S["lr_a"], j + 1)
                go(dve.tensor_tensor(ig, ig, xc, ALU.mult))
                link(dve.tensor_tensor(b, a, a, ALU.mult))
                link(dve.scalar_tensor_tensor(b, b, 1.0, th, ALU.add, ALU.mult))
                dve.tensor_scalar(b, b, 1e-30, None, ALU.max).then_inc(S["lr_t"], 1)
                starts = a[:, SEQ:T].rearrange("p (b i) -> p b i", b=NB)[:, :, 0]
                bs = b[:, SEQ:T].rearrange("p (b i) -> p b i", b=NB)[:, :, 0]
                link(dve.tensor_tensor(small[:, 32:40], starts, hist[:, 36 + j, 24:32], ALU.mult))
                go(dve.memset(a[:, 0:1], 0.0))
                go(dve.memset(starts, 0.0))
                dve.wait_ge(S["lr_sq"], j + 1)
                link(dve.tensor_tensor(b, b, ig, ALU.mult))
                link(dve.tensor_tensor(bs, bs, small[:, 32:40], ALU.add))
                dve.tensor_tensor_scan(hs, a, b, 0.0, ALU.mult, ALU.add).then_inc(S["lr_hs"], 1)
                dve.wait_ge(S["lr_hs"], j + 1)
                dve.wait_ge(S["lr_z"], j + 1)
                dve.tensor_tensor(y, hs, raws[:, T:2 * T], ALU.mult).then_inc(S["lr_y"], 1)

            def y_split(layer):
                for c in range(0, KT, 2):
                    dve.wait_ge(S["nrm_y"], KT * layer + c + 1)
                    dve.tensor_tensor(xl[:, c, :], hT(c), xh[:, c, :].bitcast(F32), ALU.subtract).then_inc(S["x_ready0"], 1)

            def out_proj(layer):
                for c in range(KT):
                    d = first[f"out{layer}"] + c
                    fill(SL * (d + 1))
                    dve.wait_ge(S["slice_done"], SL * (d + 1))
                    dve.wait_ge(S["h_loaded"], 16 * (layer + 1))
                    dve.tensor_tensor(hT(c), hT(c), psd[d % 2][:, D0:D0 + T], ALU.add)\
                       .then_inc(S[f"dense_read{d % 2}"], 1)

            def gate(layer):
                u = ("gate", layer)
                for c in range(KT):
                    d = first[f"gate{layer}"] + c
                    fill(SL * (d + 1))
                    W = group(u, f"g{c}")
                    dve.wait_ge(S[f"dense_read{d % 2}"], d // 2 + 1)
                    e = extra[:, T * (c % 2):T * (c % 2) + T]
                    dve.tensor_tensor(e, e, W[:, 0:T], ALU.mult).then_inc(S["gate_read"], 1)
                    dve.wait_ge(S["gate_read"], KT * layer + c + 1)
                    dve.tensor_tensor(hT(c), hT(c), e, ALU.add).then_inc(S["gate_done"], 1)

            dve.memset(ones[:, :], 1.0)
            dve.memset(cst[:, 0:1], EPS)
            dve.memset(cst[:, 1:2], 1.0).then_inc(S["consts_set"], 1)
            split_lo(0)
            split_lo(1)
            dve.wait_ge(S["rows_act"], 1)
            lam = pvc("lru_lambda", 0, 8)
            link(dve.tensor_scalar(small[:, 56:64], lam, -1.0, 0.0, ALU.mult, ALU.max))
            link(dve.tensor_tensor(small[:, 56:64], small[:, 56:64], small[:, 48:56], ALU.add))
            link(dve.tensor_scalar(small[:, 56:64], small[:, 56:64], 8.0, None, ALU.mult))
            link(dve.tensor_scalar(small[:, 48:56], small[:, 56:64], -1.0, None, ALU.mult))
            norm(0)
            for u in UNITS:
                if u[0] == "ab_rows":
                    rows_ab()
                    fill(SL + 2)
                    skip(u, "c0")
                elif u[0] == "dn":
                    dn(u[1])
                elif u[0] == "gla":
                    gla(u[1])
                else:
                    fill(end_slice("ab"))
            y_split(0)
            out_proj(0)
            norm(1)
            gate(0)
            norm(2)
            for u in UNITS_CD:
                if u[0] == "cd_rows":
                    rows_cd()
                    fill(first_slice("cd") + SL + 2)
                    skip(u, "eg")
                    skip(u, "c0")
                elif u[0] == "bc":
                    bc()
                elif u[0] == "ssd":
                    ssd(u[1])
                elif u[0] == "lru":
                    lru(u[1])
                else:
                    fill(end_slice("cd"))
            y_split(1)
            out_proj(1)
            norm(3)
            gate(1)
            norm(4, final=True)

        @block.gpsimd
        def _(pool):
            chained = [0]

            def link(ins):
                chained[0] += 1
                ins.then_inc(S["pool_chain"], 1)
                pool.wait_ge(S["pool_chain"], chained[0])

            def load_raws(u, z=False):
                d0, n = RAW[u]
                at = 0
                if u in zloads:
                    d0, n, at = (d0 + n - 1, 1, n - 1) if z else (d0, n - 1, 0)
                if u[0] == "lru" and not z:
                    at = 2 * (u[1] % 2)
                for e in range(2):
                    last = [staged[d][2] for d in range(d0, d0 + n) if staged[d][1] == e]
                    if last:
                        pool.wait_ge(S[f"stage_stored{e}"], last[-1])
                i = staged[d0][0]
                pool.dma_start(raws[:, at * T:(at + n) * T].rearrange("p (i t) -> p i t", i=n),
                               uT[i:i + n].rearrange("i p t -> p i t")).then_inc(S["z_loaded" if z else "u_loaded"], 16)

            def sample_rows(u, n, tile, done, src=0):
                pool.wait_ge(S["u_loaded"], loads[u])
                for i in range(n):
                    x = raws[:, T * (src + i):T * (src + i) + T]
                    h3 = hist[:, tile(i), 0:24].rearrange("p (b r) -> p b r", b=NB)
                    link(pool.tensor_copy(smp[:, i, :, 0:TAPS - 1], h3))
                    ins = pool.tensor_copy(smp[:, i, :, TAPS - 1:], x[:, SEQ:T].rearrange("p (b s) -> p b s", b=NB))
                    if i == n - 1:
                        ins.then_inc(done, 1)
                    else:
                        link(ins)
                for i in range(n):
                    x = raws[:, T * i:T * i + T]
                    if tile(i) < 36:
                        tails(x, tile(i))

            def tails(x, tile):
                link(pool.tensor_copy(hist[:, tile, 0:3], x[:, SEQ - 3:SEQ]))
                link(pool.tensor_copy(hist[:, tile, 3:27].rearrange("p (b r) -> p b r", b=NB),
                                      x[:, SEQ:T].rearrange("p (b s) -> p b s", b=NB)[:, :, 1:]))

            pool.memset(small[:, :], 0.0)
            pool.memset(hist[:, :, :], 0.0).then_inc(S["zeroed"], 1)
            pool.wait_ge(S["zeroed"], 1)
            pool.dma_start(cb16[:, :], I["cb"]).then_inc(S["masks_loaded"], 16)
            prow = slot(0)
            for name, (col, row, n) in PARAM_ROWS.items():
                pool.dma_start(prow[row:row + n, P * col:P * col + P], as_rows(I[name])).then_inc(S["params_loaded"], 16)
            hrow = arena[:, T:]
            pool.dma_start(hrow[0:24, 0:3072], I["state_dn_conv"][0].rearrange("b r c -> (b r) c")).then_inc(S["params_loaded"], 16)
            pool.dma_start(hrow[0:24, 3072:4608], I["state_ssd_conv"][0].rearrange("b r c -> (b r) c")).then_inc(S["params_loaded"], 16)
            pool.dma_start(hrow[0:24, 4608:5632], I["state_lru_conv"][0].rearrange("b r c -> (b r) c")).then_inc(S["params_loaded"], 16)
            pool.dma_start(hrow[24:32, 4608:5632], I["state_lru"][0]).then_inc(S["params_loaded"], 16)
            pool.dma_start(small[0:DN_H, 0:1], I["dn_dt_bias"].rearrange("a h -> h a"), allow_slow_non_contiguous=True).then_inc(S["rows_loaded"], 16)
            pool.dma_start(small[0:DN_H, 1:2], I["dn_a_log"].rearrange("a h -> h a"), allow_slow_non_contiguous=True).then_inc(S["rows_loaded"], 16)
            pool.dma_start(small[0:SSD_H, 10:11], I["ssd_dt_bias"].rearrange("a h -> h a"), allow_slow_non_contiguous=True).then_inc(S["rows_loaded"], 16)
            pool.dma_start(small[0:SSD_H, 11:12], I["ssd_a_log"].rearrange("a h -> h a"), allow_slow_non_contiguous=True).then_inc(S["rows_loaded"], 16)
            for e in range(2):
                pool.dma_start(egt[64 * e:64 * e + 64, SSD_H * 12:SSD_H * 12 + 8],
                               I["ssd_d"].rearrange("a (p e) -> e a p", e=2)[e].partition_broadcast(64), allow_slow_non_contiguous=True)\
                    .then_inc(S["rows_loaded"], 16)
            pool.dma_start(wa2[64:64 + GLA_R, :], I["gla_wa2"][0]).then_inc(S["rows_loaded"], 16)
            for t in range(NT + 1):
                _, n = tok(t)
                dst = raws if t % 2 == 0 else sbuf
                if t >= 2:
                    pool.wait_ge(S["in_copied"], 3 + 2 * (t - 1))
                src = I["x_prompt"][0, P * t:P * t + P] if t < NT else I["x_sample"].rearrange("b s d -> (b s) d")
                pool.dma_start(dst[0:n, 0:D_MODEL], src).then_inc(S[f"x_loaded{t % 2}"], 16)
            arena3 = arena[:, :].rearrange("p (c t) -> p c t", c=KT)

            def add_square(i, c):
                acc = sbuf[:, T:2 * T]
                pool.wait_ge(S["nrm_sq"], KT * i + c + 1)
                if c > 1:
                    pool.wait_ge(S["sq_summed"], (KT - 2) * i + c - 1)
                pool.tensor_tensor(acc, acc, extra[:, T * (2 + c % 2):T * (3 + c % 2)], ALU.add)\
                    .then_inc(S["sq_summed"] if c < KT - 1 else S["sq_added"], 1)

            def norm(i):
                if i % 2 or i == 0:
                    for c in range(1, KT):
                        add_square(i, c)
                for c in range(1, KT, 2):
                    pool.wait_ge(S["nrm_hi"], KT * i + c + 1)
                    pool.tensor_tensor(xl[:, c, :], extra[:, T * (2 + c % 2):T * (3 + c % 2)], xh[:, c, :].bitcast(F32),
                                       ALU.subtract).then_inc(S["x_ready1"], 1)

            def store_h(i):
                pool.wait_ge(S["x_ready0"], KH * (1 if i == 0 else 4))
                pool.dma_start(hD.rearrange("c p t -> p c t"), arena3).then_inc(S["h_stored"], 16)

            def mix_to_out(layer, units):
                pool.wait_ge(S["out_stored"], stored[UNITS_CD[0]] if layer == 0 else stored["end"])
                pool.dma_start(arena3, yT.rearrange("c p t -> p c t")).then_inc(S["y_loaded"], 16)
                for c in range(1, KT, 2):
                    pool.wait_ge(S["nrm_y"], KT * layer + c + 1)
                    pool.tensor_tensor(xl[:, c, :], hT(c), xh[:, c, :].bitcast(F32), ALU.subtract).then_inc(S["x_ready1"], 1)
                for i in range(2):
                    pool.wait_ge(S[f"x_ready{i}"], KH * (2 if layer == 0 else 5))
                pool.dma_start(arena3, hD.rearrange("c p t -> p c t")).then_inc(S["h_loaded"], 16)

            def load_p(layer):
                ptok = raws[:, 0:1280].rearrange("p (t c) -> p t c", t=NT + 1)
                wp = raws[:, 2368:2880].rearrange("p (s k n) -> p s k n", s=2, k=2)
                pool.dma_start(ptok[:, 0:NT, :], I["p_prompt"][layer, 0].rearrange("(t p) c -> p t c", p=P))\
                    .then_inc(S["p_loaded"], 16)
                pool.dma_start(ptok[0:NS, NT, :], I["p_sample"][layer].rearrange("b s c -> (b s) c")).then_inc(S["p_loaded"], 16)
                for c in range(KT):
                    if c >= 2:
                        pool.wait_ge(S["gate_read"], KT * layer + c - 1)
                    pool.dma_start(wp[:, c % 2], I["ple_w_proj"][layer, :, P * c:P * c + P]
                                   .rearrange("(k p) n -> p k n", p=P)).then_inc(S[f"wp_loaded{c % 2}"], 16)
                    if c >= 3:
                        add_square(2 * layer + 2, c - 2)
                for c in range(KT - 2, KT):
                    add_square(2 * layer + 2, c)

            def dn(h):
                u = ("dn", h)
                load_raws(u, z=True)
                if h == 0:
                    load_raws(u)
                    sample_rows(u, 3, lambda i: 8 * i + h, S["dn_smp"])
                pool.wait_ge(S["out_stored"], stored[u])
                pool.dma_start(sbuf[:, 0:1024].rearrange("p (b e) -> p b e", b=NB),
                               I["state_dn"][0, :, h].rearrange("b d e -> d b e")).then_inc(S["s_loaded"], 16)
                pool.wait_ge(S["s_loaded"], sloads[u])
                pool.wait_ge(S["dn_eg"], h + 1)
                ge = slot(5)[:, SEQ:T].rearrange("p (b i) -> p b i", b=NB)[:, :, LS - 1:LS].broadcast_to([P, NB, P])
                pool.tensor_tensor(sbuf[:, 1024:2048].rearrange("p (b e) -> p b e", b=NB),
                                   sbuf[:, 0:1024].rearrange("p (b e) -> p b e", b=NB), ge, ALU.mult).then_inc(S["dn_gs"], 1)
                if h + 1 < DN_H:
                    load_raws(("dn", h + 1))
                    sample_rows(("dn", h + 1), 3, lambda i: 8 * i + h + 1, S["dn_smp"])
                pool.wait_ge(S["dn_snew"], h + 1)
                pool.dma_start(O["dn_s"][0, :, h].rearrange("b d e -> d b e"),
                               sbuf[:, 1024:2048].rearrange("p (b e) -> p b e", b=NB)).then_inc(S["out_stored"], 16)
                pool.wait_ge(S["dn_s"], 4 * h + 4)
                pool.dma_start(O["dn_p"][0, 0, h], extra[:, 640 + 384:640 + 512]).then_inc(S["out_stored"], 16)
                pool.wait_ge(S["dn_y"], h + 1)
                pool.dma_start(yT[h], slot(9)).then_inc(S["out_stored"], 16)

            def gla(h):
                u = ("gla", h)
                pool.wait_ge(S["out_stored"], stored[u])
                load_raws(u)
                Sb = sbuf[:, :].rearrange("p (b e) -> p b e", b=NB)
                pool.dma_start(Sb, I["state_gla"][0, :, h].rearrange("b d e -> d b e")).then_inc(S["s_loaded"], 16)
                pool.wait_ge(S["s_loaded"], sloads[u])
                pool.wait_ge(S["gl_eg"], h + 1)
                pool.wait_ge(S["work_ready"], NO[u, "o1"] + 1)
                ge = slot(4)[:, SEQ:T].rearrange("p (b i) -> p b i", b=NB)[:, :, LS - 1:LS].broadcast_to([P, NB, 256])
                pool.tensor_tensor(Sb, Sb, ge, ALU.mult).then_inc(S["gl_gs"], 1)
                pool.wait_ge(S["gl_snew"], 2 * h + 2)
                pool.dma_start(O["gla_s"][0, :, h].rearrange("b d e -> d b e"), Sb).then_inc(S["out_stored"], 16)
                pool.dma_start(O["gla_p"][0, 0, h], extra[:, 768:1024]).then_inc(S["out_stored"], 16)
                pool.wait_ge(S["gl_y"], h + 1)
                pool.dma_start(yT[8 + 2 * h:10 + 2 * h].rearrange("c p t -> p c t"),
                               slot(9, 2).rearrange("p (c t) -> p c t", c=2)).then_inc(S["out_stored"], 16)

            def ssd(p):
                u = ("ssd", p)
                pb = SSD_N * (p // 2 % 2)
                hp = slice(pb, pb + SSD_N)
                pool.wait_ge(S["out_stored"], stored[u])
                if p:
                    pool.wait_ge(S["sp_y"], p)
                else:
                    pool.wait_ge(S["bc_conv"], 1)
                    load_raws(u)
                    sample_rows(u, 1, lambda i: 24, S["sp_smp"])
                load_raws(u, z=True)
                pool.tensor_copy(selp[0:SSD_H, :].rearrange("p (h e) -> p h e", h=2),
                                 ident[0:SSD_H, 2 * p:2 * p + 2].unsqueeze(2).broadcast_to([SSD_H, 2, SSD_N]))\
                    .then_inc(S["sp_sel"], 1)
                Sin = sbuf[hp, 0:1024].rearrange("p (b h e) -> p b h e", b=NB, h=2)
                for i in range(2):
                    pool.dma_start(Sin[:, :, i, :], I["state_ssd"][0, :, 2 * p + i].rearrange("b n e -> n b e"))\
                        .then_inc(S["s_loaded"], 16)
                if p + 1 < SSD_H // 2:
                    pool.wait_ge(S["sp_conv"], p + 1)
                    load_raws(("ssd", p + 1))
                    sample_rows(("ssd", p + 1), 1, lambda i: 24 + p + 1, S["sp_smp"])
                pool.wait_ge(S["s_loaded"], sloads[u])
                Sn = sbuf[hp, 1024:2048].rearrange("p (b h e) -> p b h e", b=NB, h=2)
                for i in range(2):
                    eg = egt[hp, 12 * (2 * p + i) + 4:12 * (2 * p + i) + 12].unsqueeze(2).broadcast_to([SSD_N, NB, SSD_N])
                    ins = pool.tensor_tensor(Sn[:, :, i, :], Sin[:, :, i, :], eg, ALU.mult)
                    if i:
                        ins.then_inc(S["sp_gs"], 1)
                    else:
                        link(ins)
                pool.wait_ge(S["sp_snew"], p + 1)
                for i in range(2):
                    pool.dma_start(O["ssd_s"][0, :, 2 * p + i].rearrange("b n e -> n b e"), Sn[:, :, i, :])\
                        .then_inc(S["ssd_stored"], 16)
                pool.wait_ge(S["sp_s"], p + 1)
                pool.dma_start(O["ssd_p"][0, 0, 2 * p:2 * p + 2].rearrange("h n e -> n h e"),
                               arena[hp, 8000 + 512:8000 + 640].rearrange("p (h e) -> p h e", h=2)).then_inc(S["out_stored"], 16)
                pool.wait_ge(S["ssd_stored"], 32 * (p + 1))
                if p % 2:
                    pool.wait_ge(S["sp_out"], p // 2 + 1)
                    pool.dma_start(yT[p - 1:p + 1].rearrange("c p t -> p c t"),
                                   extra[:, 1024:1024 + 2 * T].rearrange("p (c t) -> p c t", c=2)).then_inc(S["out_stored"], 16)

            def load_blocks(j):
                bd = sbuf[:, 256 * (j % 2):256 * (j % 2) + 256].rearrange("p (i n) -> p i n", i=2)
                for i, name in enumerate(("lru_wa", "lru_wx")):
                    for b in range(2):
                        pool.dma_start(bd[64 * b:64 * b + 64, i, 64 * b:64 * b + 64], I[name][0, 2 * j + b])\
                            .then_inc(S["s_loaded"], 16)

            def lru(j):
                u = ("lru", j)
                if j == 0:
                    load_raws(u)
                    load_blocks(0)
                    sample_rows(u, 1, lambda i: 36, S["lr_smp"])
                else:
                    pool.wait_ge(S["lr_y"], j)
                load_raws(u, z=True)
                if j + 1 < LRU_W // P:
                    pool.wait_ge(S["lr_conv"], j + 1)
                    load_raws(("lru", j + 1))
                    sample_rows(("lru", j + 1), 1, lambda i: 36 + j + 1, S["lr_smp"], src=2 * ((j + 1) % 2))
                    pool.wait_ge(S["lr_r"], j + 1)
                    load_blocks(j + 1)
                pool.wait_ge(S["lr_y"], j + 1)
                x, hs = raws[:, 2 * T * (j % 2):2 * T * (j % 2) + T], lru_slot(j, 6)
                tails(x, 36 + j)
                link(pool.tensor_copy(hist[:, 36 + j, 27:28], hs[:, SEQ - 1:SEQ]))
                link(pool.tensor_copy(hist[:, 36 + j, 28:36], hs[:, SEQ:T].rearrange("p (b i) -> p b i", b=NB)[:, :, LS - 1]))
                pool.dma_start(yT[8 + j], lru_slot(j, 1)).then_inc(S["out_stored"], 16)

            norm(0)
            store_h(0)
            for u in UNITS:
                if u[0] == "dn":
                    dn(u[1])
                elif u[0] == "gla":
                    gla(u[1])
                elif u[0] == "ab_tail":
                    pool.memset(small[0:1, 42:43], 0.0).then_inc(S["tail_made"], 1)
                    for n in range(3):
                        pool.wait_ge(S["tail_copied"], n + 1)
                        cs = slice(1024 * n, 1024 * n + 1024)
                        pool.dma_start(O["dnc_p"][0, 0, :, cs], raws[0:3, cs]).then_inc(S["out_stored"], 16)
                        pool.dma_start(O["dnc_s"][0].rearrange("b r c -> (b r) c")[:, cs], raws[3:27, cs])\
                            .then_inc(S["out_stored"], 16)
            mix_to_out(0, UNITS)
            norm(1)
            load_p(0)
            norm(2)
            store_h(1)
            for u in UNITS_CD:
                if u[0] == "bc":
                    pool.wait_ge(S["gate_done"], KT)
                    load_raws(u)
                    sample_rows(u, 4, lambda i: 32 + i, S["bc_smp"])
                elif u[0] == "ssd":
                    ssd(u[1])
                elif u[0] == "lru":
                    if u[1] == 0:
                        pool.wait_ge(S["out_stored"], stored[u])
                        link(pool.memset(sbuf[:, 0:512], 0.0))
                    lru(u[1])
                elif u[0] == "cd_tail":
                    pool.memset(small[0:1, 42:43], 0.0).then_inc(S["tail_made"], 1)
                    pool.wait_ge(S["tail_copied"], 6)
                    c_p, c_s = O["ssdc_p"][0, 0], O["ssdc_s"][0].rearrange("b r c -> (b r) c")
                    pool.dma_start(c_p, raws[0:3, 0:SSD_XBC]).then_inc(S["out_stored"], 16)
                    pool.dma_start(c_s, raws[3:27, 0:SSD_XBC]).then_inc(S["out_stored"], 16)
                    l0 = 2048
                    pool.dma_start(O["lruc_p"][0, 0], raws[0:3, l0:l0 + LRU_W]).then_inc(S["out_stored"], 16)
                    pool.dma_start(O["lruc_s"][0].rearrange("b r c -> (b r) c"), raws[3:27, l0:l0 + LRU_W])\
                        .then_inc(S["out_stored"], 16)
                    pool.dma_start(O["lru_p"][0], raws[27:28, l0:l0 + LRU_W]).then_inc(S["out_stored"], 16)
                    pool.dma_start(O["lru_s"][0], raws[28:36, l0:l0 + LRU_W]).then_inc(S["out_stored"], 16)
            mix_to_out(1, UNITS_CD)
            norm(3)
            load_p(1)
            for t in range(NT + 1):
                _, n = tok(t)
                src = raws if t % 2 == 0 else sbuf
                pool.wait_ge(S["out_copied"], 2 * t + 2)
                dst = O["y_p"][0, P * t:P * t + P] if t < NT else O["y_s"].rearrange("b s d -> (b s) d")
                pool.dma_start(dst, src[0:n, 0:D_MODEL]).then_inc(S[f"y_stored{t % 2}"], 16)
            pool.wait_ge(S["y_stored0"], 48)
            pool.wait_ge(S["y_stored1"], 32)
            pool.wait_ge(S["h_stored"], 32)


_INS = ["x_prompt", "x_sample", "state_dn", "state_dn_conv", "state_gla", "state_ssd", "state_ssd_conv", "state_lru",
        "state_lru_conv", "p_prompt", "p_sample", "norm_g", "final_norm", "ab_w_in", "dn_conv_w", "dn_a_log",
        "dn_dt_bias", "dn_norm", "gla_wa2", "gla_ba", "gla_norm", "ab_w_out", "cd_w_in", "ssd_conv_w", "ssd_conv_b",
        "ssd_a_log", "ssd_dt_bias", "ssd_d", "ssd_norm", "lru_conv_w", "lru_conv_b", "lru_wa", "lru_ba", "lru_wx",
        "lru_bx", "lru_lambda", "cd_w_out", "ple_w_proj", "ple_norm", "ple_w_gate"]
_OUTS = [("y_p", (1, SEQ, D_MODEL)), ("y_s", (NB, LS, D_MODEL)),
         ("dn_p", (1, 1, 8, 128, 128)), ("dnc_p", (1, 1, 3, 3072)), ("gla_p", (1, 1, 4, 128, 256)),
         ("ssd_p", (1, 1, 16, 64, 64)), ("ssdc_p", (1, 1, 3, 1536)), ("lru_p", (1, 1, 1024)),
         ("lruc_p", (1, 1, 3, 1024)),
         ("dn_s", (1, NB, 8, 128, 128)), ("dnc_s", (1, NB, 3, 3072)), ("gla_s", (1, NB, 4, 128, 256)),
         ("ssd_s", (1, NB, 16, 64, 64)), ("ssdc_s", (1, NB, 3, 1536)), ("lru_s", (1, NB, 1024)),
         ("lruc_s", (1, NB, 3, 1024))]


def _constants():
    import numpy as np

    r = np.arange(P)
    i, j = r[:, None], r[None, :]
    lower = []
    for l in range(7):
        s = 1 << l
        lower.append((i // (2 * s) == j // (2 * s)) & (i % (2 * s) >= s) & (j % (2 * s) < s))
    mx = np.stack(lower, 1).astype(np.float32).reshape(P, -1)
    mt = np.stack([m.T for m in lower], 1).astype(np.float32).reshape(P, -1)
    negm = np.where(j < i, -1e30, 0.0)
    s = np.arange(NS)
    negs = np.zeros((P, NS))
    negs[:NS] = np.where((s[None] < s[:, None]) | (s[None] // LS != s[:, None] // LS), -1e30, 0.0)
    tt = np.arange(T)
    starts = np.where(tt < SEQ, tt % P == 0, (tt - SEQ) % LS == 0)
    rmask = np.broadcast_to(np.where(starts, 0.0, 1.0), (P, T))
    bmask = np.broadcast_to((s[None] // LS == np.arange(NB)[:, None]).reshape(1, -1), (P, NB * NS))
    rowm = np.zeros((P, NB))
    rowm[:NS] = s[:, None] // LS == np.arange(NB)[None]
    parts = [mx, mt, np.eye(P), negm, negs, rmask, bmask, rowm]
    cb = np.concatenate([np.asarray(x, np.float32) for x in parts], 1)
    return {"cf": np.eye(P, dtype=np.float32), "cb": cb}


def kernel(**inputs):
    import numpy as _np
    import concourse.bacc as _bacc
    from concourse import mybir as _mybir
    from concourse.bass_utils import run_bass_kernel_spmd as _run

    nc = _bacc.Bacc("TRN2", target_bir_lowering=False, num_devices=1)
    arrays, I, O = {}, {}, {}
    given = {name: _np.ascontiguousarray(inputs[name]) for name in _INS}
    for name, a in {**given, **_constants()}.items():
        arrays[f"in_{name}_dram"] = a
        I[name] = nc.dram_tensor(f"in_{name}_dram", a.shape, _mybir.dt.from_np(a.dtype), kind="ExternalInput").ap()
    for name, shape in _OUTS:
        O[name] = nc.dram_tensor(f"out_{name}_dram", shape, F32, kind="ExternalOutput").ap()
    trunk(nc, I, O)
    r = _run(nc, [arrays], core_ids=[0])
    return tuple(r.results[0][f"out_{name}_dram"] for name, _ in _OUTS)
```

```python
from contextlib import ExitStack

import concourse.bass as bass
from concourse import mybir

F32, F32R, BF16, U16 = mybir.dt.float32, mybir.dt.float32r, mybir.dt.bfloat16, mybir.dt.uint16
ALU = mybir.AluOpType
ACT = mybir.ActivationFunctionType

P = 128
D_MODEL, SEQ, NB, LS = 2048, 512, 8, 4
NS = NB * LS
T = SEQ + NS
NT = SEQ // P
KT = D_MODEL // P
PLE = 256
EPS = 1e-6
DN_H, DN_QKV, DN_W = 8, 3072, 1024
GLA_H, GLA_KW, GLA_W, GLA_R = 4, 512, 1024, 16
SSD_H, SSD_W, SSD_G, SSD_N = 16, 1024, 4, 64
SSD_XBC = SSD_W + 2 * SSD_G * SSD_N
LRU_W = 1024
TAPS = 4
HALF = T // 2
D0 = SEQ - HALF

AB_BETA, AB_A, AB_Z = DN_QKV, DN_QKV + DN_H, DN_QKV + 2 * DN_H
AB_GQ = AB_Z + DN_W
AB_GK = AB_GQ + GLA_KW
AB_GV = AB_GK + GLA_KW
AB_LR = AB_GV + GLA_W
AB_GZ = AB_LR + GLA_R
CD_XBC = SSD_W
CD_DT = CD_XBC + SSD_XBC
CD_ZL = CD_DT + SSD_H
CD_XL = CD_ZL + LRU_W


def column_tiles():
    tiles = [("ab", 0, (AB_BETA, AB_A, AB_LR, AB_LR), "ab")]
    for h in range(DN_H):
        tiles += [("ab", 0, (c + P * h,), "ab") for c in (0, DN_W, 2 * DN_W, AB_Z)]
    for h in range(GLA_H):
        tiles += [("ab", 0, (c,), "ab") for c in (AB_GQ + P * h, AB_GK + P * h, AB_GV + 2 * P * h,
                                                   AB_GV + 2 * P * h + P, AB_GZ + 2 * P * h, AB_GZ + 2 * P * h + P)]
    tiles += [("abo", 0, (P * c,), "out0") for c in range(KT)]
    tiles += [("gate", 0, (P * c,), "gate0") for c in range(KT)]
    tiles += [("cd", 0, (CD_DT,), "cd")]
    tiles += [("cd", 0, (CD_XBC + SSD_W + P * c,), "cd") for c in range(4)]
    for p in range(SSD_H // 2):
        tiles += [("cd", 0, (c + P * p,), "cd") for c in (CD_XBC, 0)]
    for j in range(LRU_W // P):
        tiles += [("cd", 0, (c + P * j,), "cd") for c in (CD_XL, CD_ZL)]
    tiles += [("cdo", 0, (P * c,), "out1") for c in range(KT)]
    tiles += [("gate", 1, (P * c,), "gate1") for c in range(KT)]
    return tiles


def dn_groups():
    g = [("ssq", "dn_ln", 1), ("ssk", "dn_ln", 2), ("gbc", "dn_eg", 1), ("bbc", "dn_kb", 1), ("dm", "dn_D", 1),
         ("kk", "dn_at", 1), ("qk", "dn_qkt", 1), ("t1", "dn_t1", 1), ("kt", "dn_kend", 1), ("vt", "dn_bv", 1)]
    for l in range(1, 7):
        g.append((f"x{l}", "dn_x", l))
        if l < 6:
            g.append((f"y{l}", "dn_t", l))
        g.append((f"yt{l}", "dn_tt", l))
    return g + [("wk", "dn_nwk", 1), ("u0", "dn_u", 1), ("us", "dn_u", 2), ("s0", "dn_s", 1), ("ss", "dn_snew", 1),
                ("u1", "dn_u", 3), ("s1", "dn_s", 2), ("u2", "dn_u", 4), ("s2", "dn_s", 3), ("u3", "dn_u", 5),
                ("s3", "dn_s", 4), ("o", "dn_o1", 1), ("n", "dn_ln", 3)]


def gla_groups(h):
    return ([("lg", "gl_m", 1)] if h == 0 else []) + [("qk", "gl_at", 1)] + [(f"l{l}", "gl_at", l + 2) for l in range(7)] + \
           [("kt", "gl_kend", 1), ("v0", "gl_v", 1), ("v1", "gl_v", 2), ("sA", "gl_s", 1), ("o0", "gl_o1", 1),
            ("o1", "gl_o1", 2)] + ([("lgn", "gl_m", 2)] if h + 1 < GLA_H else []) + [("sb0", "gl_snew", 1), ("sb1", "gl_snew", 2), ("n", "gl_ln", 1)]


def ssd_groups(p):
    return [("dmA", "sp_D", 1), ("dmB", "sp_D", 2), ("ebc", "sp_ebc", 1), ("xt", "sp_v", 1), ("sP", "sp_s", 1),
            ("ss", "sp_snew", 1), ("i", "sp_i", 1), ("o", "sp_o", 1)] + ([("n", "sp_ln", 1)] if p % 2 else [])


FILL = {("bc", "bt"): 4.0, ("dn", "ssq"): 6.5, ("dn", "o"): 3.0, ("dn", "kk"): 2.0, ("dn", "x1"): 1.5, ("dn", "x3"): 1.3, ("gla", "l0"): 2.0, ("gla", "o0"): 2.0, ("gla", "o1"): 1.5, ("gla", "qk"): 2.0, ("ssd", "i"): 1.5, ("ssd", "sP"): 1.5, ("ssd", "n"): 1.3, ("lru", "i"): 1.1}
LEAD = 20

PER_UNIT = {"dn_ln": 3, "dn_x": 6, "dn_t": 5, "dn_tt": 6, "dn_u": 5, "dn_s": 4, "gl_at": 8, "gl_v": 2, "gl_o1": 2,
            "gl_snew": 2, "gl_um": 2, "gl_ed": 7, "gl_E": 7, "gl_qkt": 7, "gl_osq": 2, "sp_D": 2, "bc_b": 2,
            "bc_cb": 4, "tail_copied": 1, "nrm_ln": 1}

UNITS = [("ab_rows", 0)] + [("dn", h) for h in range(DN_H)] + [("gla", h) for h in range(GLA_H)] + [("ab_tail", 0)]
UNITS_CD = [("cd_rows", 0), ("bc", 0)] + [("ssd", p) for p in range(SSD_H // 2)] + \
           [("lru", j) for j in range(LRU_W // P)] + [("cd_tail", 0)]


def group_table():
    order, count = [], {}

    def add(unit, name, reader, value):
        order.append((unit, name, reader, value))

    def once(unit, name, reader):
        count[reader] = count.get(reader, 0) + 1
        add(unit, name, reader, count[reader])

    for t in range(NT + 1):
        for i in range(2):
            once(("setup", 0), f"x{t}{i}", "in_copied")
    once(("setup", 0), "pv", "in_copied")
    once(("setup", 0), "h0", "in_copied")
    once(("setup", 0), "h1", "in_copied")
    once(("norm", 0), "n", "nrm_ln")
    for unit in UNITS:
        kind, h = unit
        if kind == "ab_rows":
            once(unit, "c0", "rows_copied")
        if kind == "dn":
            for n, r, i in dn_groups():
                add(unit, n, r, PER_UNIT.get(r, 1) * h + i)
        if kind == "gla":
            for n, r, i in gla_groups(h):
                add(unit, n, r, PER_UNIT.get(r, 1) * h + i)
        if kind == "ab_tail":
            for i in range(3):
                once(unit, f"t{i}", "tail_copied")
    for layer in range(2):
        if layer:
            for unit in UNITS_CD:
                kind, h = unit
                if kind == "cd_rows":
                    once(unit, "eg", "rows_copied")
                    once(unit, "c0", "rows_copied")
                if kind == "bc":
                    add(unit, "bt", "bc_b", 1)
                    add(unit, "bts", "bc_b", 2)
                    for g in range(4):
                        add(unit, f"cb{g}", "bc_cb", g + 1)
                if kind == "ssd":
                    for n, r, i in ssd_groups(h):
                        add(unit, n, r, h // 2 + 1 if r == "sp_ln" else PER_UNIT.get(r, 1) * h + i)
                if kind == "lru":
                    add(unit, "r", "lr_r", h + 1)
                    add(unit, "i", "lr_i", h + 1)
                if kind == "cd_tail":
                    for i in range(3):
                        once(unit, f"t{i}", "tail_copied")
        once(("norm", 1 + 2 * layer), "n", "nrm_ln")
        for i in range(2):
            once(("gate", layer), f"p{i}", "in_copied")
        for c in range(KT):
            once(("gate", layer), f"g{c}", "gate_read")
        once(("norm", 2 + 2 * layer), "n", "nrm_ln")
    for t in range(NT + 1):
        for i in range(2):
            once(("final", 0), f"y{t}{i}", "out_copied")
    return order


SEMS = """w_landed0 w_landed1 w_landed2 hi_ready lo_ready slice_done dense_read0 dense_read1 stage_stored0 stage_stored1
act_chain dve_chain pool_chain act_evac work_ready in_copied nrm_sq nrm_ln nrm_rstd x_hi x_ready y_done y_in0 y_in1 y_in2 y_in3 y_in4 y_in5 h_loaded1 h_loaded2 h_loaded3 z_loaded dn_z gl_z sp_z sq_added sq_summed
consts_loaded params_loaded rows_loaded x_loaded0 x_loaded1 h_stored h_loaded0
rows_copied rows_act rows_dve rows_ready pool_rows eg_rows u_loaded s_loaded out_stored
dn_smp dn_conv dn_silu dn_sq dn_ln dn_rs dn_eg dn_kb dn_D dn_at dn_tt1 dn_qkt dn_t1 dn_kend dn_bv dn_x dn_t dn_tt
dn_nwk dn_mwk dn_u dn_um dn_s dn_gs dn_snew dn_osq dn_o1 dn_rstd dn_y
gl_q gl_abs gl_m gl_l gl_G gl_eg gl_kd gl_kf gl_qg gl_ed gl_E gl_qkt gl_at gl_kend gl_v gl_s gl_um gl_gs gl_snew gl_osq
gl_o1 gl_ln gl_rstd gl_y
bc_smp bc_conv bc_silu bc_b bc_cb
sp_smp sp_conv sp_silu sp_D sp_ebc sp_A sp_v sp_um sp_s sp_gs sp_snew sp_i sp_o sp_y sp_sq sp_ln sp_rstd sp_out
lr_smp lr_conv lr_r lr_i lr_a lr_z lr_t lr_sq lr_hs lr_y lr_w
tail_copied tail_made sp_sel ssd_stored y_stored0 y_stored1 p_loaded wp_loaded0 wp_loaded1 gate_sig gate_read gate_done out_copied zeroed consts_set masks_loaded""".split()


PARAM_ROWS = {
    "norm_g": (0, 0, 32), "final_norm": (0, 32, 16), "ple_norm": (0, 48, 32), "ssd_norm": (0, 80, 8),
    "dn_conv_w": (1, 0, 96), "gla_ba": (1, 96, 4), "dn_norm": (1, 100, 1), "gla_norm": (1, 101, 2),
    "ssd_conv_w": (2, 0, 48), "ssd_conv_b": (2, 48, 12), "lru_conv_w": (2, 60, 32), "lru_conv_b": (2, 92, 8),
    "lru_ba": (2, 100, 8), "lru_bx": (2, 108, 8), "lru_lambda": (2, 116, 8)}
PARAM_DMAS = len(PARAM_ROWS) + 6
ROW_DMAS = 7


def as_rows(ap):
    if len(ap.shape) == 1:
        return ap.rearrange("(c x) -> c x", x=P)
    if len(ap.shape) == 2:
        return ap.rearrange("l (c x) -> (l c) x", x=P)
    return ap.rearrange("l t (c x) -> (l t c) x", x=P)


def trunk(nc, I, O):
    with ExitStack() as ctx:
        def sb(name, shape, dt=F32):
            return ctx.enter_context(nc.sbuf_tensor(name, shape, dt))

        S = {n: ctx.enter_context(nc.semaphore("s_" + n)) for n in SEMS}

        psd = [ctx.enter_context(nc.psum_tensor(f"psd{i}", [P, 1024], F32)) for i in range(2)]
        psw = [ctx.enter_context(nc.psum_tensor(f"psw{i}", [P, 1024], F32)) for i in range(2)]
        xh, xl = sb("xh", [P, KT, T], F32R), sb("xl", [P, KT, T], F32R)
        arena = sb("arena", [P, KT * T])
        KH = KT // 2
        NW = 3
        w_raw = sb("w_raw", [P, NW, KH, P])
        w_hi, w_lo = sb("w_hi", [P, NW, KH, P], F32R), sb("w_lo", [P, NW, KH, P], F32R)
        raws = sb("raws", [P, 6 * T])
        stage = sb("stage", [P, 2, T])
        extra = sb("extra", [P, 4 * T])
        sbuf = sb("states", [P, 2048])
        hist = sb("hist", [P, 44, 36])
        smp = sb("smp", [P, 4, NB, TAPS - 1 + LS])
        pv = sb("pv", [P, 3 * P])
        cols = sb("cols", [P, NT + 1, P])
        rowG, rowB, rowlr = sb("rowG", [P, T]), sb("rowB", [P, T]), sb("rowlr", [P, T])
        ident, ones = sb("ident", [P, P]), sb("ones", [P, P])
        cb16 = sb("cb16", [P, 14 * P + P + P + 32 + T + 8 * 32 + 8], BF16)
        cst = sb("cst", [P, 8])
        egt = sb("egt", [P, SSD_H * 12 + 8])
        small = sb("small", [P, 64])
        selp = sb("selp", [P, P])
        rstd = sb("rstd", [P, T])
        wa2 = sb("wa2", [P, GLA_KW])

        MX = cb16[:, 0:7 * P].rearrange("p (l j) -> p l j", l=7)
        MT = cb16[:, 7 * P:14 * P].rearrange("p (l j) -> p l j", l=7)
        o16 = 14 * P
        ib16, negm, negs = cb16[:, o16:o16 + P], cb16[:, o16 + P:o16 + 2 * P], cb16[0:NS, o16 + 2 * P:o16 + 2 * P + NS]
        o16 += 2 * P + NS
        rmask = cb16[:, o16:o16 + T]
        bmask = cb16[:, o16 + T:o16 + T + NB * NS].rearrange("p (b i) -> p b i", b=NB)
        rowm = cb16[0:NS, o16 + T + NB * NS:o16 + T + NB * NS + NB]

        uT = nc.dram_tensor("uT_scratch", [60, P, T], F32, kind="Internal").ap()
        yT = nc.dram_tensor("yT_scratch", [KT, P, T], F32, kind="Internal").ap()
        hD = nc.dram_tensor("hT_scratch", [KT, P, T], F32, kind="Internal").ap()

        def pvc(name, i, n=1):
            col, row, _ = PARAM_ROWS[name]
            return pv[:, P * col + row + i:P * col + row + i + n]

        def slot(i, n=1, w=T):
            return arena[:, T * i:T * i + n * w]

        def ssd_x(p):
            return rowlr[:, :] if p % 2 else arena[:, 5632:5632 + T]

        def norm_scale(ph):
            name, col = {0: ("norm_g", 0), 2: ("ple_norm", 0), 3: ("norm_g", 16), 5: ("ple_norm", 16)}.get(ph, (None, 0))
            return pvc(name, col, 16) if name else None

        def lru_slot(j, i):
            return slot(7 * (j % 2) + i)

        zloads, n = {}, 0
        for u in UNITS + UNITS_CD:
            if u[0] in ("dn", "gla", "ssd", "lru"):
                n += 16
                zloads[u] = n

        def hT(c):
            return arena[:, T * c:T * (c + 1)]

        def tiles4(ap):
            return ap.rearrange("p (t i) -> p t i", t=NT)

        def bc4(ap):
            return ap.unsqueeze(1).broadcast_to([ap.shape[0], NT, ap.shape[1]])

        def tok(t):
            return (P * t, P) if t < NT else (SEQ, NS)

        TILES = column_tiles()
        GROUPS = group_table()
        NO = {(u, n): i for i, (u, n, _, _) in enumerate(GROUPS)}
        assert len(NO) == len(GROUPS)
        first = {}
        for d, t in enumerate(TILES):
            first.setdefault(t[3], d)
        staged = {}
        count = [0, 0]
        for ph in ("ab", "cd"):
            for d in [d for d, t in enumerate(TILES) if t[3] == ph][1:]:
                e = sum(count) % 2
                count[e] += 1
                staged[d] = (d - first[ph] - 1, e, 16 * count[e])
        SL = KT
        NSL = SL * len(TILES)
        phases = ["ab", "out0", "gate0", "cd", "out1", "gate1"]

        def first_slice(ph):
            return SL * first[ph]

        def end_slice(ph):
            i = phases.index(ph) + 1
            return SL * first[phases[i]] if i < len(phases) else NSL

        RAW = {}
        d = first["ab"] + 1
        for h in range(DN_H):
            RAW["dn", h] = (d, 4)
            d += 4
        for h in range(GLA_H):
            RAW["gla", h] = (d, 6)
            d += 6
        d = first["cd"] + 1
        RAW["bc", 0] = (d, 4)
        d += 4
        for p in range(SSD_H // 2):
            RAW["ssd", p] = (d, 2)
            d += 2
        for j in range(LRU_W // P):
            RAW["lru", j] = (d, 2)
            d += 2

        target = {}
        for ph, units in (("ab", UNITS), ("cd", UNITS_CD)):
            last = SL * (first[ph] + 1)
            for i, u in enumerate(units):
                nxt = [SL * (RAW[v][0] + RAW[v][1]) for v in units[i + 1:] if v in RAW]
                lead = LEAD + SL if i + 1 < len(units) and units[i + 1][0] == "gla" else LEAD if i + 1 < len(units) and units[i + 1] in zloads else 4
                end = min(nxt[0] + lead, end_slice(ph)) if nxt else end_slice(ph)
                mine = [n for (v, n, _, _) in GROUPS if v == u]
                weight = [FILL.get((u[0], n), FILL.get(u[0], 1.0)) for n in mine]
                for j, n in enumerate(mine):
                    target[u, n] = last + int((end - last) * sum(weight[:j + 1]) / sum(weight) + 1e-6)
                target[u, "start"] = last
                if mine or u[0] in RAW:
                    last = max(last, end)
                target[u, "end"] = last
        LAST = (("gla", GLA_H - 1), ("lru", LRU_W // P - 1))
        early = {}
        for layer, u in enumerate(LAST):
            mine = [n for (v, n, _, _) in GROUPS if v == u]
            for j, n in enumerate(mine):
                early[u, n] = (layer, min(KT - 2, (j + 1) * (1 if layer == 0 else 6)))
                if layer == 0:
                    target[u, n] += max(0, min(KT - 2, j - 1))

        def y_source(layer, k):
            if k < KT - 2:
                e = k % Y_BUFS[layer]
                return stage[:, e, :] if e < 2 else extra[:, T * (e - 2):T * (e - 1)]
            return slot(9 + k - (KT - 2)) if layer == 0 else lru_slot(k - 8, 1)


        Y_BUFS = (2, 6)

        STORES = {"dn": 3, "gla": 3, "ab_tail": 6, "ssd": 2, "lru": 1, "cd_tail": 6}
        stored, total = {}, 0
        for u in UNITS + UNITS_CD:
            stored[u] = total
            n = STORES.get(u[0], 0)
            if u[0] == "ssd" and u[1] % 2 == 0:
                n -= 1
            if u in (LAST[0], ("lru", LRU_W // P - 2), LAST[1]):
                n -= 1
            total += 16 * n
        stored["end"] = total
        loads = {}
        n = 0
        for u in UNITS + UNITS_CD:
            if u in RAW:
                n += 16
                loads[u] = n
        sloads, n = {}, 0
        for u in UNITS + UNITS_CD:
            if u[0] in ("dn", "gla"):
                n += 16
            if u[0] == "ssd":
                n += 32
            if u[0] == "lru":
                n += 64
            sloads[u] = n

        block = ctx.enter_context(nc.Block())

        W_DRAM = {"ab": I["ab_w_in"], "abo": I["ab_w_out"], "gate": I["ple_w_gate"], "cd": I["cd_w_in"],
                  "cdo": I["cd_w_out"]}

        @block.sync
        def _(sp):
            def load_x(t):
                _, n = tok(t)
                dst = extra if t % 2 == 0 else sbuf
                if t >= 2:
                    sp.wait_ge(S["in_copied"], 2 * (t - 1))
                src = I["x_prompt"][0, P * t:P * t + P] if t < NT else I["x_sample"].rearrange("b s d -> (b s) d")
                sp.dma_start(dst[0:n, 0:D_MODEL], src).then_inc(S[f"x_loaded{t % 2}"], 16)

            load_x(0)
            load_x(1)
            for q in range(2 * len(TILES)):
                if q in (2, 3):
                    for t in ((2, 3), (4,))[q - 2]:
                        load_x(t)
                name, layer, starts, _ = TILES[q // 2]
                if q >= NW:
                    sp.wait_ge(S["lo_ready"], q - NW + 1)
                width = P // len(starts)
                for i, c in enumerate(starts):
                    src = W_DRAM[name][layer, 1024 * (q % 2):1024 * (q % 2) + 1024, c:c + width]
                    sp.dma_start(w_raw[:, q % NW, :, width * i:width * (i + 1)],
                                 src.rearrange("(k p) n -> p k n", p=P)).then_inc(S[f"w_landed{q % NW}"], 16)

        landed, c3 = [], [0, 0, 0]
        for q in range(2 * len(TILES)):
            c3[q % NW] += 16 * len(TILES[q // 2][2])
            landed.append(c3[q % NW])

        @block.tensor
        def _(pe):
            at = [0]

            def dense_slice(n):
                d, k = n // SL, n % SL
                q, r = n // KH, (n // KH) % NW
                ph = phases.index(TILES[d][3])
                if k == 0 and d >= 2:
                    pe.wait_ge(S[f"dense_read{d % 2}"], d // 2)
                if d == first[TILES[d][3]]:
                    pe.wait_ge(S["x_ready"], KT * ph + k + 1)
                if k % KH == 0:
                    pe.wait_ge(S["lo_ready"], q + 1)
                out = psd[d % 2]
                for i, (w, x) in enumerate(((w_hi, xh), (w_hi, xl), (w_lo, xh))):
                    for half in range(2):
                        mm = pe.matmul(out[:, D0 + HALF * half:D0 + HALF * (half + 1)], w[:, r, k % KH, :],
                                       x[:, k, HALF * half:HALF * (half + 1)],
                                       start=(k == 0 and i == 0), stop=(k == KT - 1 and i == 2))
                mm.then_inc(S["slice_done"], 1)

            def fill(to):
                while at[0] < to:
                    dense_slice(at[0])
                    at[0] += 1

            def group(u, name):
                if (u, name) in target:
                    fill(target[u, name])
                g = NO[u, name]
                if g >= 2:
                    _, _, reader, value = GROUPS[g - 2]
                    pe.wait_ge(S[reader], value)
                return psw[g % 2]

            def prompt_and_samples(W, lhsT, rhs, rows=P, **kw):
                pe.matmul(W[0:rows, 0:SEQ], lhsT, rhs[:, 0:SEQ], **kw)
                return pe.matmul(W[0:rows, SEQ:T], lhsT, rhs[:, SEQ:T], **kw)

            def blocks(W, lhsT, rhs, samples=True):
                for t in range(NT):
                    mm = pe.matmul(W[:, P * t:P * t + P], lhsT[:, P * t:P * t + P], rhs[:, P * t:P * t + P],
                                   start=True, stop=True)
                if samples:
                    mm = pe.matmul(W[0:NS, SEQ:T], lhsT[0:samples, SEQ:T], rhs[0:samples, SEQ:T], start=True, stop=True)
                return mm

            def to_token_major(W, src):
                for t in range(NT):
                    pe.transpose(W[:, P * t:P * t + P], src[:, P * t:P * t + P], ident[:, :])
                return pe.transpose(W[0:NS, SEQ:SEQ + P], src[:, SEQ:T], ident[:, :])

            def norm(i):
                W = group(("norm", i), "n")
                pe.wait_ge(S["sq_added"], i + 1)
                prompt_and_samples(W, ones[:, :], sbuf[:, T:2 * T], start=True, stop=True).then_inc(S["work_ready"], 1)

            def columns_of_rows(u):
                W = group(u, "c0")
                pe.wait_ge(S["rows_ready"], 1 if u[0] == "ab_rows" else 2)
                st = slot(0)
                for t in range(NT):
                    pe.transpose(W[:, P * t:P * t + P], st[:, P * t:P * t + P], ident[:, :])
                pe.transpose(W[0:NS, SEQ:SEQ + P], st[:, SEQ:T], ident[:, :]).then_inc(S["work_ready"], 1)

            def decay_exponents(u, name, h, nh):
                W = group(u, name)
                sel = ident[0:nh, h:h + 1].broadcast_to([nh, P])
                pe.matmul(W[:, 0:SEQ], sel, rowG[0:nh, 0:SEQ], start=True, stop=False)
                pe.matmul(W[:, 0:SEQ], ib16, bc4(negm), start=False, stop=True)
                pe.matmul(W[0:NS, SEQ:T], sel[:, 0:NS], rowG[0:nh, SEQ:T], start=True, stop=False)
                pe.matmul(W[0:NS, SEQ:T], ib16[0:NS, 0:NS], negs, start=False, stop=True).then_inc(S["work_ready"], 1)

            def dn(h):
                u = ("dn", h)
                q, k, v = slot(0), slot(1), slot(2)
                Tm, X, kb, qg, AT, QKT, TT = slot(3), slot(4), slot(7), slot(8), slot(9), slot(10), slot(11)
                bgk, kend, bv = (arena[:, 12 * T + 640 * i:12 * T + 640 * (i + 1)] for i in range(3))
                nwk, osq = slot(3), slot(4)
                mwk = arena[:, 12 * T + 1920:12 * T + 1920 + 256].rearrange("p (b i) -> p b i", b=NB)
                uu, SS, um = extra[:, 0:640], extra[:, 640:640 + 512], extra[0:NS, 1152:2176]
                Sin = sbuf[:, 0:1024].rearrange("p (b e) -> p b e", b=NB)
                W = group(u, "ssq")
                pe.wait_ge(S["dn_sq"], h + 1)
                prompt_and_samples(W, ones[:, :], slot(6), start=True, stop=True).then_inc(S["work_ready"], 1)
                W = group(u, "ssk")
                prompt_and_samples(W, ones[:, :], slot(7), start=True, stop=True).then_inc(S["work_ready"], 1)
                sel = ident[0:DN_H, h:h + 1].broadcast_to([DN_H, P])
                W = group(u, "gbc")
                prompt_and_samples(W, sel, rowG[0:DN_H, :], start=True, stop=True).then_inc(S["work_ready"], 1)
                W = group(u, "bbc")
                prompt_and_samples(W, sel, rowB[0:DN_H, :], start=True, stop=True).then_inc(S["work_ready"], 1)
                decay_exponents(u, "dm", h, DN_H)
                W = group(u, "kk")
                pe.wait_ge(S["dn_kb"], h + 1)
                blocks(W, k, kb, samples=P).then_inc(S["work_ready"], 1)
                W = group(u, "qk")
                blocks(W, k, q, samples=P).then_inc(S["work_ready"], 1)
                W = group(u, "t1")
                pe.wait_ge(S["dn_tt1"], h + 1)
                for t in range(NT):
                    pe.transpose(W[:, P * t:P * t + P], TT[:, P * t:P * t + P], ident[:, :])
                pe.transpose(W[0:NS, SEQ:T], TT[0:NS, SEQ:T], ident[0:NS, 0:NS]).then_inc(S["work_ready"], 1)
                W = group(u, "kt")
                to_token_major(W, k).then_inc(S["work_ready"], 1)
                W = group(u, "vt")
                to_token_major(W, v).then_inc(S["work_ready"], 1)
                for l in range(1, 7):
                    ns = NS if l == 1 else 0
                    W = group(u, f"x{l}")
                    if l == 1:
                        pe.wait_ge(S["dn_t1"], h + 1)
                    else:
                        pe.wait_ge(S["dn_tt"], 6 * h + l - 1)
                    blocks(W, AT, Tm, samples=ns).then_inc(S["work_ready"], 1)
                    if l < 6:
                        W = group(u, f"y{l}")
                        pe.wait_ge(S["dn_x"], 6 * h + l)
                        blocks(W, TT, X, samples=ns).then_inc(S["work_ready"], 1)
                    W = group(u, f"yt{l}")
                    pe.wait_ge(S["dn_x"], 6 * h + l)
                    blocks(W, X, TT, samples=ns).then_inc(S["work_ready"], 1)
                W = group(u, "wk")
                pe.wait_ge(S["dn_tt"], 6 * h + 6)
                for t in range(NT):
                    pe.matmul(W[:, P * t:P * t + P], bgk[:, P * t:P * t + P], TT[:, P * t:P * t + P], start=True, stop=True)
                pe.matmul(W[:, SEQ:T], bgk[0:NS, SEQ:SEQ + P], TT[0:NS, SEQ:T], start=True, stop=True).then_inc(S["work_ready"], 1)

                def u_step(t):
                    W = group(u, f"u{t}")
                    mm = pe.matmul(W[:, 0:P], TT[:, P * t:P * t + P], bv[:, P * t:P * t + P], start=True, stop=t == 0)
                    if t:
                        pe.wait_ge(S["dn_nwk"], h + 1)
                        pe.wait_ge(S["dn_s"], 4 * h + t)
                        mm = pe.matmul(W[:, 0:P], nwk[:, P * t:P * t + P], SS[:, P * (t - 1):P * t], start=False, stop=True)
                    mm.then_inc(S["work_ready"], 1)

                def s_step(t):
                    W = group(u, f"s{t}")
                    pe.wait_ge(S["dn_u"], 5 * h + (1, 3, 4, 5)[t])
                    pe.matmul(W[:, 0:P], kend[:, P * t:P * t + P], uu[:, P * t:P * t + P], start=True,
                              stop=True).then_inc(S["work_ready"], 1)

                u_step(0)
                W = group(u, "us")
                pe.wait_ge(S["dn_mwk"], h + 1)
                pe.wait_ge(S["s_loaded"], sloads[u])
                pe.matmul(W[0:NS, 0:P], TT[0:NS, SEQ:T], bv[0:NS, SEQ:SEQ + P], start=True, stop=False)
                for b in range(NB):
                    mm = pe.matmul(W[0:NS, 0:P], mwk[:, b, :], Sin[:, b, :], start=False, stop=b == NB - 1)
                mm.then_inc(S["work_ready"], 1)
                s_step(0)
                W = group(u, "ss")
                pe.wait_ge(S["dn_um"], h + 1)
                for i in range(2):
                    mm = pe.matmul(W[:, 512 * i:512 * i + 512], kend[0:NS, SEQ:SEQ + P], um[:, 512 * i:512 * i + 512],
                                   start=True, stop=True)
                mm.then_inc(S["work_ready"], 1)
                for t in range(1, NT):
                    u_step(t)
                    s_step(t)
                W = group(u, "o")
                for t in range(NT):
                    if t:
                        pe.matmul(W[:, P * t:P * t + P], SS[:, P * (t - 1):P * t], qg[:, P * t:P * t + P], start=True, stop=False)
                    pe.matmul(W[:, P * t:P * t + P], uu[:, P * t:P * t + P], QKT[:, P * t:P * t + P], start=t == 0, stop=True)
                mm = pe.matmul(W[:, SEQ:T], uu[0:NS, SEQ:SEQ + P], QKT[0:NS, SEQ:T], start=True, stop=True,
                               skip_group_check=True)
                for b in range(NB):
                    cc = slice(SEQ + LS * b, SEQ + LS * b + LS)
                    mm = pe.matmul(W[:, cc], Sin[:, b, :], qg[:, cc], start=False, stop=True, skip_group_check=True)
                mm.then_inc(S["work_ready"], 1)
                W = group(u, "n")
                pe.wait_ge(S["dn_osq"], h + 1)
                prompt_and_samples(W, ones[:, :], osq, start=True, stop=True).then_inc(S["work_ready"], 1)

            def log_gates(u, name, h):
                W = group(u, name)
                prompt_and_samples(W, wa2[64:64 + GLA_R, P * h:P * h + P], rowlr[64:64 + GLA_R, :],
                                   start=True, stop=True).then_inc(S["work_ready"], 1)

            def gla(h):
                u = ("gla", h)
                q, k = raws[:, 0:T], raws[:, T:2 * T]
                qg, kendT, qt, kt, AT = slot(6), slot(7), slot(9), slot(10), slot(11)
                kend = arena[:, 12 * T:12 * T + 640]
                vt = arena[:, 12 * T + 640:12 * T + 1920].rearrange("p (t e) -> p t e", t=NT + 1)
                SS = extra[:, 0:1024].rearrange("p (t e) -> p t e", t=NT)
                um = extra[0:NS, 1024:2048]
                Sin = sbuf[:, :].rearrange("p (b e) -> p b e", b=NB)
                if h == 0:
                    log_gates(u, "lg", 0)
                W = group(u, "qk")
                pe.wait_ge(S["gl_q"], h + 1)
                blocks(W, k, q, samples=P).then_inc(S["work_ready"], 1)
                for l in range(7):
                    W = group(u, f"l{l}")
                    pe.wait_ge(S["gl_qkt"], 7 * h + l + 1)
                    blocks(W, kt, qt, samples=P if l < 2 else 0).then_inc(S["work_ready"], 1)
                W = group(u, "kt")
                to_token_major(W, kendT).then_inc(S["work_ready"], 1)
                for e in range(2):
                    W = group(u, f"v{e}")
                    to_token_major(W, raws[:, T * (2 + e):T * (3 + e)]).then_inc(S["work_ready"], 1)
                W = group(u, "sA")
                pe.wait_ge(S["gl_v"], 2 * h + 2)
                for t in range(NT):
                    mm = pe.matmul(W[:, 256 * t:256 * t + 256], kend[:, P * t:P * t + P], vt[:, t, :], start=True, stop=True)
                mm.then_inc(S["work_ready"], 1)
                for e in range(2):
                    W = group(u, f"o{e}")
                    if e == 0:
                        pe.wait_ge(S["gl_s"], h + 1)
                        pe.wait_ge(S["s_loaded"], sloads[u])
                    ec = slice(P * e, P * e + P)
                    for t in range(NT):
                        pe.matmul(W[:, P * t:P * t + P], vt[:, t, ec], AT[:, P * t:P * t + P], start=True, stop=t == 0)
                        if t:
                            pe.matmul(W[:, P * t:P * t + P], SS[:, t - 1, ec], qg[:, P * t:P * t + P], start=False, stop=True)
                    mm = pe.matmul(W[:, SEQ:T], vt[0:NS, NT, ec], AT[0:NS, SEQ:T], start=True, stop=True, skip_group_check=True)
                    for b in range(NB):
                        cc = slice(SEQ + LS * b, SEQ + LS * b + LS)
                        mm = pe.matmul(W[:, cc], Sin[:, b, ec], qg[:, cc], start=False, stop=True, skip_group_check=True)
                    mm.then_inc(S["work_ready"], 1)
                if h + 1 < GLA_H:
                    log_gates(u, "lgn", h + 1)
                for i in range(2):
                    W = group(u, f"sb{i}")
                    pe.wait_ge(S["gl_um"], 2 * h + i + 1)
                    for j in range(2):
                        mm = pe.matmul(W[:, 512 * j:512 * j + 512], kend[0:NS, SEQ:SEQ + P], um[:, 512 * j:512 * j + 512],
                                       start=True, stop=True)
                    mm.then_inc(S["work_ready"], 1)
                W = group(u, "n")
                pe.wait_ge(S["gl_osq"], 2 * h + 2)
                for e in range(2):
                    pe.matmul(W[:, 0:SEQ], ones[:, :], slot(9 + e)[:, 0:SEQ], start=e == 0, stop=e == 1)
                    mm = pe.matmul(W[:, SEQ:T], ones[:, :], slot(9 + e)[:, SEQ:T], start=e == 0, stop=e == 1)
                mm.then_inc(S["work_ready"], 1)

            def bc():
                u = ("bc", 0)
                Bt = arena[:, 8 * T:8 * T + 1280].rearrange("p (t n) -> p t n", t=NT + 1)
                W = group(u, "bt")
                pe.wait_ge(S["bc_silu"], 1)
                for t in range(NT):
                    for i in range(2):
                        mm = pe.transpose(W[:, 256 * t + P * i:256 * t + P * i + P], slot(i)[:, P * t:P * t + P], ident[:, :])
                mm.then_inc(S["work_ready"], 1)
                W = group(u, "bts")
                for i in range(2):
                    mm = pe.transpose(W[0:NS, P * i:P * i + P], slot(i)[:, SEQ:T], ident[:, :])
                mm.then_inc(S["work_ready"], 1)
                for g in range(SSD_G):
                    W = group(u, f"cb{g}")
                    pb = SSD_N * (g % 2)
                    B, C = slot(g // 2)[pb:pb + SSD_N, :], slot(2 + g // 2)[pb:pb + SSD_N, :]
                    blocks(W, B, C, samples=SSD_N).then_inc(S["work_ready"], 1)

            def ssd(p):
                u = ("ssd", p)
                g = p // 2
                pb = SSD_N * (g % 2)
                hp = slice(pb, pb + SSD_N)
                C = slot(2 + g // 2)[hp, :]
                Bt = arena[:, 8 * T:8 * T + 1280].rearrange("p (t n) -> p t n", t=NT + 1)
                A = [slot(0), slot(1)]
                xs = ssd_x(p)
                v, v2, SS = arena[:, 6720:7360], arena[:, 7360:8000], arena[:, 8000:8640]
                um = extra[0:NS, 0:1024]
                Sin = sbuf[:, 0:1024].rearrange("p (b e) -> p b e", b=NB)
                decay_exponents(u, "dmA", 2 * p, SSD_H)
                decay_exponents(u, "dmB", 2 * p + 1, SSD_H)
                W = group(u, "ebc")
                pe.wait_ge(S["sp_sel"], p + 1)
                prompt_and_samples(W, selp[0:SSD_H, :], rowG[0:SSD_H, :], start=True, stop=True).then_inc(S["work_ready"], 1)
                W = group(u, "xt")
                pe.wait_ge(S["sp_silu"], p + 1)
                to_token_major(W, xs).then_inc(S["work_ready"], 1)
                W = group(u, "sP")
                pe.wait_ge(S["sp_v"], p + 1)
                for t in range(NT):
                    mm = pe.matmul(W[hp, P * t:P * t + P], Bt[:, t, SSD_N * g:SSD_N * (g + 1)], v2[:, P * t:P * t + P],
                                   start=True, stop=True)
                mm.then_inc(S["work_ready"], 1)
                W = group(u, "ss")
                pe.wait_ge(S["sp_um"], p + 1)
                for i in range(2):
                    mm = pe.matmul(W[hp, 512 * i:512 * i + 512], Bt[0:NS, NT, SSD_N * g:SSD_N * (g + 1)],
                                   um[:, 512 * i:512 * i + 512], start=True, stop=True)
                mm.then_inc(S["work_ready"], 1)
                W = group(u, "i")
                pe.wait_ge(S["sp_s"], p + 1)
                pe.wait_ge(S["s_loaded"], sloads[u])
                for t in range(NT):
                    pe.matmul(W[:, P * t:P * t + P], SS[hp, P * t:P * t + P], C[:, P * t:P * t + P], start=True, stop=True)
                for b in range(NB):
                    cc = slice(SEQ + LS * b, SEQ + LS * b + LS)
                    mm = pe.matmul(W[:, cc], Sin[hp, b, :], C[:, cc], start=True, stop=True)
                mm.then_inc(S["work_ready"], 1)
                W = group(u, "o")
                pe.wait_ge(S["sp_A"], p + 1)
                for e in range(2):
                    he = slice(SSD_N * e, SSD_N * (e + 1))
                    for t in range(NT):
                        pe.matmul(W[he, P * t:P * t + P], v[:, P * t + SSD_N * e:P * t + SSD_N * (e + 1)],
                                  A[e][:, P * t:P * t + P], start=True, stop=True)
                    mm = pe.matmul(W[he, SEQ:T], v[0:NS, SEQ + SSD_N * e:SEQ + SSD_N * (e + 1)], A[e][0:NS, SEQ:T],
                                   start=True, stop=True)
                mm.then_inc(S["work_ready"], 1)
                if p % 2:
                    W = group(u, "n")
                    pe.wait_ge(S["sp_sq"], p + 1)
                    for e in range(2):
                        sq = raws[:, T * (2 + e):T * (3 + e)]
                        pe.matmul(W[:, 0:SEQ], ones[:, :], sq[:, 0:SEQ], start=e == 0, stop=e == 1)
                        mm = pe.matmul(W[:, SEQ:T], ones[:, :], sq[:, SEQ:T], start=e == 0, stop=e == 1)
                    mm.then_inc(S["work_ready"], 1)

            def lru(j):
                u = ("lru", j)
                bd = sbuf[:, 256 * (j % 2):256 * (j % 2) + 256].rearrange("p (i n) -> p i n", i=2)
                for i, name in enumerate("ri"):
                    W = group(u, name)
                    if i == 0:
                        pe.wait_ge(S["lr_conv"], j + 1)
                        pe.wait_ge(S["s_loaded"], sloads[u])
                    prompt_and_samples(W, bd[:, i, :], lru_slot(j, 0), start=True, stop=True).then_inc(S["work_ready"], 1)

            def tail(u, ntiles, base, rows):
                pe.wait_ge(S["tail_made"], 1 if u[0] == "ab_tail" else 2)
                i = 0
                for n, (b0, nt) in enumerate(zip(base, ntiles)):
                    W = group(u, f"t{n}")
                    for j in range(nt):
                        mm = pe.transpose(W[0:rows[n], P * j:P * j + P], hist[:, b0 + j, 0:rows[n]], ident[:, :])
                    mm.then_inc(S["work_ready"], 1)

            def gate(layer):
                u = ("gate", layer)
                ptok = raws[:, 0:1280].rearrange("p (t c) -> p t c", t=NT + 1)
                pT = raws[:, 1280:1280 + 2 * T].rearrange("p (k t) -> p k t", k=2)
                wp = raws[:, 2368:2880].rearrange("p (s k n) -> p s k n", s=2, k=2)
                for i in range(2):
                    W = group(u, f"p{i}")
                    if i == 0:
                        pe.wait_ge(S["p_loaded"], 32 * (layer + 1))
                    for t in range(NT + 1):
                        c, n = tok(t)
                        mm = pe.transpose(W[:, c:c + n], ptok[0:n, t, P * i:P * i + P], ident[0:n, 0:n])
                    mm.then_inc(S["work_ready"], 1)
                _, _, reader, value = GROUPS[NO[u, "p1"]]
                pe.wait_ge(S[reader], value)
                for c in range(KT):
                    fill(first_slice(f"gate{layer}") + SL * (c + 1))
                    W = group(u, f"g{c}")
                    pe.wait_ge(S[f"wp_loaded{c % 2}"], 16 * (8 * layer + c // 2 + 1))
                    for k in range(2):
                        pe.matmul(W[:, 0:SEQ], wp[:, c % 2, k, :], pT[:, k, 0:SEQ], start=k == 0, stop=k == 1)
                        mm = pe.matmul(W[:, SEQ:T], wp[:, c % 2, k, :], pT[:, k, SEQ:T], start=k == 0, stop=k == 1)
                    mm.then_inc(S["work_ready"], 1)

            u = ("setup", 0)
            pe.wait_ge(S["consts_loaded"], 16)
            pe.wait_ge(S["consts_set"], 1)
            for t in range(NT + 1):
                _, n = tok(t)
                src = extra if t % 2 == 0 else sbuf
                for i in range(2):
                    W = group(u, f"x{t}{i}")
                    if i == 0:
                        pe.wait_ge(S[f"x_loaded{t % 2}"], 16 * (t // 2 + 1))
                    for c in range(8):
                        mm = pe.transpose(W[:, P * c:P * c + n], src[0:n, P * (8 * i + c):P * (8 * i + c) + P],
                                          ident[0:n, 0:n])
                    mm.then_inc(S["work_ready"], 1)
            W = group(u, "pv")
            pe.wait_ge(S["params_loaded"], PARAM_DMAS * 16)
            for i, n in enumerate((88, 103, 124)):
                mm = pe.transpose(W[:, P * i:P * i + n], cols[0:n, i, :], ident[0:n, 0:n])
            mm.then_inc(S["work_ready"], 1)
            W = group(u, "h0")
            for i in range(24):
                mm = pe.transpose(W[:, 32 * i:32 * i + 24], raws[0:24, P * i:P * i + P], ident[0:24, 0:24])
            mm.then_inc(S["work_ready"], 1)
            W = group(u, "h1")
            for i in range(12):
                pe.transpose(W[:, 24 * i:24 * i + 24], (rowG, rowB, rowlr)[i // 4][0:24, P * (i % 4):P * (i % 4) + P],
                             ident[0:24, 0:24])
            lru_rows = stage[0:32, :, :].rearrange("p e t -> p (e t)")
            for i in range(8):
                mm = pe.transpose(W[:, 512 + 32 * i:512 + 32 * i + 32], lru_rows[:, P * i:P * i + P], ident[0:32, 0:32])
            mm.then_inc(S["work_ready"], 1)
            pe.wait_ge(S["masks_loaded"], 16)
            fill(2 * SL)
            norm(0)
            for u in UNITS:
                if u[0] == "ab_rows":
                    columns_of_rows(u)
                elif u[0] == "dn":
                    dn(u[1])
                elif u[0] == "gla":
                    gla(u[1])
                else:
                    fill(first_slice("out0") + SL)
                    tail(u, (8, 8, 8), (0, 8, 16), (27, 27, 27))
            fill(first_slice("gate0") + 2 * SL)
            norm(1)
            gate(0)
            fill(first_slice("cd") + 2 * SL)
            norm(2)
            for u in UNITS_CD:
                if u[0] == "cd_rows":
                    W = group(u, "eg")
                    pe.wait_ge(S["eg_rows"], 1)
                    for h in range(SSD_H):
                        mm = pe.matmul(W[:, 12 * h:12 * h + 12], ident[0:SSD_H, h:h + 1].broadcast_to([SSD_H, P]),
                                  small[0:SSD_H, 16:28], start=True, stop=True)
                    mm.then_inc(S["work_ready"], 1)
                    columns_of_rows(u)
                elif u[0] == "bc":
                    bc()
                elif u[0] == "ssd":
                    ssd(u[1])
                elif u[0] == "lru":
                    lru(u[1])
                else:
                    fill(first_slice("out1") + SL)
                    tail(u, (8, 4, 8), (24, 32, 36), (27, 27, 36))
            fill(first_slice("gate1") + 2 * SL)
            norm(3)
            gate(1)
            norm(4)
            pe.wait_ge(S["y_done"], KT)
            for t in range(NT + 1):
                c0, n = tok(t)
                for i in range(2):
                    W = group(("final", 0), f"y{t}{i}")
                    for c in range(8):
                        mm = pe.transpose(W[0:n, P * c:P * c + P], hT(8 * i + c)[:, c0:c0 + n], ident[:, :])
                    mm.then_inc(S["work_ready"], 1)

        @block.scalar
        def _(act):
            at, chained, stores, split = [0], [0], [0], [0, 0]

            def link(ins):
                chained[0] += 1
                ins.then_inc(S["act_chain"], 1)
                act.wait_ge(S["act_chain"], chained[0])

            def split_hi(q):
                act.wait_ge(S[f"w_landed{q % NW}"], landed[q])
                if q >= NW:
                    act.wait_ge(S["slice_done"], KH * (q - NW + 1))
                act.copy(w_hi[:, q % NW], w_raw[:, q % NW]).then_inc(S["hi_ready"], 1)

            def store_tile(d):
                stores[0] = d + 1
                if d in staged:
                    i, e, n = staged[d]
                    act.wait_ge(S[f"dense_read{d % 2}"], d // 2 + 1)
                    act.dma_start(uT[i], stage[:, e, :]).then_inc(S[f"stage_stored{e}"], 16)

            def fill(to):
                while at[0] < to:
                    n = at[0]
                    if n % KH == 0 and n // KH + 2 < NSL // KH:
                        split_hi(n // KH + 2)
                    if n % SL == 3 and stores[0] < n // SL:
                        store_tile(n // SL - 1)
                    at[0] += 1
                if to in (end_slice("ab"), end_slice("cd")) and stores[0] < to // SL:
                    store_tile(to // SL - 1)

            def group(u, name):
                skip(u, name)
                g = NO[u, name]
                act.wait_ge(S["work_ready"], g + 1)
                return psw[g % 2]

            def skip(u, name):
                if (u, name) in early:
                    y_parts(*early[u, name])
                if (u, name) in target:
                    fill(target[u, name])

            def free(u):
                act.wait_ge(S["out_stored"], stored[u])

            def rstd_of(W, out, ready, value, done, ln):
                act.activation(out, W[:, 0:T], ACT.Ln, bias=cst[:, 0:1], scale=ready).then_inc(ln, 1)
                act.wait_ge(ln, value)
                act.activation(out, out, ACT.Exp, scale=-0.5).then_inc(done, 1)

            def square(i, c, before=None):
                if i % 2:
                    d = first[f"out{i // 2}"] + c
                    act.wait_ge(S[f"dense_read{d % 2}"], d // 2 + 1)
                elif i:
                    act.wait_ge(S["gate_done"], KT * (i // 2 - 1) + c + 1)
                if before:
                    before()
                if c >= 3:
                    act.wait_ge(S["sq_summed"], (KT - 2) * i + c - 2)
                dst = sbuf[:, T:2 * T] if c == 0 else extra[:, T * (2 + c % 2):T * (3 + c % 2)]
                act.activation(dst, hT(c), ACT.Square).then_inc(S["nrm_sq"], 1)

            def norm(i):
                W = group(("norm", i), "n")
                rstd_of(W, rstd[:, :], 1.0 / D_MODEL, i + 1, S["nrm_rstd"], S["nrm_ln"])

            def hi_part(ph, c, y=None):
                if ph:
                    act.wait_ge(S["slice_done"], first_slice(phases[ph]) - SL + c + 1)
                src = norm_scale(ph)
                if src is None:
                    act.copy(xh[:, c, :], y).then_inc(S["x_hi"], 1)
                else:
                    act.mul(xh[:, c, :], hT(c), src[:, c:c + 1]).then_inc(S["x_hi"], 1)

            def last_tile(ph, square_of):
                base = first_slice(phases[ph]) - SL
                fill(base + KH + 1)
                for c in range(KH):
                    hi_part(ph, c)
                fill(base + SL)
                for c in range(KH, KT - 1):
                    hi_part(ph, c)
                square_of(KT - 1, lambda: hi_part(ph, KT - 1))

            def rows_ab():
                fill(SL + 2)
                act.wait_ge(S["rows_loaded"], 16 * ROW_DMAS)
                act.wait_ge(S["h_stored"], 16)
                act.wait_ge(S["dense_read0"], 1)
                H = slice(0, DN_H)
                act.activation(rowB[H, :], rowlr[0:DN_H, :], ACT.Sigmoid).then_inc(S["rows_act"], 1)
                link(act.activation(slot(1)[H, :], rowlr[32:32 + DN_H, :], ACT.Identity))
                rows_tail(DN_H, 1, small[H, 0:1], small[H, 1:2], slot(1))

            def rows_tail(nh, n, bias, alog, a):
                H = slice(0, nh)
                link(act.activation(slot(2)[H, :], a[H, :], ACT.Abs, bias=bias))
                link(act.activation(slot(2)[H, :], slot(2)[H, :], ACT.Exp, scale=-1.0))
                act.activation(slot(2)[H, :], slot(2)[H, :], ACT.Ln, bias=cst[H, 1:2]).then_inc(S["rows_act"], 1)
                act.activation(small[H, 40:41], alog, ACT.Exp).then_inc(S["rows_act"], 1)
                act.wait_ge(S["rows_dve"], n)
                act.activation(slot(5)[H, :], rowG[H, :], ACT.Exp)
                act.activation(slot(6)[H, :], slot(6)[H, :], ACT.Exp).then_inc(S["rows_act"], 1)

            def columns_of_rows(u):
                W = group(u, "c0")
                act.copy(cols[:, 0:NT, :], tiles4(W[:, 0:SEQ]))
                act.copy(cols[0:NS, NT, :], W[0:NS, SEQ:SEQ + P]).then_inc(S["rows_copied"], 1)

            def decays(W, dst, col, done):
                for t in range(NT):
                    act.activation(dst[:, P * t:P * t + P], W[:, P * t:P * t + P], ACT.Exp, bias=cols[:, t, col:col + 1])
                act.activation(dst[0:NS, SEQ:T], W[0:NS, SEQ:T], ACT.Exp, bias=cols[0:NS, NT, col:col + 1]).then_inc(done, 1)

            def silu_squares(h):
                act.wait_ge(S["dn_conv"], h + 1)
                act.activation(slot(0, 3), slot(0, 3), ACT.Silu).then_inc(S["dn_silu"], 1)
                act.wait_ge(S["dn_silu"], h + 1)
                act.activation(slot(6, 2), slot(0, 2), ACT.Square).then_inc(S["dn_sq"], 1)

            def dn(h):
                u = ("dn", h)
                if h == 0:
                    fill(target[u, "start"])
                    act.wait_ge(S["rows_copied"], 1)
                    silu_squares(0)
                uu = extra[:, 0:640]
                W = group(u, "ssq")
                if h:
                    act.wait_ge(S["dn_y"], h)
                act.activation(slot(3), W[:, 0:T], ACT.Ln, bias=cst[:, 0:1]).then_inc(S["dn_ln"], 1)
                W = group(u, "ssk")
                act.activation(slot(4), W[:, 0:T], ACT.Ln, bias=cst[:, 0:1]).then_inc(S["dn_ln"], 1)
                act.wait_ge(S["dn_ln"], 3 * h + 2)
                act.activation(slot(3, 2), slot(3, 2), ACT.Exp, scale=-0.5).then_inc(S["dn_rs"], 1)
                W = group(u, "gbc")
                if h:
                    act.wait_ge(S["dn_s"], 4 * h)
                    act.wait_ge(S["dn_gs"], h)
                act.activation(slot(5), W[:, 0:T], ACT.Exp).then_inc(S["dn_eg"], 1)
                skip(u, "bbc")
                W = group(u, "dm")
                decays(W, slot(6), h, S["dn_D"])
                skip(u, "kk")
                skip(u, "qk")
                W = group(u, "t1")
                act.wait_ge(S["dn_kb"], h + 1)
                act.copy(slot(3)[:, 0:SEQ], W[:, 0:SEQ])
                act.copy(slot(3)[0:NS, SEQ:T], W[0:NS, SEQ:T]).then_inc(S["dn_t1"], 1)
                for n, _, _ in dn_groups()[8:27]:
                    if n != "wk":
                        skip(u, n)
                W = group(u, "wk")
                act.mul(slot(3), W[:, 0:T], -1.0).then_inc(S["dn_nwk"], 1)

                def u_copy(t):
                    W = group(u, f"u{t}")
                    act.copy(uu[:, P * t:P * t + P], W[:, 0:P]).then_inc(S["dn_u"], 1)

                u_copy(0)
                W = group(u, "us")
                act.copy(uu[0:NS, SEQ:SEQ + P], W[0:NS, 0:P]).then_inc(S["dn_u"], 1)
                skip(u, "s0")
                skip(u, "ss")
                for t in range(1, NT):
                    u_copy(t)
                    skip(u, f"s{t}")
                z = raws[:, 3 * T:4 * T]
                act.wait_ge(S["z_loaded"], zloads[u])
                act.activation(z, z, ACT.Silu).then_inc(S["dn_z"], 1)
                W = group(u, "o")
                act.activation(slot(4), W[:, 0:T], ACT.Square).then_inc(S["dn_osq"], 1)
                W = group(u, "n")
                rstd_of(W, slot(3), 1.0 / P, 3 * h + 3, S["dn_rstd"], S["dn_ln"])
                if h + 1 < DN_H:
                    silu_squares(h + 1)

            def gate_logs(u, name, h):
                W = group(u, name)
                act.activation(slot(5), W[:, 0:T], ACT.Abs, bias=pvc("gla_ba", h)).then_inc(S["gl_abs"], 1)
                act.wait_ge(S["gl_abs"], h + 1)
                link(act.activation(slot(5), slot(5), ACT.Exp, scale=-1.0))
                act.activation(slot(5), slot(5), ACT.Ln, bias=cst[:, 1:2]).then_inc(S["gl_l"], 1)

            def gate_exps(h):
                act.wait_ge(S["gl_G"], h + 1)
                if h:
                    act.wait_ge(S["gl_s"], h)
                    act.wait_ge(S["gl_gs"], h)
                act.activation(slot(4), slot(3), ACT.Exp, scale=1.0 / 16).then_inc(S["gl_eg"], 1)
                act.wait_ge(S["gl_kd"], h + 1)
                act.activation(slot(5), slot(5), ACT.Exp, scale=1.0 / 16).then_inc(S["gl_kf"], 1)

            def gla(h):
                u = ("gla", h)
                kend = arena[:, 12 * T:12 * T + 640]
                vt = arena[:, 12 * T + 640:12 * T + 1920].rearrange("p (t e) -> p t e", t=NT + 1)
                act.wait_ge(S["u_loaded"], loads[u])
                act.mul(raws[:, 0:T], raws[:, 0:T], float(P) ** -0.5).then_inc(S["gl_q"], 1)
                if h == 0:
                    fill(target[u, "start"])
                    free(u)
                    gate_logs(u, "lg", 0)
                    gate_exps(0)
                skip(u, "qk")
                for l in range(7):
                    E = slot((8, 2)[l % 2])
                    act.wait_ge(S["gl_ed"], 7 * h + l + 1)
                    act.activation(E, E, ACT.Exp, scale=1.0 / 16).then_inc(S["gl_E"], 1)
                    skip(u, f"l{l}")
                W = group(u, "kt")
                act.copy(kend[:, 0:SEQ], W[:, 0:SEQ])
                act.copy(kend[0:NS, SEQ:SEQ + P], W[0:NS, SEQ:SEQ + P]).then_inc(S["gl_kend"], 1)
                for e in range(2):
                    W = group(u, f"v{e}")
                    ec = slice(P * e, P * e + P)
                    act.copy(vt[:, 0:NT, ec], tiles4(W[:, 0:SEQ]))
                    act.copy(vt[0:NS, NT, ec], W[0:NS, SEQ:SEQ + P]).then_inc(S["gl_v"], 1)
                act.wait_ge(S["z_loaded"], zloads[u])
                act.activation(raws[:, 4 * T:6 * T], raws[:, 4 * T:6 * T], ACT.Silu).then_inc(S["gl_z"], 1)
                skip(u, "sA")
                for e in range(2):
                    W = group(u, f"o{e}")
                    act.activation(slot(9 + e), W[:, 0:T], ACT.Square).then_inc(S["gl_osq"], 1)
                if h + 1 < GLA_H:
                    gate_logs(u, "lgn", h + 1)
                skip(u, "sb0")
                skip(u, "sb1")
                if h + 1 < GLA_H:
                    gate_exps(h + 1)
                W = group(u, "n")
                rstd_of(W, slot(2), 1.0 / 256, h + 1, S["gl_rstd"], S["gl_ln"])

            def bc():
                u = ("bc", 0)
                fill(target[u, "start"])
                Bt = arena[:, 8 * T:8 * T + 1280].rearrange("p (t n) -> p t n", t=NT + 1)
                fill((target[u, "start"] + target[u, "bt"]) // 2)
                act.wait_ge(S["bc_conv"], 1)
                act.activation(slot(0, 4), slot(0, 4), ACT.Silu).then_inc(S["bc_silu"], 1)
                W = group(u, "bt")
                act.copy(Bt[:, 0:NT, :], W[:, :].rearrange("p (t n) -> p t n", t=NT)).then_inc(S["bc_b"], 1)
                W = group(u, "bts")
                act.copy(Bt[0:NS, NT, :], W[0:NS, 0:256]).then_inc(S["bc_b"], 1)
                for g in range(SSD_G):
                    W = group(u, f"cb{g}")
                    act.copy(slot(4 + g)[:, 0:SEQ], W[:, 0:SEQ])
                    act.copy(slot(4 + g)[0:NS, SEQ:T], W[0:NS, SEQ:T]).then_inc(S["bc_cb"], 1)

            def ssd(p):
                u = ("ssd", p)
                if p == 0:
                    fill(target[u, "start"])
                    free(u)
                    act.wait_ge(S["sp_conv"], 1)
                    act.activation(ssd_x(0), ssd_x(0), ACT.Silu).then_inc(S["sp_silu"], 1)
                    act.wait_ge(S["rows_copied"], 3)
                    act.wait_ge(S["bc_cb"], 4)
                for i, n in enumerate(("dmA", "dmB")):
                    W = group(u, n)
                    decays(W, slot(i), 2 * p + i, S["sp_D"])
                W = group(u, "ebc")
                act.activation(arena[:, 6176:6176 + T], W[:, 0:T], ACT.Exp).then_inc(S["sp_ebc"], 1)
                act.wait_ge(S["z_loaded"], zloads[u])
                act.activation(raws[:, T:2 * T], raws[:, T:2 * T], ACT.Silu).then_inc(S["sp_z"], 1)
                for n in ("xt", "sP", "ss", "i"):
                    skip(u, n)
                if p + 1 < SSD_H // 2:
                    act.wait_ge(S["sp_conv"], p + 2)
                    act.activation(ssd_x(p + 1), ssd_x(p + 1), ACT.Silu).then_inc(S["sp_silu"], 1)
                skip(u, "o")
                act.wait_ge(S["sp_y"], p + 1)
                e = p % 2
                act.activation(raws[:, T * (2 + e):T * (3 + e)], extra[:, 1024 + T * e:1024 + T * (e + 1)],
                               ACT.Square).then_inc(S["sp_sq"], 1)
                if e:
                    W = group(u, "n")
                    rstd_of(W, raws[:, 5 * T:6 * T], 1.0 / 256, p // 2 + 1, S["sp_rstd"], S["sp_ln"])

            def lru(j):
                u = ("lru", j)
                if j == 0:
                    fill(target[u, "start"])
                free(("lru", max(j - 1, 0)))
                W = group(u, "r")
                act.activation(lru_slot(j, 1), W[:, 0:T], ACT.Sigmoid, bias=pvc("lru_ba", j)).then_inc(S["lr_r"], 1)
                W = group(u, "i")
                act.activation(lru_slot(j, 2), W[:, 0:T], ACT.Sigmoid, bias=pvc("lru_bx", j)).then_inc(S["lr_i"], 1)
                act.wait_ge(S["lr_r"], j + 1)
                act.activation(lru_slot(j, 3), lru_slot(j, 1), ACT.Exp, scale=small[:, 48 + j:49 + j])
                act.activation(lru_slot(j, 4), lru_slot(j, 1), ACT.Tanh, scale=small[:, 56 + j:57 + j]).then_inc(S["lr_a"], 1)
                act.wait_ge(S["z_loaded"], zloads[u])
                act.activation(raws[:, T:2 * T], raws[:, T:2 * T], ACT.Silu).then_inc(S["lr_z"], 1)
                if j + 1 < LRU_W // P:
                    fill((target[u, "i"] + target[("lru", j + 1), "r"]) // 2)
                act.wait_ge(S["lr_t"], j + 1)
                act.activation(lru_slot(j, 5), lru_slot(j, 5), ACT.Sqrt).then_inc(S["lr_sq"], 1)

            def tail(u, first_group):
                for n in range(3):
                    rows = 36 if (u[0], n) == ("cd_tail", 2) else 27
                    W = group(u, f"t{n}")
                    if n == 0:
                        free(u)
                    act.copy(raws[0:rows, 1024 * n:1024 * n + 1024] if (u[0], n) != ("cd_tail", 1) else
                             raws[0:rows, 1024:1536], W[0:rows, 0:1024] if (u[0], n) != ("cd_tail", 1) else
                             W[0:rows, 0:512]).then_inc(S["tail_copied"], 1)

            def y_load(layer, k):
                nb = Y_BUFS[layer]
                e = k % nb
                if k == 0:
                    act.wait_ge(S["out_stored"], stored[LAST[0]] if layer == 0 else stored["lru", 6])
                if k < 2:
                    act.wait_ge(S[f"stage_stored{e}"], max(n for d, (_, f, n) in staged.items()
                                                           if f == e and (layer or d < first["out0"])))
                if k >= nb:
                    act.wait_ge(S["x_ready"], KT * (1 + 3 * layer) + k - nb + 1)
                act.dma_start(y_source(layer, k), yT[k]).then_inc(S[f"y_in{e}"], 16)

            def y_parts(layer, to):
                nb = Y_BUFS[layer]
                while split[layer] < to:
                    k = split[layer]
                    if k == 0:
                        for n in range(nb - 1):
                            y_load(layer, n)
                    if k + nb - 1 < KT - 2:
                        y_load(layer, k + nb - 1)
                    if k < KT - 2:
                        act.wait_ge(S[f"y_in{k % nb}"], 16 * (k // nb + 1 + (7 if layer and k % nb < 2 else 0)))
                    elif layer == 0:
                        act.wait_ge(S["gl_y"], GLA_H)
                    else:
                        act.wait_ge(S["lr_y"], k - 7)
                    hi_part(1 + 3 * layer, k, y_source(layer, k))
                    split[layer] += 1

            def out_proj(layer):
                for c in range(KT):
                    if c < KT - 1:
                        fill(SL * (first[f"out{layer}"] + c + 1))
                    if c:
                        square(2 * layer + 1, c - 1)
                last_tile(2 + 3 * layer, lambda c, f: square(2 * layer + 1, c, f))

            def sigmoid(layer, c):
                d = first[f"gate{layer}"] + c
                act.wait_ge(S[f"dense_read{d % 2}"], d // 2 + 1)
                e = extra[:, T * (c % 2):T * (c % 2) + T]
                act.activation(e, e, ACT.Sigmoid).then_inc(S["gate_sig"], 1)

            def gate(layer):
                u = ("gate", layer)
                pT = raws[:, 1280:1280 + 2 * T].rearrange("p (k t) -> p k t", k=2)
                for i in range(2):
                    W = group(u, f"p{i}")
                    act.copy(pT[:, i, :], W[:, 0:T]).then_inc(S["in_copied"], 1)
                for c in range(KT):
                    d = first[f"gate{layer}"] + c
                    if c < KT - 1:
                        fill(SL * (d + 1))
                    elif layer == 0:
                        square(2, c - 1)
                        last_tile(3, lambda c, f: (sigmoid(0, c), square(2, c, f)))
                        return
                    else:
                        fill(SL * (d + 1))
                    sigmoid(layer, c)
                    if c:
                        square(2 * layer + 2, c - 1)
                square(2 * layer + 2, KT - 1)

            act.dma_start(ident[:, :], I["cf"]).then_inc(S["consts_loaded"], 16)
            act.wait_ge(S["consts_set"], 1)
            act.wait_ge(S["zeroed"], 1)
            u = ("setup", 0)
            for t in range(NT + 1):
                c0, n = tok(t)
                for i in range(2):
                    W = group(u, f"x{t}{i}")
                    dst = arena[:, :].rearrange("p (c t) -> p c t", c=KT)[:, 8 * i:8 * i + 8, c0:c0 + n]
                    act.copy(dst, W[:, :].rearrange("p (c t) -> p c t", c=8)[:, :, 0:n]).then_inc(S["in_copied"], 1)
            split_hi(0)
            split_hi(1)
            W = group(u, "pv")
            act.copy(pv[:, 0:88], W[:, 0:88])
            act.copy(pv[:, P:P + 103], W[:, P:P + 103])
            act.copy(pv[:, 2 * P:2 * P + 124], W[:, 2 * P:2 * P + 124]).then_inc(S["in_copied"], 1)
            W = group(u, "h0")
            act.copy(hist[:, 0:24, 0:24], W[:, 0:768].rearrange("p (i r) -> p i r", i=24)[:, :, 0:24]).then_inc(S["in_copied"], 1)
            W = group(u, "h1")
            act.copy(hist[:, 24:36, 0:24], W[:, 0:288].rearrange("p (i r) -> p i r", i=12))
            act.copy(hist[:, 36:44, 0:32], W[:, 512:768].rearrange("p (i r) -> p i r", i=8)).then_inc(S["in_copied"], 1)
            act.wait_ge(S["in_copied"], 2 * (NT + 1) + 1)
            lam = pvc("lru_lambda", 0, 8)
            link(act.activation(small[:, 48:56], lam, ACT.Abs))
            link(act.activation(small[:, 48:56], small[:, 48:56], ACT.Exp, scale=-1.0))
            act.activation(small[:, 48:56], small[:, 48:56], ACT.Ln, bias=cst[:, 1:2]).then_inc(S["rows_act"], 1)
            act.wait_ge(S["in_copied"], 3 + 2 * (NT + 1))
            for c in range(KT):
                hi_part(0, c)
            for c in range(KT):
                square(0, c)
            fill(SL)
            norm(0)
            for u in UNITS:
                if u[0] == "ab_rows":
                    rows_ab()
                    columns_of_rows(u)
                elif u[0] == "dn":
                    dn(u[1])
                elif u[0] == "gla":
                    gla(u[1])
                else:
                    fill(target[u, "start"])
                    y_parts(0, KT)
                    fill(first_slice("out0") + SL)
                    tail(u, 0)
            out_proj(0)
            fill(first_slice("gate0") + SL)
            norm(1)
            gate(0)
            fill(first_slice("cd") + SL)
            norm(2)
            for u in UNITS_CD:
                if u[0] == "cd_rows":
                    fill(first_slice("cd") + SL + 2)
                    act.wait_ge(S["h_stored"], 32)
                    act.wait_ge(S[f"dense_read{first['cd'] % 2}"], first["cd"] // 2 + 1)
                    H = slice(0, SSD_H)
                    rows_tail(SSD_H, 2, small[H, 10:11], small[H, 11:12], rowlr)
                    act.activation(small[H, 16:20], rowG[H, 0:SEQ].rearrange("p (t i) -> p t i", t=NT)[:, :, P - 1], ACT.Exp)
                    act.activation(small[H, 20:28], rowG[H, SEQ:T].rearrange("p (b i) -> p b i", b=NB)[:, :, LS - 1],
                                   ACT.Exp).then_inc(S["eg_rows"], 1)
                    W = group(u, "eg")
                    act.copy(egt[:, 0:SSD_H * 12], W[:, 0:SSD_H * 12]).then_inc(S["rows_copied"], 1)
                    columns_of_rows(u)
                elif u[0] == "bc":
                    bc()
                elif u[0] == "ssd":
                    ssd(u[1])
                elif u[0] == "lru":
                    lru(u[1])
                else:
                    y_parts(1, KT)
                    fill(first_slice("out1") + SL)
                    tail(u, 3)
            out_proj(1)
            fill(first_slice("gate1") + SL)
            norm(3)
            gate(1)
            norm(4)
            for t in range(NT + 1):
                _, n = tok(t)
                dst = raws if t % 2 == 0 else sbuf
                for i in range(2):
                    W = group(("final", 0), f"y{t}{i}")
                    if t >= 2 and i == 0:
                        act.wait_ge(S[f"y_stored{t % 2}"], 16 * (t // 2))
                    act.copy(dst[0:n, 1024 * i:1024 * i + 1024], W[0:n, :]).then_inc(S["out_copied"], 1)

        @block.vector
        def _(dve):
            at, chained, evac, split = [0], [0], [0], [0, 0]

            def go(ins):
                chained[0] += 1
                ins.then_inc(S["dve_chain"], 1)

            def wait_chain():
                dve.wait_ge(S["dve_chain"], chained[0])

            def link(ins):
                go(ins)
                wait_chain()

            def split_lo(q):
                dve.wait_ge(S["hi_ready"], q + 1)
                dve.tensor_tensor(w_lo[:, q % NW], w_raw[:, q % NW], w_hi[:, q % NW].bitcast(F32),
                                  ALU.subtract).then_inc(S["lo_ready"], 1)

            def evacuate(d):
                evac[0] = d + 1
                if TILES[d][3] not in ("ab", "cd"):
                    return
                dve.wait_ge(S["slice_done"], SL * (d + 1))
                dst = rowlr[:, :]
                if d in staged:
                    _, e, n = staged[d]
                    dst = stage[:, e, :]
                    if n > 16:
                        dve.wait_ge(S[f"stage_stored{e}"], n - 16)
                if d in (first["ab"], first["cd"]):
                    dve.wait_ge(S["nrm_rstd"], 1 if d == first["ab"] else 3)
                dve.tensor_tensor(dst, psd[d % 2][:, D0:D0 + T], rstd[:, :], ALU.mult)\
                   .then_inc(S[f"dense_read{d % 2}"], 1)

            def fill(to):
                while at[0] < to:
                    n = at[0]
                    if n % KH == 0 and n // KH + 2 < NSL // KH:
                        split_lo(n // KH + 2)
                    if n % SL == 1 and evac[0] < n // SL:
                        evacuate(n // SL - 1)
                    at[0] += 1
                if to in (end_slice("ab"), end_slice("cd")) and evac[0] < to // SL:
                    evacuate(to // SL - 1)

            def group(u, name):
                skip(u, name)
                g = NO[u, name]
                dve.wait_ge(S["work_ready"], g + 1)
                return psw[g % 2]

            def skip(u, name):
                if (u, name) in early:
                    y_parts(*early[u, name])
                if (u, name) in target:
                    fill(target[u, name])

            def free(u):
                dve.wait_ge(S["out_stored"], stored[u])

            def lo_part(ph, c, y=None):
                dve.wait_ge(S["x_hi"], KT * ph + c + 1)
                src = norm_scale(ph)
                if src is None:
                    dve.tensor_tensor(xl[:, c, :], y, xh[:, c, :].bitcast(F32), ALU.subtract).then_inc(S["x_ready"], 1)
                else:
                    dve.scalar_tensor_tensor(xl[:, c, :], hT(c), src[:, c:c + 1], xh[:, c, :].bitcast(F32), ALU.mult,
                                             ALU.subtract).then_inc(S["x_ready"], 1)

            def last_tile(ph):
                base = first_slice(phases[ph]) - SL
                fill(base + KH + 1)
                for c in range(KH):
                    lo_part(ph, c)
                fill(base + SL)
                for c in range(KH, KT - 1):
                    lo_part(ph, c)

            def final_norm():
                g = pvc("final_norm", 0, 16)
                dve.wait_ge(S["nrm_rstd"], 5)
                for c in range(KT):
                    dve.scalar_tensor_tensor(hT(c), hT(c), g[:, c:c + 1], rstd[:, :], ALU.mult, ALU.mult)\
                       .then_inc(S["y_done"], 1)

            def conv_tap(n, tap, samples, wcol, bcol, dst, done, src=0):
                if tap:
                    wait_chain()
                for i in range(n):
                    w = wcol(i, TAPS - 1 - tap)
                    if samples:
                        y = dst(i)[:, SEQ:T].rearrange("p (b s) -> p b s", b=NB)
                        x = smp[:, i, :, TAPS - 1 - tap:TAPS - 1 - tap + LS]
                    else:
                        y = dst(i)[:, tap:SEQ]
                        x = raws[:, T * (src + i):T * (src + i) + SEQ - tap]
                    if tap == 0:
                        go(dve.tensor_scalar(y, x, w, bcol(i) if bcol else None, ALU.mult, *([ALU.add] if bcol else [])))
                    elif samples and tap == TAPS - 1 and i == n - 1:
                        dve.scalar_tensor_tensor(y, x, w, y, ALU.mult, ALU.add).then_inc(done, 1)
                    else:
                        go(dve.scalar_tensor_tensor(y, x, w, y, ALU.mult, ALU.add))

            def conv(n, wcol, bcol, dst, smp_ready, value, done, src=0):
                for tap in range(TAPS):
                    conv_tap(n, tap, False, wcol, bcol, dst, done, src)
                dve.wait_ge(smp_ready, value)
                for tap in range(TAPS):
                    conv_tap(n, tap, True, wcol, bcol, dst, done, src)
                wait_chain()

            def by_token(dst, W, col, width=P, nh=1, done=None):
                w = width // nh

                def view(ap, t):
                    return ap.rearrange("p (t h e) -> p t h e", t=t, h=nh)
                a = dve.tensor_tensor(view(dst[:, 0:SEQ], NT), view(W[:, 0:SEQ], NT),
                                      cols[:, 0:NT, col:col + nh].unsqueeze(3).broadcast_to([P, NT, nh, w]), ALU.mult)
                go(a)
                b = dve.tensor_tensor(view(dst[0:NS, SEQ:SEQ + P], 1), view(W[0:NS, SEQ:SEQ + P], 1),
                                      cols[0:NS, NT:NT + 1, col:col + nh].unsqueeze(3).broadcast_to([NS, 1, nh, w]), ALU.mult)
                if done is None:
                    go(b)
                else:
                    b.then_inc(done, 1)

            def masked(dst, W, mask, done, samples=True):
                a = dve.tensor_tensor(tiles4(dst[:, 0:SEQ]), tiles4(W[:, 0:SEQ]), bc4(mask), ALU.mult)
                if samples:
                    go(a)
                    a = dve.tensor_tensor(dst[0:NS, SEQ:T], W[0:NS, SEQ:T], mask[0:NS, 0:NS], ALU.mult)
                if done is None:
                    go(a)
                else:
                    a.then_inc(done, 1)

            def minus(dst, W, samples, done):
                a = dve.tensor_tensor(dst[:, 0:SEQ], dst[:, 0:SEQ], W[:, 0:SEQ], ALU.subtract)
                if samples:
                    go(a)
                    a = dve.tensor_tensor(dst[0:NS, SEQ:T], dst[0:NS, SEQ:T], W[0:NS, SEQ:T], ALU.subtract)
                a.then_inc(done, 1)

            def cumsum(rows, src, dst, done):
                return dve.tensor_tensor_scan(dst, rmask[0:rows, :], src, 0.0, ALU.mult, ALU.add)

            def to_chunk_end(rows, dst, G, done):
                for a, b, n, m in ((0, SEQ, NT, P), (SEQ, T, NB, LS)):
                    g = G[0:rows, a:b].rearrange("p (t i) -> p t i", t=n)
                    ins = dve.tensor_tensor(dst[0:rows, a:b].rearrange("p (t i) -> p t i", t=n),
                                            g[:, :, m - 1:m].broadcast_to([rows, n, m]), g, ALU.subtract)
                    if b == T:
                        ins.then_inc(done, 1)
                    else:
                        go(ins)

            def rows_g(nh, n, bias, a):
                H = slice(0, nh)
                dve.wait_ge(S["rows_act"], 4 if n == 1 else 7)
                link(dve.tensor_scalar(slot(3)[H, :], a[H, :], bias, 0.0, ALU.add, ALU.max))
                link(dve.tensor_tensor(slot(3)[H, :], slot(3)[H, :], slot(2)[H, :], ALU.add))
                link(dve.tensor_scalar(slot(4)[H, :], slot(3)[H, :], small[H, 40:41], -1.0, ALU.mult, ALU.mult))
                link(cumsum(nh, slot(4)[H, :], rowG[H, :], None))
                to_chunk_end(nh, slot(6), rowG, S["rows_dve"])

            def rows_ab():
                fill(SL + 2)
                dve.wait_ge(S["h_stored"], 16)
                dve.memset(slot(0), 0.0).then_inc(S["dve_chain"], 1)
                chained[0] += 1
                H = slice(0, DN_H)
                dve.wait_ge(S["rows_act"], 4)
                wait_chain()
                rows_g(DN_H, 1, small[H, 0:1], slot(1))
                go(dve.tensor_scalar(slot(0)[0:DN_H, :], rowG[H, :], -1.0, None, ALU.mult))
                go(dve.tensor_copy(slot(0)[32:32 + DN_H, :], rowB[H, :]))
                dve.wait_ge(S["rows_act"], 5)
                go(dve.tensor_tensor(slot(0)[64:64 + DN_H, :], rowB[H, :], slot(5)[H, :], ALU.mult))
                go(dve.tensor_copy(slot(0)[96:96 + DN_H, :], slot(6)[H, :]))
                wait_chain()
                dve.tensor_scalar(small[:, 41:42], cst[:, 1:2], 1.0, None, ALU.mult).then_inc(S["rows_ready"], 1)

            def rows_cd():
                fill(first_slice("cd") + SL + 2)
                dve.wait_ge(S["h_stored"], 32)
                link(dve.memset(slot(0), 0.0))
                H = slice(0, SSD_H)
                dve.wait_ge(S["rows_act"], 7)
                rows_g(SSD_H, 2, small[H, 10:11], rowlr)
                go(dve.tensor_scalar(slot(0)[0:SSD_H, :], rowG[H, :], -1.0, None, ALU.mult))
                go(dve.tensor_copy(slot(0)[32:32 + SSD_H, :], slot(3)[H, :]))
                dve.wait_ge(S["rows_act"], 8)
                go(dve.tensor_tensor(slot(0)[64:64 + SSD_H, :], slot(3)[H, :], slot(6)[H, :], ALU.mult))
                wait_chain()
                dve.tensor_scalar(small[:, 41:42], cst[:, 1:2], 1.0, None, ALU.mult).then_inc(S["rows_ready"], 1)

            def dn_conv(h, tap, samples=False):
                steps = range(tap, TAPS) if h == 0 else (tap,)
                for tap in steps:
                    conv_tap(3, tap, samples, lambda i, w: pvc("dn_conv_w", 24 * w + 8 * i + h), None, slot, S["dn_conv"])

            def dn(h):
                u = ("dn", h)
                if h == 0:
                    fill(target[u, "start"])
                q, k = slot(0), slot(1)
                Tm, X, eG, Dm, kb, qg, AT, QKT, TT = (slot(i) for i in range(3, 12))
                bgk, kend, bv = (arena[:, 12 * T + 640 * i:12 * T + 640 * (i + 1)] for i in range(3))
                nwk = slot(3)
                mwk = arena[:, 12 * T + 1920:12 * T + 1920 + 256].rearrange("p (b i) -> p b i", b=NB)
                uu, SS = extra[:, 0:640], extra[:, 640:640 + 512]
                um = extra[0:NS, 1152:2176].rearrange("p (b e) -> p b e", b=NB)
                Snew = sbuf[:, 1024:2048]
                if h == 0:
                    dve.wait_ge(S["u_loaded"], loads[u])
                    dve.wait_ge(S["rows_copied"], 1)
                    dn_conv(0, 0)
                    dve.wait_ge(S["dn_smp"], 1)
                    dn_conv(0, 0, samples=True)
                for n in ("ssq", "ssk", "gbc"):
                    skip(u, n)
                dve.wait_ge(S["dn_rs"], h + 1)
                go(dve.scalar_tensor_tensor(q, q, float(P) ** -0.5, slot(3), ALU.mult, ALU.mult))
                link(dve.tensor_tensor(k, k, slot(4), ALU.mult))
                dve.wait_ge(S["dn_eg"], h + 1)
                go(dve.tensor_tensor(qg, q, eG, ALU.mult))
                W = group(u, "bbc")
                dve.tensor_tensor(kb, k, W[:, 0:T], ALU.mult).then_inc(S["dn_kb"], 1)
                skip(u, "dm")
                W = group(u, "kk")
                dve.wait_ge(S["dn_D"], h + 1)
                free(u)
                go(dve.tensor_tensor(AT[:, 0:SEQ], W[:, 0:SEQ], Dm[:, 0:SEQ], ALU.mult))
                dve.tensor_tensor(AT[0:NS, SEQ:T], W[0:NS, SEQ:T], Dm[0:NS, SEQ:T], ALU.mult).then_inc(S["dn_at"], 1)
                dve.wait_ge(S["dn_at"], h + 1)
                masked(X, AT, MT[:, 0, :], None)
                wait_chain()
                go(dve.tensor_tensor(tiles4(TT[:, 0:SEQ]), bc4(ident[:, :]), tiles4(X[:, 0:SEQ]), ALU.subtract))
                dve.tensor_tensor(TT[0:NS, SEQ:T], ident[0:NS, 0:NS], X[0:NS, SEQ:T], ALU.subtract).then_inc(S["dn_tt1"], 1)
                W = group(u, "qk")
                go(dve.tensor_tensor(QKT[:, 0:SEQ], W[:, 0:SEQ], Dm[:, 0:SEQ], ALU.mult))
                dve.tensor_tensor(QKT[0:NS, SEQ:T], W[0:NS, SEQ:T], Dm[0:NS, SEQ:T], ALU.mult).then_inc(S["dn_qkt"], 1)
                skip(u, "t1")
                W = group(u, "kt")
                by_token(bgk, W, 64 + h)
                by_token(kend, W, 96 + h, done=S["dn_kend"])
                W = group(u, "vt")
                by_token(bv, W, 32 + h, done=S["dn_bv"])
                for l in range(1, 7):
                    W = group(u, f"x{l}")
                    masked(X, W, MX[:, l, :], S["dn_x"], samples=l == 1)
                    if l < 6:
                        W = group(u, f"y{l}")
                        if l == 1:
                            dve.wait_ge(S["dn_t1"], h + 1)
                        minus(Tm, W, l == 1, S["dn_t"])
                    W = group(u, f"yt{l}")
                    minus(TT, W, l == 1, S["dn_tt"])
                skip(u, "wk")
                dve.wait_ge(S["dn_nwk"], h + 1)
                dve.tensor_tensor(mwk, nwk[:, SEQ:T].unsqueeze(1).broadcast_to([P, NB, NS]), bmask, ALU.mult)\
                   .then_inc(S["dn_mwk"], 1)
                skip(u, "u0")
                skip(u, "us")
                dve.wait_ge(S["dn_u"], 5 * h + 2)
                dve.tensor_tensor(um, uu[0:NS, SEQ:SEQ + P].unsqueeze(1).broadcast_to([NS, NB, P]),
                                  rowm.unsqueeze(2).broadcast_to([NS, NB, P]), ALU.mult).then_inc(S["dn_um"], 1)

                def s_step(t):
                    W = group(u, f"s{t}")
                    if t == 0:
                        dve.tensor_copy(SS[:, 0:P], W[:, 0:P]).then_inc(S["dn_s"], 1)
                    else:
                        dve.wait_ge(S["dn_s"], 4 * h + t)
                        dve.scalar_tensor_tensor(SS[:, P * t:P * t + P], SS[:, P * (t - 1):P * t],
                                                 eG[:, P * t + P - 1:P * t + P], W[:, 0:P], ALU.mult,
                                                 ALU.add).then_inc(S["dn_s"], 1)

                s_step(0)
                W = group(u, "ss")
                dve.wait_ge(S["dn_gs"], h + 1)
                dve.tensor_tensor(Snew, Snew, W[:, 0:1024], ALU.add).then_inc(S["dn_snew"], 1)
                ahead = h + 1 < DN_H
                if ahead:
                    dve.wait_ge(S["u_loaded"], loads["dn", h + 1])
                    dn_conv(h + 1, 0)
                for t in range(1, NT):
                    skip(u, f"u{t}")
                    s_step(t)
                    if ahead:
                        dn_conv(h + 1, t)
                if ahead:
                    dve.wait_ge(S["dn_smp"], h + 2)
                    for tap in range(TAPS):
                        dn_conv(h + 1, tap, samples=True)
                W = group(u, "o")
                dve.wait_ge(S["dn_osq"], h + 1)
                dve.wait_ge(S["dn_z"], h + 1)
                dve.scalar_tensor_tensor(slot(9), W[:, 0:T], pvc("dn_norm", 0), raws[:, 3 * T:4 * T], ALU.mult,
                                         ALU.mult).then_inc(S["dn_o1"], 1)
                skip(u, "n")
                dve.wait_ge(S["dn_rstd"], h + 1)
                dve.wait_ge(S["dn_o1"], h + 1)
                dve.tensor_tensor(slot(9), slot(9), slot(3), ALU.mult).then_inc(S["dn_y"], 1)

            def gla(h):
                u = ("gla", h)
                if h == 0:
                    fill(target[u, "start"])
                    free(u)
                q, k = raws[:, 0:T], raws[:, T:2 * T]
                G, eG, kf, qg, kendT, qt, kt, AT = slot(3), slot(4), slot(5), slot(6), slot(7), slot(9), slot(10), slot(11)
                vt = arena[:, 12 * T + 640:12 * T + 1920].rearrange("p (t e) -> p t e", t=NT + 1)
                SS = extra[:, 0:1024].rearrange("p (t e) -> p t e", t=NT)
                um = extra[0:NS, 1024:2048].rearrange("p (b e) -> p b e", b=4)

                def gates(u, name, h):
                    W = group(u, name)
                    dve.wait_ge(S["gl_abs"], h + 1)
                    dve.tensor_scalar(slot(7), W[:, 0:T], pvc("gla_ba", h), 0.0, ALU.add, ALU.min).then_inc(S["gl_m"], 1)

                def gate_sums(h):
                    dve.wait_ge(S["gl_m"], h + 1)
                    dve.wait_ge(S["gl_l"], h + 1)
                    link(dve.tensor_tensor(slot(7), slot(7), slot(5), ALU.subtract))
                    cumsum(P, slot(7), G, None).then_inc(S["gl_G"], 1)
                    dve.wait_ge(S["gl_G"], h + 1)
                    to_chunk_end(P, kf, G, S["gl_kd"])

                if h == 0:
                    gates(u, "lg", 0)
                    gate_sums(0)

                def exponents(l):
                    s = 1 << l
                    E = slot((8, 2)[l % 2])
                    w = T if l < 2 else SEQ
                    g = G[:, 0:w].rearrange("p (n i) -> p n i", i=2 * s)
                    e = E[:, 0:w].rearrange("p (n i) -> p n i", i=2 * s)
                    ref = g[:, :, s - 1:s].broadcast_to([P, w // (2 * s), s])
                    go(dve.tensor_tensor(e[:, :, 0:s], ref, g[:, :, 0:s], ALU.subtract))
                    if l >= 2:
                        dve.tensor_tensor(e[:, :, s:], g[:, :, s:], ref, ALU.subtract).then_inc(S["gl_ed"], 1)
                    else:
                        dve.tensor_tensor(e[:, :, s:], g[:, :, s:], ref, ALU.subtract).then_inc(S["gl_ed"], 1)

                if h == 0:
                    exponents(0)
                dve.wait_ge(S["gl_q"], h + 1)
                dve.wait_ge(S["gl_eg"], h + 1)
                go(dve.tensor_tensor(qg, q, eG, ALU.mult))
                dve.wait_ge(S["gl_kf"], h + 1)
                dve.tensor_tensor(kendT, k, kf, ALU.mult).then_inc(S["gl_qg"], 1)
                W = group(u, "qk")
                masked(AT, W, ident[:, :], S["gl_at"])
                free(u)
                if h:
                    dve.wait_ge(S["gl_y"], h)
                for l in range(7):
                    if l < 6:
                        exponents(l + 1)
                    s = 1 << l
                    w = T if l < 2 else SEQ
                    E = slot((8, 2)[l % 2])
                    dve.wait_ge(S["gl_E"], 7 * h + l + 1)

                    def part(ap, lo):
                        return ap[:, 0:w].rearrange("p (n i) -> p n i", i=2 * s)[:, :, lo:lo + s]
                    go(dve.tensor_tensor(part(qt, s), part(q, s), part(E, s), ALU.mult))
                    dve.tensor_tensor(part(kt, 0), part(k, 0), part(E, 0), ALU.mult).then_inc(S["gl_qkt"], 1)
                    W = group(u, f"l{l}")
                    dve.wait_ge(S["gl_at"], 8 * h + l + 1)
                    if l < 2:
                        go(dve.copy_predicated(AT[0:NS, SEQ:T], MT[0:NS, l, 0:NS].bitcast(U16), W[0:NS, SEQ:T]))
                    dve.copy_predicated(tiles4(AT[:, 0:SEQ]), bc4(MT[:, l, :].bitcast(U16)), tiles4(W[:, 0:SEQ]))\
                       .then_inc(S["gl_at"], 1)
                for n in ("kt", "v0", "v1"):
                    skip(u, n)
                W = group(u, "sA")
                link(dve.tensor_copy(SS[:, 0, :], W[:, 0:256]))
                for t in range(1, NT):
                    ins = dve.scalar_tensor_tensor(SS[:, t, :], SS[:, t - 1, :], eG[:, P * t + P - 1:P * t + P],
                                                   W[:, 256 * t:256 * t + 256], ALU.mult, ALU.add)
                    if t < NT - 1:
                        link(ins)
                    else:
                        ins.then_inc(S["gl_s"], 1)

                def mask_v(i):
                    dve.wait_ge(S["gl_v"], 2 * h + 2)
                    dve.tensor_tensor(um, vt[0:NS, NT, :].unsqueeze(1).broadcast_to([NS, 4, 256]),
                                      rowm[:, 4 * i:4 * i + 4].unsqueeze(2).broadcast_to([NS, 4, 256]),
                                      ALU.mult).then_inc(S["gl_um"], 1)

                mask_v(0)
                for e in range(2):
                    W = group(u, f"o{e}")
                    dve.wait_ge(S["gl_osq"], 2 * h + e + 1)
                    dve.wait_ge(S["gl_z"], h + 1)
                    dve.scalar_tensor_tensor(slot(e), W[:, 0:T], pvc("gla_norm", e), raws[:, T * (4 + e):T * (5 + e)],
                                             ALU.mult, ALU.mult).then_inc(S["gl_o1"], 1)
                if h + 1 < GLA_H:
                    gates(u, "lgn", h + 1)
                for i in range(2):
                    W = group(u, f"sb{i}")
                    if i == 0:
                        dve.wait_ge(S["gl_gs"], h + 1)
                    if i == 0:
                        mask_v(1)
                    half = sbuf[:, 1024 * i:1024 * i + 1024]
                    dve.tensor_tensor(half, half, W[:, 0:1024], ALU.add).then_inc(S["gl_snew"], 1)
                    if i == 0 and h + 1 < GLA_H:
                        gate_sums(h + 1)
                if h + 1 < GLA_H:
                    exponents(0)
                skip(u, "n")
                dve.wait_ge(S["gl_rstd"], h + 1)
                dve.wait_ge(S["gl_o1"], 2 * h + 2)
                dve.tensor_tensor(slot(9, 2).rearrange("p (e t) -> p e t", e=2), slot(0, 2).rearrange("p (e t) -> p e t", e=2),
                                  slot(2).unsqueeze(1).broadcast_to([P, 2, T]), ALU.mult).then_inc(S["gl_y"], 1)

            def bc():
                u = ("bc", 0)
                fill(target[u, "start"])
                dve.wait_ge(S["u_loaded"], loads[u])
                dve.wait_ge(S["rows_copied"], 3)
                conv(4, lambda i, w: pvc("ssd_conv_w", 12 * w + 8 + i), lambda i: pvc("ssd_conv_b", 8 + i), slot,
                     S["bc_smp"], 1, S["bc_conv"])
                for n in ("bt", "bts", "cb0", "cb1", "cb2", "cb3"):
                    skip(u, n)
                link(dve.memset(arena[:, 8000:8000 + P], 0.0))

            def ssd(p):
                u = ("ssd", p)
                if p == 0:
                    fill(target[u, "start"])
                    free(u)
                g, e2 = p // 2, p % 2
                pb = SSD_N * (g % 2)
                hp = slice(pb, pb + SSD_N)
                xs, ebc = ssd_x(p), arena[:, 6176:6176 + T]
                v, v2, SS = arena[:, 6720:7360], arena[:, 7360:8000], arena[:, 8000:8640]
                um = extra[0:NS, 0:1024].rearrange("p (b e) -> p b e", b=NB)
                y = extra[:, 1024 + T * e2:1024 + T * (e2 + 1)]
                t1 = raws[:, 4 * T:5 * T]
                def conv_x(n):
                    dve.wait_ge(S["u_loaded"], loads["ssd", n])
                    if n > 1:
                        dve.wait_ge(S["sp_y"], n - 1)
                    conv(1, lambda i, w: pvc("ssd_conv_w", 12 * w + n), lambda i: pvc("ssd_conv_b", n),
                         lambda i: ssd_x(n), S["sp_smp"], n + 1, S["sp_conv"])

                if p == 0:
                    conv_x(0)
                for n in ("dmA", "dmB", "ebc"):
                    skip(u, n)
                W = group(u, "xt")
                by_token(v, W, 32 + 2 * p, nh=2)
                by_token(v2, W, 64 + 2 * p, nh=2, done=S["sp_v"])
                dve.wait_ge(S["sp_v"], p + 1)
                dve.tensor_tensor(um, v2[0:NS, SEQ:SEQ + P].unsqueeze(1).broadcast_to([NS, NB, P]),
                                  rowm.unsqueeze(2).broadcast_to([NS, NB, P]), ALU.mult).then_inc(S["sp_um"], 1)
                dve.wait_ge(S["bc_cb"], 4)
                dve.wait_ge(S["sp_D"], 2 * p + 2)
                for e in range(2):
                    go(dve.tensor_tensor(slot(e)[:, 0:SEQ], slot(e)[:, 0:SEQ], slot(4 + g)[:, 0:SEQ], ALU.mult))
                    ins = dve.tensor_tensor(slot(e)[0:NS, SEQ:T], slot(e)[0:NS, SEQ:T], slot(4 + g)[0:NS, SEQ:T], ALU.mult)
                    if e:
                        ins.then_inc(S["sp_A"], 1)
                    else:
                        go(ins)
                free(u)
                W = group(u, "sP")
                eg = egt[hp, 24 * p:24 * p + 24].rearrange("p (h c) -> p h c", h=2)
                for t in range(NT):
                    a = SS[hp, P * t:P * t + P].rearrange("p (h e) -> p h e", h=2)
                    b = SS[hp, P * t + P:P * t + 2 * P].rearrange("p (h e) -> p h e", h=2)
                    link(dve.tensor_tensor(b, a, eg[:, :, t:t + 1].broadcast_to([SSD_N, 2, SSD_N]), ALU.mult))
                    ins = dve.tensor_tensor(SS[hp, P * t + P:P * t + 2 * P], SS[hp, P * t + P:P * t + 2 * P],
                                            W[hp, P * t:P * t + P], ALU.add)
                    if t < NT - 1:
                        link(ins)
                    else:
                        ins.then_inc(S["sp_s"], 1)
                W = group(u, "ss")
                dve.wait_ge(S["sp_gs"], p + 1)
                dve.tensor_tensor(sbuf[hp, 1024:2048], sbuf[hp, 1024:2048], W[hp, 0:1024], ALU.add).then_inc(S["sp_snew"], 1)
                if p + 1 < SSD_H // 2:
                    conv_x(p + 1)
                W = group(u, "i")
                dve.wait_ge(S["sp_ebc"], p + 1)
                dve.tensor_tensor(t1, W[:, 0:T], ebc, ALU.mult).then_inc(S["sp_i"], 1)
                dve.wait_ge(S["sp_i"], p + 1)
                W = group(u, "o")
                dve.tensor_tensor(t1, W[:, 0:T], t1, ALU.add).then_inc(S["sp_o"], 1)
                dve.wait_ge(S["sp_o"], p + 1)
                link(dve.scalar_tensor_tensor(t1, xs, egt[:, SSD_H * 12 + p:SSD_H * 12 + p + 1], t1, ALU.mult, ALU.add))
                dve.wait_ge(S["sp_z"], p + 1)
                dve.tensor_tensor(y, t1, raws[:, T:2 * T], ALU.mult).then_inc(S["sp_y"], 1)
                if e2:
                    skip(u, "n")
                    dve.wait_ge(S["sp_rstd"], p // 2 + 1)
                    dve.wait_ge(S["sp_y"], p + 1)
                    for e in range(2):
                        ye = extra[:, 1024 + T * e:1024 + T * (e + 1)]
                        ins = dve.scalar_tensor_tensor(ye, ye, pvc("ssd_norm", p - 1 + e), raws[:, 5 * T:6 * T], ALU.mult,
                                                       ALU.mult)
                        if e:
                            ins.then_inc(S["sp_out"], 1)
                        else:
                            go(ins)

            def lru(j):
                u = ("lru", j)
                if j == 0:
                    fill(target[u, "start"])
                    free(u)
                for n in ((0, 1) if j == 0 else (j + 1,)):
                    if n < LRU_W // P:
                        dve.wait_ge(S["u_loaded"], loads["lru", n])
                        conv(1, lambda i, w: pvc("lru_conv_w", 8 * w + n), lambda i: pvc("lru_conv_b", n),
                             lambda i: lru_slot(n, 0), S["lr_smp"], n + 1, S["lr_conv"], src=2 * (n % 2))
                skip(u, "r")
                skip(u, "i")
                if j:
                    free(("lru", j - 1))
                xc, y, ig, a, th, b, hs = (lru_slot(j, i) for i in range(7))
                dve.wait_ge(S["lr_a"], j + 1)
                go(dve.tensor_tensor(ig, ig, xc, ALU.mult))
                link(dve.tensor_tensor(b, a, a, ALU.mult))
                link(dve.scalar_tensor_tensor(b, b, 1.0, th, ALU.add, ALU.mult))
                dve.tensor_scalar(b, b, 1e-30, None, ALU.max).then_inc(S["lr_t"], 1)
                starts = a[:, SEQ:T].rearrange("p (b i) -> p b i", b=NB)[:, :, 0]
                bs = b[:, SEQ:T].rearrange("p (b i) -> p b i", b=NB)[:, :, 0]
                link(dve.tensor_tensor(small[:, 32:40], starts, hist[:, 36 + j, 24:32], ALU.mult))
                go(dve.memset(a[:, 0:1], 0.0))
                go(dve.memset(starts, 0.0))
                if j + 1 < LRU_W // P:
                    fill((target[u, "i"] + target[("lru", j + 1), "r"]) // 2)
                dve.wait_ge(S["lr_sq"], j + 1)
                link(dve.tensor_tensor(b, b, ig, ALU.mult))
                link(dve.tensor_tensor(bs, bs, small[:, 32:40], ALU.add))
                dve.tensor_tensor_scan(hs, a, b, 0.0, ALU.mult, ALU.add).then_inc(S["lr_hs"], 1)
                dve.wait_ge(S["lr_hs"], j + 1)
                dve.wait_ge(S["lr_z"], j + 1)
                dve.tensor_tensor(y, hs, raws[:, T:2 * T], ALU.mult).then_inc(S["lr_y"], 1)

            def y_parts(layer, to):
                while split[layer] < to:
                    k = split[layer]
                    lo_part(1 + 3 * layer, k, y_source(layer, k))
                    split[layer] += 1

            def out_proj(layer):
                for c in range(KT):
                    d = first[f"out{layer}"] + c
                    if c < KT - 1:
                        fill(SL * (d + 1))
                    else:
                        last_tile(2 + 3 * layer)
                    dve.wait_ge(S["slice_done"], SL * (d + 1))
                    if c % 4 == 0:
                        dve.wait_ge(S[f"h_loaded{c // 4}"], 16 * (layer + 1))
                    dve.tensor_tensor(hT(c), hT(c), psd[d % 2][:, D0:D0 + T], ALU.add)\
                       .then_inc(S[f"dense_read{d % 2}"], 1)
                lo_part(2 + 3 * layer, KT - 1)
                fill(first_slice(f"gate{layer}"))

            def gate(layer):
                u = ("gate", layer)
                for c in range(KT):
                    d = first[f"gate{layer}"] + c
                    if c < KT - 1 or layer:
                        fill(SL * (d + 1))
                    else:
                        last_tile(3)
                    dve.wait_ge(S["slice_done"], SL * (d + 1))
                    if c == 0:
                        dve.wait_ge(S["nrm_rstd"], 2 * layer + 2)
                    else:
                        dve.wait_ge(S["gate_done"], KT * layer + c)
                    e = extra[:, T * (c % 2):T * (c % 2) + T]
                    dve.tensor_tensor(e, psd[d % 2][:, D0:D0 + T], rstd[:, :], ALU.mult)\
                       .then_inc(S[f"dense_read{d % 2}"], 1)
                    W = group(u, f"g{c}")
                    dve.wait_ge(S["gate_sig"], KT * layer + c + 1)
                    dve.tensor_tensor(e, e, W[:, 0:T], ALU.mult).then_inc(S["gate_read"], 1)
                    dve.wait_ge(S["gate_read"], KT * layer + c + 1)
                    dve.tensor_tensor(hT(c), hT(c), e, ALU.add).then_inc(S["gate_done"], 1)
                if layer == 0:
                    dve.wait_ge(S["gate_done"], KT)
                    lo_part(3, KT - 1)

            dve.memset(ones[:, :], 1.0)
            dve.memset(cst[:, 0:1], EPS)
            dve.memset(cst[:, 1:2], 1.0).then_inc(S["consts_set"], 1)
            split_lo(0)
            split_lo(1)
            dve.wait_ge(S["rows_act"], 1)
            lam = pvc("lru_lambda", 0, 8)
            link(dve.tensor_scalar(small[:, 56:64], lam, -1.0, 0.0, ALU.mult, ALU.max))
            link(dve.tensor_tensor(small[:, 56:64], small[:, 56:64], small[:, 48:56], ALU.add))
            link(dve.tensor_scalar(small[:, 56:64], small[:, 56:64], 8.0, None, ALU.mult))
            link(dve.tensor_scalar(small[:, 48:56], small[:, 56:64], -1.0, None, ALU.mult))
            for c in range(KT):
                lo_part(0, c)
            for u in UNITS:
                if u[0] == "ab_rows":
                    rows_ab()
                    skip(u, "c0")
                elif u[0] == "dn":
                    dn(u[1])
                elif u[0] == "gla":
                    gla(u[1])
                else:
                    y_parts(0, KT)
            out_proj(0)
            gate(0)
            for u in UNITS_CD:
                if u[0] == "cd_rows":
                    rows_cd()
                    skip(u, "eg")
                    skip(u, "c0")
                elif u[0] == "bc":
                    bc()
                elif u[0] == "ssd":
                    ssd(u[1])
                elif u[0] == "lru":
                    lru(u[1])
                else:
                    y_parts(1, KT)
            out_proj(1)
            gate(1)
            final_norm()

        @block.gpsimd
        def _(pool):
            chained = [0]

            def link(ins):
                chained[0] += 1
                ins.then_inc(S["pool_chain"], 1)
                pool.wait_ge(S["pool_chain"], chained[0])

            def load_raws(u, z=False):
                d0, n = RAW[u]
                at = 0
                if u in zloads:
                    nz = 2 if u[0] == "gla" else 1
                    d0, n, at = (d0 + n - nz, nz, n - nz) if z else (d0, n - nz, 0)
                if u[0] == "lru" and not z:
                    at = 2 * (u[1] % 2)
                for e in range(2):
                    last = [staged[d][2] for d in range(d0, d0 + n) if staged[d][1] == e]
                    if last:
                        pool.wait_ge(S[f"stage_stored{e}"], last[-1])
                i = staged[d0][0]
                pool.dma_start(raws[:, at * T:(at + n) * T].rearrange("p (i t) -> p i t", i=n),
                               uT[i:i + n].rearrange("i p t -> p i t")).then_inc(S["z_loaded" if z else "u_loaded"], 16)

            def sample_rows(u, n, tile, done, src=0):
                pool.wait_ge(S["u_loaded"], loads[u])
                for i in range(n):
                    x = raws[:, T * (src + i):T * (src + i) + T]
                    h3 = hist[:, tile(i), 0:24].rearrange("p (b r) -> p b r", b=NB)
                    link(pool.tensor_copy(smp[:, i, :, 0:TAPS - 1], h3))
                    ins = pool.tensor_copy(smp[:, i, :, TAPS - 1:], x[:, SEQ:T].rearrange("p (b s) -> p b s", b=NB))
                    if i == n - 1:
                        ins.then_inc(done, 1)
                    else:
                        link(ins)
                for i in range(n):
                    x = raws[:, T * i:T * i + T]
                    if tile(i) < 36:
                        tails(x, tile(i))

            def tails(x, tile):
                link(pool.tensor_copy(hist[:, tile, 0:3], x[:, SEQ - 3:SEQ]))
                link(pool.tensor_copy(hist[:, tile, 3:27].rearrange("p (b r) -> p b r", b=NB),
                                      x[:, SEQ:T].rearrange("p (b s) -> p b s", b=NB)[:, :, 1:]))

            pool.memset(small[:, :], 0.0)
            pool.memset(hist[:, :, :], 0.0).then_inc(S["zeroed"], 1)
            pool.wait_ge(S["zeroed"], 1)
            for name, (col, row, n) in PARAM_ROWS.items():
                pool.dma_start(cols[row:row + n, col, :], as_rows(I[name])).then_inc(S["params_loaded"], 16)
            pool.dma_start(raws[0:24, 0:3072], I["state_dn_conv"][0].rearrange("b r c -> (b r) c")).then_inc(S["params_loaded"], 16)
            for i, dst in enumerate((rowG, rowB, rowlr)):
                pool.dma_start(dst[0:24, 0:4 * P], I["state_ssd_conv"][0, :, :, 4 * P * i:4 * P * (i + 1)]
                               .rearrange("b r c -> (b r) c")).then_inc(S["params_loaded"], 16)
            lru_rows = stage[0:32, :, :].rearrange("p e t -> p (e t)")
            pool.dma_start(lru_rows[0:24, 0:1024], I["state_lru_conv"][0].rearrange("b r c -> (b r) c"))\
                .then_inc(S["params_loaded"], 16)
            pool.dma_start(lru_rows[24:32, 0:1024], I["state_lru"][0]).then_inc(S["params_loaded"], 16)
            pool.dma_start(cb16[:, :], I["cb"]).then_inc(S["masks_loaded"], 16)
            pool.dma_start(small[0:DN_H, 0:1], I["dn_dt_bias"].rearrange("a h -> h a"), allow_slow_non_contiguous=True).then_inc(S["rows_loaded"], 16)
            pool.dma_start(small[0:DN_H, 1:2], I["dn_a_log"].rearrange("a h -> h a"), allow_slow_non_contiguous=True).then_inc(S["rows_loaded"], 16)
            pool.dma_start(small[0:SSD_H, 10:11], I["ssd_dt_bias"].rearrange("a h -> h a"), allow_slow_non_contiguous=True).then_inc(S["rows_loaded"], 16)
            pool.dma_start(small[0:SSD_H, 11:12], I["ssd_a_log"].rearrange("a h -> h a"), allow_slow_non_contiguous=True).then_inc(S["rows_loaded"], 16)
            for e in range(2):
                pool.dma_start(egt[64 * e:64 * e + 64, SSD_H * 12:SSD_H * 12 + 8],
                               I["ssd_d"].rearrange("a (p e) -> e a p", e=2)[e].partition_broadcast(64), allow_slow_non_contiguous=True)\
                    .then_inc(S["rows_loaded"], 16)
            pool.dma_start(wa2[64:64 + GLA_R, :], I["gla_wa2"][0]).then_inc(S["rows_loaded"], 16)
            arena3 = arena[:, :].rearrange("p (c t) -> p c t", c=KT)

            def add_square(i, c):
                acc = sbuf[:, T:2 * T]
                pool.wait_ge(S["nrm_sq"], KT * i + c + 1)
                if c > 1:
                    pool.wait_ge(S["sq_summed"], (KT - 2) * i + c - 1)
                pool.tensor_tensor(acc, acc, extra[:, T * (2 + c % 2):T * (3 + c % 2)], ALU.add)\
                    .then_inc(S["sq_summed"] if c < KT - 1 else S["sq_added"], 1)

            def norm(i):
                if i % 2 or i == 0:
                    for c in range(1, KT):
                        add_square(i, c)

            def store_h(i):
                pool.wait_ge(S["x_ready"], KT * (1 if i == 0 else 4))
                pool.dma_start(hD.rearrange("c p t -> p c t"), arena3).then_inc(S["h_stored"], 16)

            def load_h(layer):
                pool.wait_ge(S["out_stored"], stored["ab_tail", 0] if layer == 0 else stored["cd_tail", 0])
                pool.wait_ge(S["x_ready"], KT * (2 + 3 * layer))
                for q in range(4):
                    pool.dma_start(arena3[:, 4 * q:4 * q + 4], hD[4 * q:4 * q + 4].rearrange("c p t -> p c t"))\
                        .then_inc(S[f"h_loaded{q}"], 16)

            def load_p(layer):
                ptok = raws[:, 0:1280].rearrange("p (t c) -> p t c", t=NT + 1)
                wp = raws[:, 2368:2880].rearrange("p (s k n) -> p s k n", s=2, k=2)
                pool.dma_start(ptok[:, 0:NT, :], I["p_prompt"][layer, 0].rearrange("(t p) c -> p t c", p=P))\
                    .then_inc(S["p_loaded"], 16)
                pool.dma_start(ptok[0:NS, NT, :], I["p_sample"][layer].rearrange("b s c -> (b s) c")).then_inc(S["p_loaded"], 16)
                for c in range(KT):
                    if c >= 2:
                        pool.wait_ge(S["gate_read"], KT * layer + c - 1)
                    pool.dma_start(wp[:, c % 2], I["ple_w_proj"][layer, :, P * c:P * c + P]
                                   .rearrange("(k p) n -> p k n", p=P)).then_inc(S[f"wp_loaded{c % 2}"], 16)
                    if c >= 3:
                        add_square(2 * layer + 2, c - 2)
                for c in range(KT - 2, KT):
                    add_square(2 * layer + 2, c)

            def dn(h):
                u = ("dn", h)
                load_raws(u, z=True)
                if h == 0:
                    load_raws(u)
                    sample_rows(u, 3, lambda i: 8 * i + h, S["dn_smp"])
                pool.wait_ge(S["out_stored"], stored[u])
                pool.dma_start(sbuf[:, 0:1024].rearrange("p (b e) -> p b e", b=NB),
                               I["state_dn"][0, :, h].rearrange("b d e -> d b e")).then_inc(S["s_loaded"], 16)
                pool.wait_ge(S["s_loaded"], sloads[u])
                pool.wait_ge(S["dn_eg"], h + 1)
                ge = slot(5)[:, SEQ:T].rearrange("p (b i) -> p b i", b=NB)[:, :, LS - 1:LS].broadcast_to([P, NB, P])
                pool.tensor_tensor(sbuf[:, 1024:2048].rearrange("p (b e) -> p b e", b=NB),
                                   sbuf[:, 0:1024].rearrange("p (b e) -> p b e", b=NB), ge, ALU.mult).then_inc(S["dn_gs"], 1)
                if h + 1 < DN_H:
                    load_raws(("dn", h + 1))
                    sample_rows(("dn", h + 1), 3, lambda i: 8 * i + h + 1, S["dn_smp"])
                pool.wait_ge(S["dn_snew"], h + 1)
                pool.dma_start(O["dn_s"][0, :, h].rearrange("b d e -> d b e"),
                               sbuf[:, 1024:2048].rearrange("p (b e) -> p b e", b=NB)).then_inc(S["out_stored"], 16)
                pool.wait_ge(S["dn_s"], 4 * h + 4)
                pool.dma_start(O["dn_p"][0, 0, h], extra[:, 640 + 384:640 + 512]).then_inc(S["out_stored"], 16)
                pool.wait_ge(S["dn_y"], h + 1)
                pool.dma_start(yT[h], slot(9)).then_inc(S["out_stored"], 16)

            def gla(h):
                u = ("gla", h)
                if h:
                    pool.wait_ge(S["gl_o1"], 2 * h)
                else:
                    pool.wait_ge(S["out_stored"], stored[u])
                    load_raws(u)
                load_raws(u, z=True)
                pool.wait_ge(S["out_stored"], stored[u])
                Sb = sbuf[:, :].rearrange("p (b e) -> p b e", b=NB)
                pool.dma_start(Sb, I["state_gla"][0, :, h].rearrange("b d e -> d b e")).then_inc(S["s_loaded"], 16)
                pool.wait_ge(S["s_loaded"], sloads[u])
                if h + 1 < GLA_H:
                    pool.wait_ge(S["gl_qkt"], 7 * h + 7)
                    pool.wait_ge(S["gl_v"], 2 * h + 2)
                    load_raws(("gla", h + 1))
                pool.wait_ge(S["gl_eg"], h + 1)
                pool.wait_ge(S["work_ready"], NO[u, "o1"] + 1)
                ge = slot(4)[:, SEQ:T].rearrange("p (b i) -> p b i", b=NB)[:, :, LS - 1:LS].broadcast_to([P, NB, 256])
                pool.tensor_tensor(Sb, Sb, ge, ALU.mult).then_inc(S["gl_gs"], 1)
                pool.wait_ge(S["gl_snew"], 2 * h + 2)
                pool.dma_start(O["gla_s"][0, :, h].rearrange("b d e -> d b e"), Sb).then_inc(S["out_stored"], 16)
                pool.dma_start(O["gla_p"][0, 0, h], extra[:, 768:1024]).then_inc(S["out_stored"], 16)
                if u == LAST[0]:
                    return
                pool.wait_ge(S["gl_y"], h + 1)
                pool.dma_start(yT[8 + 2 * h:10 + 2 * h].rearrange("c p t -> p c t"),
                               slot(9, 2).rearrange("p (c t) -> p c t", c=2)).then_inc(S["out_stored"], 16)

            def ssd(p):
                u = ("ssd", p)
                pb = SSD_N * (p // 2 % 2)
                hp = slice(pb, pb + SSD_N)
                pool.wait_ge(S["out_stored"], stored[u])
                if p:
                    pool.wait_ge(S["sp_y"], p)
                else:
                    pool.wait_ge(S["bc_conv"], 1)
                    load_raws(u)
                    sample_rows(u, 1, lambda i: 24, S["sp_smp"])
                load_raws(u, z=True)
                pool.tensor_copy(selp[0:SSD_H, :].rearrange("p (h e) -> p h e", h=2),
                                 ident[0:SSD_H, 2 * p:2 * p + 2].unsqueeze(2).broadcast_to([SSD_H, 2, SSD_N]))\
                    .then_inc(S["sp_sel"], 1)
                Sin = sbuf[hp, 0:1024].rearrange("p (b h e) -> p b h e", b=NB, h=2)
                for i in range(2):
                    pool.dma_start(Sin[:, :, i, :], I["state_ssd"][0, :, 2 * p + i].rearrange("b n e -> n b e"))\
                        .then_inc(S["s_loaded"], 16)
                if p + 1 < SSD_H // 2:
                    pool.wait_ge(S["sp_conv"], p + 1)
                    load_raws(("ssd", p + 1))
                    sample_rows(("ssd", p + 1), 1, lambda i: 24 + p + 1, S["sp_smp"])
                pool.wait_ge(S["s_loaded"], sloads[u])
                Sn = sbuf[hp, 1024:2048].rearrange("p (b h e) -> p b h e", b=NB, h=2)
                for i in range(2):
                    eg = egt[hp, 12 * (2 * p + i) + 4:12 * (2 * p + i) + 12].unsqueeze(2).broadcast_to([SSD_N, NB, SSD_N])
                    ins = pool.tensor_tensor(Sn[:, :, i, :], Sin[:, :, i, :], eg, ALU.mult)
                    if i:
                        ins.then_inc(S["sp_gs"], 1)
                    else:
                        link(ins)
                pool.wait_ge(S["sp_snew"], p + 1)
                for i in range(2):
                    pool.dma_start(O["ssd_s"][0, :, 2 * p + i].rearrange("b n e -> n b e"), Sn[:, :, i, :])\
                        .then_inc(S["ssd_stored"], 16)
                pool.wait_ge(S["sp_s"], p + 1)
                pool.dma_start(O["ssd_p"][0, 0, 2 * p:2 * p + 2].rearrange("h n e -> n h e"),
                               arena[hp, 8000 + 512:8000 + 640].rearrange("p (h e) -> p h e", h=2)).then_inc(S["out_stored"], 16)
                pool.wait_ge(S["ssd_stored"], 32 * (p + 1))
                if p % 2:
                    pool.wait_ge(S["sp_out"], p // 2 + 1)
                    pool.dma_start(yT[p - 1:p + 1].rearrange("c p t -> p c t"),
                                   extra[:, 1024:1024 + 2 * T].rearrange("p (c t) -> p c t", c=2)).then_inc(S["out_stored"], 16)

            def load_blocks(j):
                bd = sbuf[:, 256 * (j % 2):256 * (j % 2) + 256].rearrange("p (i n) -> p i n", i=2)
                for i, name in enumerate(("lru_wa", "lru_wx")):
                    for b in range(2):
                        pool.dma_start(bd[64 * b:64 * b + 64, i, 64 * b:64 * b + 64], I[name][0, 2 * j + b])\
                            .then_inc(S["s_loaded"], 16)

            def lru(j):
                u = ("lru", j)
                if j == 0:
                    load_raws(u)
                    load_blocks(0)
                    sample_rows(u, 1, lambda i: 36, S["lr_smp"])
                else:
                    pool.wait_ge(S["lr_y"], j)
                load_raws(u, z=True)
                if j + 1 < LRU_W // P:
                    pool.wait_ge(S["lr_conv"], j + 1)
                    load_raws(("lru", j + 1))
                    sample_rows(("lru", j + 1), 1, lambda i: 36 + j + 1, S["lr_smp"], src=2 * ((j + 1) % 2))
                    pool.wait_ge(S["lr_r"], j + 1)
                    load_blocks(j + 1)
                pool.wait_ge(S["lr_y"], j + 1)
                x, hs = raws[:, 2 * T * (j % 2):2 * T * (j % 2) + T], lru_slot(j, 6)
                tails(x, 36 + j)
                link(pool.tensor_copy(hist[:, 36 + j, 27:28], hs[:, SEQ - 1:SEQ]))
                link(pool.tensor_copy(hist[:, 36 + j, 28:36], hs[:, SEQ:T].rearrange("p (b i) -> p b i", b=NB)[:, :, LS - 1]))
                if j < LRU_W // P - 2:
                    pool.dma_start(yT[8 + j], lru_slot(j, 1)).then_inc(S["out_stored"], 16)

            norm(0)
            store_h(0)
            for u in UNITS:
                if u[0] == "dn":
                    dn(u[1])
                elif u[0] == "gla":
                    gla(u[1])
                elif u[0] == "ab_tail":
                    pool.memset(small[0:1, 42:43], 0.0).then_inc(S["tail_made"], 1)
                    load_h(0)
                    for n in range(3):
                        pool.wait_ge(S["tail_copied"], n + 1)
                        cs = slice(1024 * n, 1024 * n + 1024)
                        pool.dma_start(O["dnc_p"][0, 0, :, cs], raws[0:3, cs]).then_inc(S["out_stored"], 16)
                        pool.dma_start(O["dnc_s"][0].rearrange("b r c -> (b r) c")[:, cs], raws[3:27, cs])\
                            .then_inc(S["out_stored"], 16)
            pool.wait_ge(S["out_stored"], stored[UNITS_CD[0]])
            norm(1)
            load_p(0)
            norm(2)
            store_h(1)
            for u in UNITS_CD:
                if u[0] == "bc":
                    pool.wait_ge(S["gate_done"], KT)
                    load_raws(u)
                    sample_rows(u, 4, lambda i: 32 + i, S["bc_smp"])
                elif u[0] == "ssd":
                    ssd(u[1])
                elif u[0] == "lru":
                    if u[1] == 0:
                        pool.wait_ge(S["out_stored"], stored[u])
                        link(pool.memset(sbuf[:, 0:512], 0.0))
                    lru(u[1])
                elif u[0] == "cd_tail":
                    pool.memset(small[0:1, 42:43], 0.0).then_inc(S["tail_made"], 1)
                    load_h(1)
                    pool.wait_ge(S["tail_copied"], 6)
                    c_p, c_s = O["ssdc_p"][0, 0], O["ssdc_s"][0].rearrange("b r c -> (b r) c")
                    pool.dma_start(c_p, raws[0:3, 0:SSD_XBC]).then_inc(S["out_stored"], 16)
                    pool.dma_start(c_s, raws[3:27, 0:SSD_XBC]).then_inc(S["out_stored"], 16)
                    l0 = 2048
                    pool.dma_start(O["lruc_p"][0, 0], raws[0:3, l0:l0 + LRU_W]).then_inc(S["out_stored"], 16)
                    pool.dma_start(O["lruc_s"][0].rearrange("b r c -> (b r) c"), raws[3:27, l0:l0 + LRU_W])\
                        .then_inc(S["out_stored"], 16)
                    pool.dma_start(O["lru_p"][0], raws[27:28, l0:l0 + LRU_W]).then_inc(S["out_stored"], 16)
                    pool.dma_start(O["lru_s"][0], raws[28:36, l0:l0 + LRU_W]).then_inc(S["out_stored"], 16)
            pool.wait_ge(S["out_stored"], stored["end"])
            norm(3)
            load_p(1)
            for t in range(NT + 1):
                _, n = tok(t)
                src = raws if t % 2 == 0 else sbuf
                pool.wait_ge(S["out_copied"], 2 * t + 2)
                dst = O["y_p"][0, P * t:P * t + P] if t < NT else O["y_s"].rearrange("b s d -> (b s) d")
                pool.dma_start(dst, src[0:n, 0:D_MODEL]).then_inc(S[f"y_stored{t % 2}"], 16)
            pool.wait_ge(S["y_stored0"], 48)
            pool.wait_ge(S["y_stored1"], 32)
            pool.wait_ge(S["h_stored"], 32)


_INS = ["x_prompt", "x_sample", "state_dn", "state_dn_conv", "state_gla", "state_ssd", "state_ssd_conv", "state_lru",
        "state_lru_conv", "p_prompt", "p_sample", "norm_g", "final_norm", "ab_w_in", "dn_conv_w", "dn_a_log",
        "dn_dt_bias", "dn_norm", "gla_wa2", "gla_ba", "gla_norm", "ab_w_out", "cd_w_in", "ssd_conv_w", "ssd_conv_b",
        "ssd_a_log", "ssd_dt_bias", "ssd_d", "ssd_norm", "lru_conv_w", "lru_conv_b", "lru_wa", "lru_ba", "lru_wx",
        "lru_bx", "lru_lambda", "cd_w_out", "ple_w_proj", "ple_norm", "ple_w_gate"]
_OUTS = [("y_p", (1, SEQ, D_MODEL)), ("y_s", (NB, LS, D_MODEL)),
         ("dn_p", (1, 1, 8, 128, 128)), ("dnc_p", (1, 1, 3, 3072)), ("gla_p", (1, 1, 4, 128, 256)),
         ("ssd_p", (1, 1, 16, 64, 64)), ("ssdc_p", (1, 1, 3, 1536)), ("lru_p", (1, 1, 1024)),
         ("lruc_p", (1, 1, 3, 1024)),
         ("dn_s", (1, NB, 8, 128, 128)), ("dnc_s", (1, NB, 3, 3072)), ("gla_s", (1, NB, 4, 128, 256)),
         ("ssd_s", (1, NB, 16, 64, 64)), ("ssdc_s", (1, NB, 3, 1536)), ("lru_s", (1, NB, 1024)),
         ("lruc_s", (1, NB, 3, 1024))]


def _constants():
    import numpy as np

    r = np.arange(P)
    i, j = r[:, None], r[None, :]
    lower = []
    for l in range(7):
        s = 1 << l
        lower.append((i // (2 * s) == j // (2 * s)) & (i % (2 * s) >= s) & (j % (2 * s) < s))
    mx = np.stack(lower, 1).astype(np.float32).reshape(P, -1)
    mt = np.stack([m.T for m in lower], 1).astype(np.float32).reshape(P, -1)
    negm = np.where(j < i, -1e30, 0.0)
    s = np.arange(NS)
    negs = np.zeros((P, NS))
    negs[:NS] = np.where((s[None] < s[:, None]) | (s[None] // LS != s[:, None] // LS), -1e30, 0.0)
    tt = np.arange(T)
    starts = np.where(tt < SEQ, tt % P == 0, (tt - SEQ) % LS == 0)
    rmask = np.broadcast_to(np.where(starts, 0.0, 1.0), (P, T))
    bmask = np.broadcast_to((s[None] // LS == np.arange(NB)[:, None]).reshape(1, -1), (P, NB * NS))
    rowm = np.zeros((P, NB))
    rowm[:NS] = s[:, None] // LS == np.arange(NB)[None]
    parts = [mx, mt, np.eye(P), negm, negs, rmask, bmask, rowm]
    cb = np.concatenate([np.asarray(x, np.float32) for x in parts], 1)
    return {"cf": np.eye(P, dtype=np.float32), "cb": cb}


def kernel(**inputs):
    import numpy as _np
    import concourse.bacc as _bacc
    from concourse import mybir as _mybir
    from concourse.bass_utils import run_bass_kernel_spmd as _run

    nc = _bacc.Bacc("TRN2", target_bir_lowering=False, num_devices=1)
    arrays, I, O = {}, {}, {}
    given = {name: _np.ascontiguousarray(inputs[name]) for name in _INS}
    for name, a in {**given, **_constants()}.items():
        arrays[f"in_{name}_dram"] = a
        I[name] = nc.dram_tensor(f"in_{name}_dram", a.shape, _mybir.dt.from_np(a.dtype), kind="ExternalInput").ap()
    for name, shape in _OUTS:
        O[name] = nc.dram_tensor(f"out_{name}_dram", shape, F32, kind="ExternalOutput").ap()
    trunk(nc, I, O)
    r = _run(nc, [arrays], core_ids=[0])
    return tuple(r.results[0][f"out_{name}_dram"] for name, _ in _OUTS)
```
